# Optimizing a Trainium2 kernel written in Bass

```python
import math
import jax
import jax.numpy as jnp
from jax import lax
import numpy as np

D_MODEL = 1024
BATCH = 1
SEQ = 512
DEPTH = 1

SSM_WIDTH = D_MODEL // 2
SSM_GROUP = 16
SSM_GROUPS = SSM_WIDTH // SSM_GROUP
SSM_STATE = 64
DT_MIN = 1e-3
DT_MAX = 1e-1

N_HEADS = 8
HEAD_DIM = 64
ATTN_WIDTH = N_HEADS * HEAD_DIM
IDX_HEADS = 8
IDX_DIM = 64
TOPK_KEYS = 256
Q_BLOCK = 128

N_EXPERTS = 32
TOP_K = 4
D_FF = D_MODEL
SWIGLU_LIMIT = 7.0
SWIGLU_ALPHA = 1.702
MOE_BLOCK = 128

N_BRANCHES = 2
LN_EPS = 1e-5
DEEPNORM_ALPHA = (2 * DEPTH) ** 0.25
DEEPNORM_BETA = (8 * DEPTH) ** -0.25

IN_SIZES = (SSM_WIDTH, ATTN_WIDTH, ATTN_WIDTH, ATTN_WIDTH, IDX_HEADS * IDX_DIM, IDX_DIM, IDX_HEADS, N_BRANCHES * D_MODEL)
IN_WIDTH = SSM_WIDTH + 3 * ATTN_WIDTH + IDX_HEADS * IDX_DIM + IDX_DIM + IDX_HEADS + N_BRANCHES * D_MODEL

kernel_name = "hybrid_s5_dsa_moe_deepnorm"

def layer_norm(x, g, b):
    xf = x.astype(jnp.float32)
    mu = jnp.mean(xf, axis=-1, keepdims=True)
    var = jnp.mean(jnp.square(xf - mu), axis=-1, keepdims=True)
    y = (xf - mu) * lax.rsqrt(var + LN_EPS) * g.astype(jnp.float32) + b.astype(jnp.float32)
    return y.astype(x.dtype)

def alibi_slopes(n_heads):
    return jnp.asarray([2.0 ** (-8.0 * (hh + 1) / n_heads) for hh in range(n_heads)], jnp.float32)

def s5_branch(u, lam_re, lam_im, log_dt, b_re, b_im, c_re, c_im, d_skip, w_glu):
    f32 = jnp.float32
    bsz, seq, _ = u.shape
    uf = u.astype(f32).reshape(bsz, seq, SSM_GROUPS, SSM_GROUP)
    lam = lax.complex(lam_re.astype(f32), lam_im.astype(f32))
    dt = jnp.exp(log_dt.astype(f32))[:, None]
    a_bar = jnp.exp(lam * dt)
    b_c = lax.complex(b_re.astype(f32), b_im.astype(f32))
    b_bar = ((a_bar - 1.0) / lam)[..., None] * b_c
    bu = jnp.einsum('blgp,gnp->blgn', uf.astype(jnp.complex64), b_bar)
    a_seq = jnp.broadcast_to(a_bar, bu.shape)

    def combine(e1, e2):
        a1, s1 = e1
        a2, s2 = e2
        return a1 * a2, a2 * s1 + s2

    _, states = lax.associative_scan(combine, (a_seq, bu), axis=1)
    c_c = lax.complex(c_re.astype(f32), c_im.astype(f32))
    y = jnp.einsum('blgn,gpn->blgp', states, c_c).real + d_skip.astype(f32) * uf
    y = jax.nn.gelu(y.reshape(bsz, seq, SSM_WIDTH)).astype(u.dtype)
    val, gate = jnp.split(y @ w_glu, 2, axis=-1)
    return val * jax.nn.sigmoid(gate)

def dsa_branch(q, k, v, q_idx, k_idx, w_idx):
    f32 = jnp.float32
    bsz, seq = q.shape[:2]
    n_sel = min(TOPK_KEYS, seq // 4)
    n_blk = seq // Q_BLOCK
    slopes = alibi_slopes(N_HEADS)
    key_pos = jnp.arange(seq, dtype=jnp.int32)
    k_idx_f = k_idx.astype(f32)

    def to_blocks(t):
        return t.reshape(bsz, n_blk, Q_BLOCK, *t.shape[2:]).swapaxes(0, 1)

    def block_fn(args):
        blk, qb, qib, wb = args
        q_pos = blk * Q_BLOCK + jnp.arange(Q_BLOCK, dtype=jnp.int32)
        causal = key_pos[None, :] <= q_pos[:, None]
        dots = jnp.einsum('bqhd,bsd->bhqs', qib.astype(f32), k_idx_f) * IDX_DIM ** -0.5
        score = jnp.einsum('bqh,bhqs->bqs', wb.astype(f32) * IDX_HEADS ** -0.5, jax.nn.relu(dots))
        score = jnp.where(causal[None], score, -jnp.inf)
        _, sel = lax.top_k(score, n_sel)
        k_sel = jax.vmap(lambda kk, ii: kk[ii])(k, sel)
        v_sel = jax.vmap(lambda vv, ii: vv[ii])(v, sel)
        dist = (q_pos[None, :, None] - sel).astype(f32)
        logits = jnp.einsum('bqhd,bqkhd->bhqk', qb.astype(f32), k_sel.astype(f32)) * HEAD_DIM ** -0.5
        logits = logits - slopes[None, :, None, None] * dist[:, None]
        logits = jnp.where((dist >= 0)[:, None], logits, -jnp.inf)
        p = jax.nn.softmax(logits, axis=-1)
        return jnp.einsum('bhqk,bqkhd->bqhd', p.astype(v.dtype), v_sel)

    outs = lax.map(block_fn, (jnp.arange(n_blk, dtype=jnp.int32), to_blocks(q), to_blocks(q_idx), to_blocks(w_idx)))
    return outs.swapaxes(0, 1).reshape(bsz, seq, N_HEADS * HEAD_DIM)

def moe_ffn(x, w_router, b_router, w_up, b_up, w_down, b_down):
    bsz, seq, d = x.shape
    xt = x.reshape(-1, d)
    n_tok = xt.shape[0]
    logits = (xt @ w_router + b_router).astype(jnp.float32)
    top_val, top_idx = lax.top_k(logits, TOP_K)
    gates = jax.nn.softmax(top_val, axis=-1)
    n_assign = n_tok * TOP_K
    flat_e = top_idx.reshape(-1)
    flat_tok = jnp.repeat(jnp.arange(n_tok, dtype=jnp.int32), TOP_K)
    flat_g = gates.reshape(-1)
    order = jnp.argsort(flat_e)
    se, stok, sg = flat_e[order], flat_tok[order], flat_g[order]
    counts = jnp.bincount(flat_e, length=N_EXPERTS)
    starts = jnp.cumsum(counts) - counts
    padded = (counts + MOE_BLOCK - 1) // MOE_BLOCK * MOE_BLOCK
    pends = jnp.cumsum(padded)
    pstarts = pends - padded
    dest = pstarts[se] + jnp.arange(n_assign, dtype=jnp.int32) - starts[se]
    n_rows = n_assign + N_EXPERTS * MOE_BLOCK
    n_blocks = n_rows // MOE_BLOCK
    row_tok = jnp.full((n_rows,), n_tok, jnp.int32).at[dest].set(stok)
    row_gate = jnp.zeros((n_rows,), jnp.float32).at[dest].set(sg)
    blk_start = jnp.arange(n_blocks, dtype=jnp.int32) * MOE_BLOCK
    blk_expert = jnp.minimum(jnp.searchsorted(pends, blk_start, side='right'), N_EXPERTS - 1)

    def expert_block(args):
        e, toks, g = args
        xb = jnp.take(xt, toks, axis=0, mode='clip')
        hdn = xb @ w_up[e] + b_up[e]
        h_gate, h_lin = jnp.split(hdn, 2, axis=-1)
        h_gate = jnp.minimum(h_gate, SWIGLU_LIMIT)
        h_lin = jnp.clip(h_lin, -SWIGLU_LIMIT, SWIGLU_LIMIT)
        act = (h_lin + 1.0) * (h_gate * jax.nn.sigmoid(SWIGLU_ALPHA * h_gate))
        y = act @ w_down[e] + b_down[e]
        return y * g[:, None].astype(y.dtype)

    ys = lax.map(expert_block, (blk_expert, row_tok.reshape(n_blocks, MOE_BLOCK), row_gate.reshape(n_blocks, MOE_BLOCK)))
    out = jnp.zeros_like(xt).at[row_tok].add(ys.reshape(n_rows, d), mode='drop')
    return out.reshape(bsz, seq, d)

def setup_inputs(seed: int = 0) -> dict:
    key = jax.random.key(seed)
    ks = jax.random.split(key, 26)
    f32 = jnp.float32

    def nrm(k, shape, scale):
        return scale * jax.random.normal(k, shape, f32)

    nl, d = DEPTH, D_MODEL
    n_idx = jnp.arange(SSM_STATE, dtype=f32)
    g_shape = (nl, SSM_GROUPS, SSM_STATE)
    return {
        "x": nrm(ks[0], (BATCH, SEQ, d), 1.0),
        "ln_in_g": 1.0 + nrm(ks[1], (d,), 0.02),
        "ln_in_b": nrm(ks[2], (d,), 0.02),
        "w_in": nrm(ks[3], (nl, d, IN_WIDTH), d ** -0.5),
        "b_gate": nrm(ks[4], (nl, N_BRANCHES * d), 0.02),
        "lam_re": -0.5 + nrm(ks[5], g_shape, 0.01),
        "lam_im": math.pi * n_idx + nrm(ks[6], g_shape, 0.01),
        "log_dt": jax.random.uniform(ks[7], (nl, SSM_GROUPS), f32, math.log(DT_MIN), math.log(DT_MAX)),
        "b_re": nrm(ks[8], (nl, SSM_GROUPS, SSM_STATE, SSM_GROUP), (2 * SSM_GROUP) ** -0.5),
        "b_im": nrm(ks[9], (nl, SSM_GROUPS, SSM_STATE, SSM_GROUP), (2 * SSM_GROUP) ** -0.5),
        "c_re": nrm(ks[10], (nl, SSM_GROUPS, SSM_GROUP, SSM_STATE), 0.5),
        "c_im": nrm(ks[11], (nl, SSM_GROUPS, SSM_GROUP, SSM_STATE), 0.5),
        "d_skip": nrm(ks[12], (nl, SSM_GROUPS, SSM_GROUP), 1.0),
        "w_glu": nrm(ks[13], (nl, SSM_WIDTH, 2 * d), SSM_WIDTH ** -0.5),
        "w_attn_proj": nrm(ks[14], (nl, ATTN_WIDTH, d), ATTN_WIDTH ** -0.5),
        "w_o": nrm(ks[15], (nl, d, d), DEEPNORM_BETA * d ** -0.5),
        "ln1_g": 1.0 + nrm(ks[16], (nl, d), 0.02),
        "ln1_b": nrm(ks[17], (nl, d), 0.02),
        "w_router": nrm(ks[18], (nl, d, N_EXPERTS), d ** -0.5),
        "b_router": nrm(ks[19], (nl, N_EXPERTS), 0.01),
        "w_up": nrm(ks[20], (nl, N_EXPERTS, d, 2 * D_FF), d ** -0.5),
        "b_up": nrm(ks[21], (nl, N_EXPERTS, 2 * D_FF), 0.02),
        "w_down": nrm(ks[22], (nl, N_EXPERTS, D_FF, d), DEEPNORM_BETA * D_FF ** -0.5),
        "b_down": nrm(ks[23], (nl, N_EXPERTS, d), 0.02),
        "ln2_g": 1.0 + nrm(ks[24], (nl, d), 0.02),
        "ln2_b": nrm(ks[25], (nl, d), 0.02),
    }

def reference(x, ln_in_g, ln_in_b, w_in, b_gate, lam_re, lam_im, log_dt, b_re, b_im, c_re, c_im, d_skip, w_glu, w_attn_proj, w_o, ln1_g, ln1_b, w_router, b_router, w_up, b_up, w_down, b_down, ln2_g, ln2_b):
    bsz, seq, _ = x.shape
    split_points = np.cumsum(np.array(IN_SIZES))[:-1].tolist()
    h = layer_norm(x, ln_in_g, ln_in_b)
    for l in range(DEPTH):
        proj = h @ w_in[l]
        u, q, k, v, q_idx, k_idx, w_idx, gate_pre = jnp.split(proj, split_points, axis=-1)
        y_ssm = s5_branch(u, lam_re[l], lam_im[l], log_dt[l], b_re[l], b_im[l], c_re[l], c_im[l], d_skip[l], w_glu[l])
        y_att = dsa_branch(q.reshape(bsz, seq, N_HEADS, HEAD_DIM),
                           k.reshape(bsz, seq, N_HEADS, HEAD_DIM),
                           v.reshape(bsz, seq, N_HEADS, HEAD_DIM),
                           q_idx.reshape(bsz, seq, IDX_HEADS, IDX_DIM),
                           k_idx, w_idx) @ w_attn_proj[l]
        g_ssm, g_att = jnp.split(jax.nn.sigmoid(gate_pre + b_gate[l]), N_BRANCHES, axis=-1)
        mix = (g_ssm * y_ssm + g_att * y_att) @ w_o[l]
        h = layer_norm(DEEPNORM_ALPHA * h + mix, ln1_g[l], ln1_b[l])
        ffn = moe_ffn(h, w_router[l], b_router[l], w_up[l], b_up[l], w_down[l], b_down[l])
        h = layer_norm(DEEPNORM_ALPHA * h + ffn, ln2_g[l], ln2_b[l])
    return h


_drawn_inputs = setup_inputs


def setup_inputs(seed=0):
    import zlib

    import numpy as np

    out = dict(_drawn_inputs(seed))
    spreads = {}
    factors = {'b_gate': 24.376,
     'lam_re': 64.0,
     'b_router': 3.365,
     'b_up': 8.0,
     'b_down': 6.424,
     'ln2_g': 8.141,
     'ln2_b': 8.007,
     'b_re': 3.373,
     'b_im': 2.874,
     'c_re': 3.028,
     'c_im': 3.312}
    for name, (base, spread) in spreads.items():
        noise = np.random.default_rng([zlib.crc32(name.encode()), seed]).standard_normal(out[name].shape)
        drawn = base * np.exp(spread * noise) if base else spread * noise
        out[name] = jnp.asarray(drawn.astype(out[name].dtype))
    for name, factor in factors.items():
        out[name] = (out[name] * factor).astype(out[name].dtype)
    return out
```

```python
from contextlib import ExitStack

import concourse.bass as bass
import numpy as np
from concourse import mybir

ACT = mybir.ActivationFunctionType
ALU = mybir.AluOpType
AXL = mybir.AxisListType
F32 = mybir.dt.float32
BF16 = mybir.dt.bfloat16
I32 = mybir.dt.int32
U32 = mybir.dt.uint32

P = 128
SEQ = 512
DM = 1024
TT = SEQ // P
KD = DM // P
SSM = 512
GROUP = 16
STATES = 64
SJ = SSM // GROUP * STATES // P
HEADS = 8
HD = 64
NSEL = min(256, SEQ // 4)
NE = 32
TOPK = 4
DFF = 1024
NB = NE + SEQ * TOPK // P
NOROW = SEQ * TOPK
ALPHA = 2.0 ** 0.25
EPS = 1e-5
LIMIT = 7.0
SWI = 1.702
TWO_PI = 6.283185307179586
PI_C1 = 6.28125
PI_C2 = 2029.0 / 1048576.0
PI_C3 = TWO_PI - PI_C1 - PI_C2
PI_SAFE = 3.1415925
ROUND = 12582912.0
ROUND14 = 768.0
MASKED = -3.0e38
TAKEN = -3.3e38
FAR = 1.0e30
SLOPES = [2.0 ** (-8.0 * (h + 1) / HEADS) for h in range(HEADS)]
CHUNK = 4096
C_U, C_Q, C_K, C_V, C_QI, C_KI, C_WI, C_G = 0, 512, 1024, 1536, 2048, 2560, 2624, 2632
NSMALL = 136


class Steps:

    def __init__(self, engine, sem):
        self.engine, self.sem, self.n, self.base = engine, sem, 0, None

    def __call__(self, instruction):
        instruction.then_inc(self.sem, 1)
        self.n += 1
        self.engine.wait_ge(self.sem, self.n if self.base is None else self.base + self.n)


def build(nc, a, out):
    h1_rows = nc.dram_tensor("h1_rows", [SEQ, DM], F32, kind="Internal").ap()
    y_rows = nc.dram_tensor("y_rows", [SEQ * TOPK, DM], F32, kind="Internal").ap()
    slot_list = nc.dram_tensor("slot_list", [P * NB, 1], I32, kind="Internal").ap()

    x_v = a["x"][0].rearrange("(t p) d -> p t d", p=P)
    w_in = a["w_in"][0].rearrange("(k p) n -> p k n", p=P)
    w_glu = a["w_glu"][0].rearrange("(k p) n -> p k n", p=P)
    w_att = a["w_attn_proj"][0].rearrange("(k p) n -> p k n", p=P)
    w_o = a["w_o"][0].rearrange("(k p) n -> p k n", p=P)
    out_v = out[0].rearrange("(t p) d -> p t d", p=P)

    with ExitStack() as ctx:
        def sb(name, shape, dt=F32):
            return ctx.enter_context(nc.sbuf_tensor(name, shape, dt))

        def sem(name):
            return ctx.enter_context(nc.semaphore(name))

        ring = sb("ring", [P, 6, CHUNK])
        hT = ring[:, 2, :].rearrange("p (k t) -> p k t", k=KD)
        qT = ring[:, 3, 0:2048].rearrange("p (k t) -> p k t", k=4)
        kT = ring[:, 3, 2048:4096].rearrange("p (k t) -> p k t", k=4)
        gate = ring[:, 4:6, :].rearrange("p s (k t) -> p (s k) t", k=KD)
        mixT = gate

        craw = ring[:, 4, 0:1024].rearrange("p (r q n) -> p r q n", r=2, q=4)
        bT = ring[:, 4, 1024:2048].rearrange("p (r q n) -> p r q n", r=2, q=4)
        small = ring[:, 4, 2048:2048 + KD * NSMALL].rearrange("p (k n) -> p k n", k=KD)
        cblk = ring[:, 5, 0:1024].rearrange("p (r j c) -> p r j c", r=2, j=SJ)

        h = sb("h", [P, TT, DM])
        uT = sb("uT", [P, 4, SEQ])
        v = sb("v", [P, TT, SSM])
        qiT = sb("qiT", [P, 4, SEQ])
        kiT = sb("kiT", [P, SEQ])
        wi = sb("wi", [P, TT, HEADS])
        far = sb("far", [P, TT, SEQ])
        ident = sb("ident", [P, P])
        tcol = sb("tcol", [P, SEQ])
        qpos = sb("qpos", [P, TT])
        gb = sb("gb", [P, 2, DM])
        gbc = sb("gbc", [P, 2, KD])
        bgate = sb("bgate", [P, 16])
        dskip = sb("dskip", [P, 4])
        eps = sb("eps", [P, 1])
        half_pi = sb("half_pi", [P, 1])
        stats = sb("stats", [P, 2, 6])
        mv = sb("mv", [P, 2])
        rstd = sb("rstd", [P, 2])
        sp_in = sb("sp_in", [P, 3, SJ])
        spw = sb("spw", [P, 24, SJ])
        tcol_i = far[:, 3, :].bitcast(I32)
        braw = far[:, 0:2, 0:SJ * GROUP].rearrange("p r (j c) -> p r j c", c=GROUP)
        bblk = far[:, 2:4, :].rearrange("p r (j c) -> p r j c", c=2 * GROUP)
        scr = sb("scr", [P, 16, SEQ])
        phase, turn, trig = scr[:, 0:2], scr[:, 2:4], scr[:, 4:8].rearrange("p (b r) t -> p b r t", b=2)
        m = scr[:, 8:12]
        w_st = scr[:, 12:16].rearrange("p (b r) t -> p b r t", b=2)
        score, relu = scr[:, 0:2], scr[:, 2:4]
        logit, prob, pT, glu_t = scr[:, 4:6], scr[:, 6:8], scr[:, 8:10], scr[:, 10:12]
        oq, mix_t = scr[:, 12:13], scr[:, 13:16]
        top8 = sb("top8", [P, 8])
        amax = sb("amax", [P, 2])
        rsum = sb("rsum", [P, TT, HEADS])
        rinv = sb("rinv", [P, HEADS])

        w_rt = sb("w_rt", [P, KD, NE])
        b_rt = sb("b_rt", [P, NE])
        lg = sb("lg", [P, NE])
        rt8 = sb("rt8", [P, TT, 8])
        ri8 = sb("ri8", [P, TT, 8], U32)
        rif = sb("rif", [P, TT, 8])
        gates = sb("gates", [P, TT, TOPK])
        gsum = sb("gsum", [P, 2])
        gneg = sb("gneg", [P, 1])
        chosen = sb("chosen", [P, TT, NE])
        chosen_b = sb("chosen_b", [P, TT, NE], BF16)
        before = sb("before", [P, P], BF16)
        ones_b = sb("ones_b", [P, P], BF16)
        rw = sb("rw", [P, 6, NE])
        posw = sb("posw", [P, TT, 3, NE])
        addr = sb("addr", [P, TT, TOPK])
        addr_i = sb("addr_i", [P, TT * TOPK], I32)
        code = sb("code", [P, TT * TOPK], I32)
        empty = sb("empty", [P, NB], I32)
        slots = sb("slots", [P, NB], I32)
        toks = sb("toks", [P, NB], I32)
        tok_now = sb("tok_now", [P, 1], I32)
        row_now = sb("row_now", [P, 1], I32)
        etab_i = sb("etab_i", [1, NB + 1], I32)
        etab = sb("etab", [1, NB + 1])
        bias3 = sb("bias3", [96, 3 * DFF], BF16)
        pick = sb("pick", [96, P], BF16)
        eye96 = sb("eye96", [96, NE])
        E = scr[:, :, :].rearrange("p a b -> p (a b)")
        xg = E[:, 6 * DFF:6 * DFF + DM]
        xcmp = far[0:1, 0, 0:(NB - NE) * NE].rearrange("o (b e) -> o b e", e=NE)
        braw_b = E[0:96, 0:3 * DFF]
        brem = E[0:96, 3 * DFF:6 * DFF]
        hT1 = uT[:, 0:2, :].rearrange("p a t -> p (a t)").rearrange("p (k t) -> p k t", k=KD)
        xT = v[:, 0:2, :].rearrange("p a t -> p (a t)").rearrange("p (k t) -> p k t", k=KD)
        actT = v[:, 2:4, :].rearrange("p a t -> p (a t)").rearrange("p (k t) -> p k t", k=KD)
        swg, sig, swl, act_s = qiT[:, 0, :], qiT[:, 1, :], qiT[:, 2, :], far[:, 0:2, :]
        ysb = far[:, 2:4, :]

        ps = [ctx.enter_context(nc.psum_tensor(f"ps{i}", [P, 512], F32)) for i in range(8)]

        s_x = sem("x_loaded")
        s_dend = sem("last_vector_steps")
        s_par = [sem(f"params{i}_loaded") for i in range(4)]
        s_small = sem("small_loaded")
        s_lnp = sem("ln_in_params_loaded")
        s_gb1, s_gb2, s_gb3 = sem("ln_in_rows_loaded"), sem("ln1_rows_loaded"), sem("ln2_rows_loaded")
        s_w = [sem(f"weights_loaded{i}") for i in range(6)]
        s_wi = sem("w_idx_done")
        s_const = sem("pool_constants")
        s_one = sem("vector_constants")
        s_d, s_a, s_g = sem("vector_steps"), sem("scalar_steps"), sem("pool_steps")
        s_xhat, s_rstd, s_var = sem("xhat_ready"), sem("std_ready"), sem("var_ready")
        s_lnT, s_hT = sem("xhat_transposed"), sem("hT_ready")
        s_hrow = sem("h_rows_ready")
        s_tile, s_tile_a, s_tile_v = sem("tile_done"), sem("tile_taken_by_scalar"), sem("tile_taken_by_vector")
        s_dt, s_sc = sem("dt_ready"), sem("sincos_ready")
        s_th = sem("theta_ready")
        s_bb, s_bbT, s_bT = sem("b_blocks_ready"), sem("b_transposed"), sem("bT_ready")
        s_cT, s_cblk, s_tau = sem("c_transposed"), sem("c_blocks_ready"), sem("turns_ready")
        s_ph, s_trig, s_phfree, s_rot = sem("phase_ready"), sem("trig_ready"), sem("phase_used"), sem("trig_used")
        s_bu, s_bufree = sem("bu_done"), sem("bu_taken")
        s_st, s_stfree = sem("states_ready"), sem("states_used")
        s_y, s_yfree, s_gelu = sem("y_done"), sem("y_taken"), sem("gelu_done")
        s_dot, s_relu, s_relufree = sem("dots_done"), sem("relu_ready"), sem("relu_used")
        s_scored, s_masked, s_far0 = sem("scores_summed"), sem("scores_masked"), sem("first_tile_distances")
        s_far = sem("distances_ready")
        s_qk, s_lg, s_pr = sem("qk_done"), sem("logits_ready"), sem("probs_ready")
        s_pTp, s_pT, s_pv = sem("probs_transposed"), sem("pT_ready"), sem("pv_done")
        s_on, s_oTp, s_oT = sem("o_normed"), sem("o_transposed"), sem("oT_ready")
        s_gg, s_mix = sem("glu_gate_ready"), sem("mix_ready")
        s_wo, s_wofree = sem("wo_done"), sem("wo_taken")
        s_h1, s_h1T, s_h1e, s_lgt, s_lgfree = (sem("h1_ready"), sem("h1_transposed"), sem("h1T_ready"),
                                               sem("router_done"), sem("router_taken"))
        s_v8, s_ge = sem("top_ready"), sem("gate_exp_ready")
        s_h1row = sem("h1_rows_written")
        s_chosen, s_cnt, s_adr = sem("chosen_ready"), sem("counts_done"), sem("addresses_ready")
        s_scat, s_slots = sem("list_written"), sem("slots_loaded")
        s_tok, s_tab = sem("token_ids_ready"), sem("table_ready")
        s_bias, s_b3l, s_b3 = sem("biases_loaded"), sem("bias_parts_ready"), sem("pick_ready")
        s_gat, s_tnow, s_rnow = sem("rows_gathered"), sem("tokens_picked"), sem("rows_picked")
        s_tr, s_ev = sem("moe_transposed"), sem("moe_evacuated")
        s_up, s_sig, s_act, s_upfree = sem("up_done"), sem("sigmoid_ready"), sem("act_ready"), sem("up_taken")
        s_g7 = sem("gate_clipped")
        s_cu = sem("chunk_used")
        s_ysb, s_yout = sem("y_ready"), sem("pool_stores_done")
        s_yld = [sem(f"y_loaded{t}") for t in range(TT)]
        s_oln, s_out = sem("out_ready"), sem("out_written")

        FRONT = [("u", C_U), ("qi", C_QI), ("q", C_Q), ("k", C_K), ("v", C_V)]
        FRONT += [("g", C_G + 512 * i) for i in range(4)]
        FRONT += [("glu", 0), ("glu", 1), ("att", 0), ("wo", 0), ("wo", 1)]
        NFRONT = len(FRONT)

        tiles = []
        for kind, n in (("u", 4), ("qi", 4), ("ki", 1), ("q", 4), ("k", 4), ("v", 4), ("g", 16)):
            tiles += [(kind, i, "a") for i in range(n)]
        for i in range(8):
            tiles += [("gg", i, "a"), ("val", i, "v")]
        for i in range(8):
            tiles += [("at", i, "v")]
        taken, na, nv = [], 0, 0
        for _, _, who in tiles:
            na, nv = na + (who == "a"), nv + (who == "v")
            taken.append((s_tile_a, na) if who == "a" else (s_tile_v, nv))
        first_tile = {}
        for n, (kind, _, _) in enumerate(tiles):
            first_tile.setdefault(kind, n)

        tiles_upto = [4, 8, 13, 17, 21, 25, 29, 33, 37, 45, 53, 61]

        NQT = [P * (t + 1) for t in range(TT)]
        STEPS = [(t, hh) for t in range(TT) for hh in range(HEADS)]

        ctx.enter_context(nc.allow_non_contiguous_dma(reason="small parameters, one number for each partition"))
        block = ctx.enter_context(nc.Block())

        @block.sync
        def _(sp):
            for t in range(TT):
                sp.dma_start(h[:, t, :], x_v[:, t, :]).then_inc(s_x, 16)

            def chunk(n):
                kind, c = FRONT[n]
                dst = ring[:, n % 2, :]
                if n >= 2:
                    sp.wait_ge(s_tile, tiles_upto[n - 2])
                if kind == "glu":
                    d4 = dst.rearrange("p (k r n) -> p k r n", k=4, r=2)
                    for r in range(2):
                        sp.dma_start(d4[:, :, r, :], w_glu[:, :, DM * r + 512 * c:DM * r + 512 * c + 512])\
                            .then_inc(s_w[n % 2], 8 * 2)
                elif kind == "att":
                    sp.dma_start(dst.rearrange("p (k n) -> p k n", k=4), w_att).then_inc(s_w[n % 2], 16)
                else:
                    src = w_o[:, :, 512 * c:512 * c + 512] if kind == "wo" else w_in[:, :, c:c + 512]
                    sp.dma_start(dst.rearrange("p (k n) -> p k n", k=KD), src).then_inc(s_w[n % 2], 16)

            chunk(0)
            sp.dma_start(small[:, :, 0:64], w_in[:, :, C_KI:C_KI + 64]).then_inc(s_small, 16)
            sp.dma_start(small[:, :, 64:136], w_in[:, :, C_KI:C_KI + 72]).then_inc(s_small, 16)
            for n in range(1, NFRONT):
                chunk(n)

            def expert_chunk(c, e):
                if c < 4:
                    half, lin = c // 2, c % 2
                    col = DFF * lin + 512 * half
                    src = a["w_up"][0, e].rearrange("(k p) n -> p k n", p=P)[:, :, col:col + 512] if isinstance(e, int) \
                        else a["w_up"][0, bass.ds(e, 1)].rearrange("o (k p) n -> p (o k) n", p=P)[:, :, col:col + 512]
                    dst = ring[:, c, :].rearrange("p (k n) -> p k n", k=KD)
                else:
                    r0 = (c - 4) * 512
                    src = a["w_down"][0, e][r0:r0 + 512, :].rearrange("(k p) n -> p k n", p=P) if isinstance(e, int) \
                        else a["w_down"][0, bass.ds(e, 1), r0:r0 + 512, :].rearrange("o (k p) n -> p (o k) n", p=P)
                    dst = ring[:, c, :].rearrange("p (k n) -> p k n", k=4)
                sp.dma_start(dst, src).then_inc(s_w[c], 16)

            sp.wait_ge(s_tile, first_tile["gg"])
            expert_chunk(2, 0)
            sp.wait_ge(s_qk, len(STEPS))
            expert_chunk(3, 0)
            sp.wait_ge(s_wo, 2 * TT)
            expert_chunk(0, 0)
            expert_chunk(1, 0)
            expert_chunk(4, 0)
            expert_chunk(5, 0)
            sp.wait_ge(s_scat, 16 * TT * TOPK)
            sp.dma_start(slots[:, :], slot_list.rearrange("(p b) o -> p (b o)", p=P)).then_inc(s_slots, 16)
            sp.wait_ge(s_tab, 1)
            nblk = sp.value_load(etab_i[0:1, NB:NB + 1], min_val=NE, max_val=NB - 1)
            with sp.Fori(1, nblk) as i:
                e = sp.value_load(etab_i[0:1, bass.ds(i, 1)], min_val=0, max_val=NE - 1)
                for c in range(6):
                    sp.wait_ge(s_cu, (i - 1) * 6 + c + 2)
                    expert_chunk(c, e)
            for t in range(TT):
                if t == 0:
                    out_rows = sp.snap(nblk * 16 + 16)
                    sp.wait_ge(s_yout, out_rows)
                sp.dma_start(ring[:, t, :], y_rows[P * TOPK * t:P * TOPK * (t + 1), :]
                             .rearrange("(p k) d -> p (k d)", k=TOPK)).then_inc(s_yld[t], 16)
            for t in range(TT):
                sp.wait_ge(s_oln, t + 1)
                sp.dma_start(out_v[:, t, :], h[:, t, :]).then_inc(s_out, 16)
            sp.wait_ge(s_out, 16 * TT)

        @block.gpsimd
        def _(pool):
            step = Steps(pool, s_g)
            g = nc.gpsimd
            step(g.memset(ident[:, :], 0.0))
            g.affine_select(out=ident[:, :], in_=ident[:, :], compare_op=ALU.not_equal, fill=1.0, base=0,
                            pattern=[[-1, P]], channel_multiplier=1).then_inc(s_const, 1)
            step(g.iota(tcol_i[:, :], pattern=[[1, SEQ]], base=0, channel_multiplier=0))
            g.tensor_copy(tcol[:, :], tcol_i[:, :]).then_inc(s_const, 1)
            pool.wait_ge(s_const, 2)
            for j in range(SJ):
                if j == 0:
                    pool.wait_ge(s_tau, 1)
                if j >= 2:
                    pool.wait_ge(s_phfree, j - 1)
                tau, tau_hi, tau_lo = (spw[:, q, j:j + 1] for q in (20, 21, 22))
                f, r = phase[:, j % 2, :], turn[:, 0, :]
                lo = turn[:, 1, :]
                step(g.tensor_scalar(r, tcol[:, :], tau, ROUND, ALU.mult, ALU.add))
                step(g.tensor_scalar(r, r, ROUND, None, ALU.subtract))
                step(g.tensor_scalar(f, tcol[:, :], tau_hi, None, ALU.mult))
                step(g.tensor_tensor(f, f, r, ALU.subtract))
                step(g.tensor_scalar(lo, tcol[:, :], tau_lo, None, ALU.mult))
                step(g.tensor_tensor(f, f, lo, ALU.add))
                g.tensor_scalar(f, f, 0.5 * 0.9999999, -0.5 * 0.9999999, ALU.min, ALU.max).then_inc(s_ph, 1)
            step(g.memset(ones_b[:, :], 1.0))
            step(g.memset(before[:, :], 1.0))
            step(g.affine_select(out=before[:, :], in_=before[:, :], compare_op=ALU.is_gt, fill=0.0, base=0,
                                 pattern=[[1, P]], channel_multiplier=-1))
            step(g.memset(empty[:, :], NOROW))
            g.dma_start(slot_list.rearrange("(p b) o -> p (b o)", p=P), empty[:, :]).then_inc(s_yout, 16)
            step(g.iota(code[:, :], pattern=[[P * TOPK, TT], [1, TOPK]], base=0, channel_multiplier=TOPK))
            step(g.memset(eye96[:, :], 0.0))
            for r in range(3):
                step(g.affine_select(out=eye96[:, :], in_=eye96[:, :], compare_op=ALU.not_equal, fill=1.0,
                                     base=-NE * r, pattern=[[-1, NE]], channel_multiplier=1))
            pool.wait_ge(s_gb1, 32)
            pool.wait_ge(s_lnT, KD)
            for t in range(TT):
                step(g.tensor_tensor(h[:, t, :], h[:, t, :], gb[:, 0, :], ALU.mult))
                g.tensor_tensor(h[:, t, :], h[:, t, :], gb[:, 1, :], ALU.add).then_inc(s_hrow, 1)
                pool.wait_ge(s_hrow, t + 1)
            pool.wait_ge(s_far0, 1)
            g.affine_select(out=far[:, 0, :], in_=far[:, 0, :], compare_op=ALU.is_ge, fill=FAR, base=0,
                            pattern=[[-1, SEQ]], channel_multiplier=1).then_inc(s_masked, 1)
            for t in range(1, TT):
                pool.wait_ge(s_relufree, HEADS * t)
                g.affine_select(out=score[:, t % 2, P * t:P * t + P], in_=score[:, t % 2, P * t:P * t + P],
                                compare_op=ALU.is_ge, fill=MASKED, base=0, pattern=[[-1, P]],
                                channel_multiplier=1).then_inc(s_masked, 1)
            pool.wait_ge(s_yout, 16)
            for t in range(TT):
                pool.wait_ge(s_adr, t + 1)
                for k in range(TOPK):
                    c = TOPK * t + k
                    g.indirect_dma_start(slot_list, bass.IndirectOffsetOnAxis(ap=addr_i[:, c:c + 1], axis=0),
                                         code[:, c:c + 1], None, bounds_check=P * NB - 1,
                                         oob_is_err=False).then_inc(s_scat, 16)
            pool.wait_ge(s_tab, 1)
            nblk = pool.value_load(etab_i[0:1, NB:NB + 1], min_val=NE, max_val=NB - 1)
            pool.wait_ge(s_h1row, 16 * TT)
            g.memset(xg[:, :], 0.0).then_inc(s_one, 1)
            pool.wait_ge(s_one, 1)

            zero, last_tok, last_row = (pool.alloc_register(x) for x in ("nothing", "last_token", "last_row"))
            pool.reg_mov(zero, 0)

            def gather(i):
                pool.wait_ge(s_tnow, i + 1)
                pool.reg_add(last_tok, zero, SEQ - 1)
                g.indirect_dma_start(xg[:, :], None, h1_rows,
                                     bass.IndirectOffsetOnAxis(ap=tok_now[:, 0:1], axis=0),
                                     bounds_check=last_tok, oob_is_err=False).then_inc(s_gat, 16)

            gather(0)
            with pool.Fori(0, nblk) as i:
                pool.wait_ge(s_tr, i * 4 + 2)
                gather(i + 1)
                pool.wait_ge(s_rnow, i + 1)
                pool.wait_ge(s_ysb, i * 2 + 3)
                pool.reg_add(last_row, zero, SEQ * TOPK - 1)
                g.indirect_dma_start(y_rows, bass.IndirectOffsetOnAxis(ap=row_now[:, 0:1], axis=0),
                                     ysb.rearrange("p a b -> p (a b)"), None, bounds_check=last_row,
                                     oob_is_err=False).then_inc(s_yout, 16)
            pool.wait_ge(s_yout, nblk * 16 + 16)
            pool.wait_ge(s_gat, nblk * 16 + 16)

        @block.scalar
        def _(act):
            s = nc.scalar
            step = Steps(act, s_a)
            act.dma_start(sp_in[:, 0, :], a["lam_re"][0].rearrange("(j w) n -> (w n) j", w=2)).then_inc(s_par[0], 16)
            act.dma_start(sp_in[:, 1, :], a["lam_im"][0].rearrange("(j w) n -> (w n) j", w=2)).then_inc(s_par[0], 16)
            for w in range(2):
                src = a["log_dt"].rearrange("o (j w) -> w o j", w=2)[w].partition_broadcast(STATES)
                act.dma_start(sp_in[64 * w:64 * w + 64, 2, :], src.rearrange("p o j -> p (o j)")
                              if len(src.shape) == 3 else src).then_inc(s_par[0], 16)
            act.dma_start(gbc[:, 0, :], a["ln_in_g"].rearrange("(k p) -> p k", p=P)).then_inc(s_lnp, 16)
            act.dma_start(gbc[:, 1, :], a["ln_in_b"].rearrange("(k p) -> p k", p=P)).then_inc(s_lnp, 16)
            for r, nm in enumerate(("b_re", "b_im")):
                act.dma_start(braw[:, r], a[nm][0].rearrange("(j w) n c -> (w n) j c", w=2)).then_inc(s_par[1], 16)
            for r, nm in enumerate(("c_re", "c_im")):
                src = a[nm][0].rearrange("(q g) c n -> (g c) q n", q=4)
                for dup in range(2):
                    act.dma_start(craw[:, r, :, 64 * dup:64 * dup + 64], src).then_inc(s_par[2], 16)
            act.dma_start(bgate[:, :], a["b_gate"][0].rearrange("(k p) -> p k", p=P)).then_inc(s_par[3], 16)
            act.dma_start(dskip[:, :], a["d_skip"][0].rearrange("(q g) c -> (g c) q", q=4)).then_inc(s_par[3], 16)
            for r, nm in enumerate(("ln_in_g", "ln_in_b")):
                act.dma_start(gb[:, r, :], a[nm].partition_broadcast(P)).then_inc(s_gb1, 16)
            act.dma_start(w_rt[:, :, :], a["w_router"][0].rearrange("(k p) n -> p k n", p=P)).then_inc(s_par[3], 16)
            act.dma_start(b_rt[:, :], a["b_router"][0].partition_broadcast(P)).then_inc(s_par[3], 16)

            act.wait_ge(s_par[0], 64)
            s.activation(spw[:, 0, :], sp_in[:, 2, :], ACT.Exp).then_inc(s_dt, 1)
            act.wait_ge(s_th, 1)
            s.activation(spw[:, 2, :], spw[:, 1, :], ACT.Exp).then_inc(s_dt, 1)
            for t in range(TT):
                act.wait_ge(s_var, t + 1)
                s.activation(rstd[:, 0:1], mv[:, 1:2], ACT.Sqrt, bias=eps[:, 0:1]).then_inc(s_rstd, 1)
            act.wait_ge(s_th, 2)
            s.activation(spw[:, 5, :], spw[:, 4, :], ACT.Sin).then_inc(s_sc, 1)
            step(s.activation(spw[:, 6, :], spw[:, 4, :], ACT.Abs))
            s.activation(spw[:, 7, :], spw[:, 6, :], ACT.Sin, scale=-1.0, bias=half_pi[:, 0:1]).then_inc(s_sc, 1)
            act.wait_ge(s_lnp, 32)
            for k in range(KD):
                act.wait_ge(s_lnT, k + 1)
                s.activation(hT[:, k, :], ps[4 + k % 4][:, :], ACT.Identity, scale=gbc[:, 0, k:k + 1],
                             bias=gbc[:, 1, k:k + 1]).then_inc(s_hT, 1)
            for q in range(8):
                act.wait_ge(s_bbT, q + 1)
                r, qq = q // 4, q % 4
                s.activation(bT[:, r, qq, :], ps[4 + q % 4][:, 0:P], ACT.Copy).then_inc(s_bT, 1)

            def trigs(j):
                act.wait_ge(s_ph, j + 1)
                if j >= 2:
                    act.wait_ge(s_rot, j - 1)
                s.activation(trig[:, j % 2, 1, :], phase[:, j % 2, :], ACT.Sin, scale=TWO_PI).then_inc(s_trig, 1)
                step(s.activation(trig[:, j % 2, 0, :], phase[:, j % 2, :], ACT.Abs))
                s.activation(trig[:, j % 2, 0, :], trig[:, j % 2, 0, :], ACT.Sin, scale=-TWO_PI,
                             bias=half_pi[:, 0:1]).then_inc(s_phfree, 1)

            def gelu(q):
                act.wait_ge(s_yfree, q + 1)
                s.activation(uT[:, q, :], uT[:, q, :], ACT.Gelu_apprx_tanh).then_inc(s_gelu, 1)

            def relus(n):
                act.wait_ge(s_dot, n + 1)
                if n >= 2:
                    act.wait_ge(s_relufree, n - 1)
                t = 1 + n // HEADS
                s.activation(relu[:, n % 2, 0:NQT[t]], ps[5 + n % 2][:, 0:NQT[t]], ACT.Relu,
                             scale=64.0 ** -0.5).then_inc(s_relu, 1)

            def take(n):
                kind, i, _ = tiles[n]
                act.wait_ge(s_tile, n + 1)
                src = ps[n % 2]
                if kind == "g":
                    ins = s.activation(gate[:, i, :], src[:, :], ACT.Sigmoid, bias=bgate[:, i:i + 1])
                elif kind == "gg":
                    if i >= 2:
                        act.wait_ge(s_tile_v, i - 1)
                    ins = s.activation(glu_t[:, i % 2, :], src[:, :], ACT.Sigmoid)
                elif kind == "ki":
                    ins = s.activation(kiT[:, :], src[:, :], ACT.Copy)
                else:
                    dst = {"u": uT, "qi": qiT, "q": qT, "k": kT, "v": v}[kind]
                    ins = s.activation(dst[:, i, :], src[:, :], ACT.Copy)
                ins.then_inc(s_tile_a, 1)

            n = 0
            while tiles[n][0] == "u":
                take(n)
                n += 1
            for j in range(SJ):
                trigs(j)
                take(n)
                n += 1
            while tiles[n][0] != "g":
                take(n)
                n += 1
            for i in range(24):
                relus(i)
            act.wait_ge(s_par[3], 64)
            for q in range(4):
                gelu(q)
            while tiles[n][0] == "g":
                take(n)
                n += 1

            def exps(i):
                t, hh = STEPS[i]
                act.wait_ge(s_lg, i + 1)
                if i >= 2:
                    act.wait_ge(s_pTp, i - 1)
                s.activation(prob[:, i % 2, 0:NQT[t]], logit[:, i % 2, 0:NQT[t]], ACT.Exp, scale=HD ** -0.5,
                             bias=amax[:, i % 2:i % 2 + 1], accum_out=rsum[:, t, hh:hh + 1]).then_inc(s_pr, 1)

            def keep_pT(i):
                t, hh = STEPS[i]
                act.wait_ge(s_pTp, i + 1)
                if i >= 2:
                    act.wait_ge(s_pv, i - 1)
                s.activation(pT[:, i % 2, 0:NQT[t]], ps[7][:, 0:NQT[t]], ACT.Copy).then_inc(s_pT, 1)

            for i in range(len(STEPS) + 2):
                if i < len(STEPS):
                    exps(i)
                if 1 <= i <= len(STEPS):
                    keep_pT(i - 1)
                if i % 4 == 1 and n < first_tile["at"]:
                    take(n)
                    n += 2
                if i >= 2 and STEPS[i - 2][1] == HEADS - 1:
                    t = STEPS[i - 2][0]
                    act.wait_ge(s_oTp, t + 1)
                    s.activation(qiT[:, :, P * t:P * t + P], ps[3][:, :].rearrange("p (k q) -> p k q", k=4),
                                 ACT.Copy).then_inc(s_oT, 1)
            while n < first_tile["at"]:
                take(n)
                n += 2
            act.wait_ge(s_hrow, TT)
            for r, nm in enumerate(("ln1_g", "ln1_b")):
                act.dma_start(gb[:, r, :], a[nm][0].partition_broadcast(P)).then_inc(s_gb2, 16)
            for t in range(TT):
                act.wait_ge(s_var, TT + t + 1)
                s.activation(rstd[:, 0:1], mv[:, 1:2], ACT.Sqrt, bias=eps[:, 0:1]).then_inc(s_rstd, 1)
                act.wait_ge(s_h1, t + 1)
                act.dma_start(h1_rows.rearrange("(t p) d -> p t d", p=P)[:, t, :], h[:, t, :]).then_inc(s_h1row, 16)
                for r in range(2):
                    act.wait_ge(s_h1T, 2 * t + r + 1)
                    if t > 0:
                        act.wait_ge(s_lgt, t)
                    s.activation(hT1[:, 4 * r:4 * r + 4, :], ps[6 + r][:, :].rearrange("p (k q) -> p k q", k=4),
                                 ACT.Copy).then_inc(s_h1e, 1)
                act.wait_ge(s_v8, t + 1)
                s.activation(gates[:, t, :], rt8[:, t, 0:TOPK], ACT.Exp, bias=gneg[:, 0:1],
                             accum_out=gsum[:, 0:1]).then_inc(s_ge, 1)
            for r, nm in enumerate(("ln2_g", "ln2_b")):
                act.dma_start(gb[:, r, :], a[nm][0].partition_broadcast(P)).then_inc(s_gb3, 16)
            act.wait_ge(s_mix, 8)
            for r in range(3):
                act.dma_start(braw_b[NE * r:NE * r + NE, 0:2 * DFF], a["b_up"][0]).then_inc(s_bias, 16)
                act.dma_start(braw_b[NE * r:NE * r + NE, 2 * DFF:3 * DFF], a["b_down"][0]).then_inc(s_bias, 16)
            act.wait_ge(s_tab, 1)
            nblk = act.value_load(etab_i[0:1, NB:NB + 1], min_val=NE, max_val=NB - 1)

            def evac(dst, half, wait):
                act.wait_ge(s_tr, wait)
                s.activation(dst[:, 4 * half:4 * half + 4, :],
                             ps[6 + half][:, :].rearrange("p (k q) -> p k q", k=4), ACT.Copy).then_inc(s_ev, 1)

            act.sem_inc(s_ysb, 1)
            evac(xT, 0, 1)
            evac(xT, 1, 2)
            with act.Fori(0, nblk) as i:
                for half in range(2):
                    act.wait_ge(s_g7, i * 2 + half + 1)
                    s.activation(sig, swg, ACT.Sigmoid, scale=SWI).then_inc(s_sig, 1)
                    if half == 0:
                        evac(actT, 0, i * 4 + 3)
                evac(actT, 1, i * 4 + 4)
                evac(xT, 0, i * 4 + 5)
                evac(xT, 1, i * 4 + 6)
                act.wait_ge(s_cu, i * 6 + 7)
                for r in range(2):
                    if r == 0:
                        act.wait_ge(s_rnow, i + 1)
                    s.activation(ysb[:, r, :], ps[4 + r][:, :], ACT.Copy).then_inc(s_ysb, 1)
            act.wait_ge(s_ysb, nblk * 2 + 1)
            for t in range(TT):
                act.wait_ge(s_var, 2 * TT + t + 1)
                s.activation(rstd[:, 0:1], mv[:, 1:2], ACT.Sqrt, bias=eps[:, 0:1]).then_inc(s_rstd, 1)

        @block.vector
        def _(dve):
            d = nc.vector
            step = Steps(dve, s_d)
            nvar = [0]
            step(d.memset(eps[:, :], EPS))
            step(d.memset(half_pi[:, :], TWO_PI / 4))

            def norm(row, n, step):
                for r in range(2):
                    step(d.bn_stats(stats[:, r, :], row[:, 512 * r:512 * r + 512]))
                d.bn_aggr(mv[:, :], stats[:, :, :]).then_inc(s_var, 1)
                dve.wait_ge(s_rstd, n)
                step(d.reciprocal(rstd[:, 1:2], rstd[:, 0:1]))
                dve.wait_ge(s_var, n)
                return d.tensor_scalar(row, row, mv[:, 0:1], rstd[:, 1:2], ALU.subtract, ALU.mult)

            lr, li = sp_in[:, 0, :], sp_in[:, 1, :]
            W = lambda q: spw[:, q, :]
            dve.wait_ge(s_dt, 1)
            d.tensor_tensor(W(1), lr, W(0), ALU.mult).then_inc(s_th, 1)
            step(d.tensor_tensor(W(3), li, W(0), ALU.mult))
            step(d.tensor_scalar(W(8), W(3), 1.0 / TWO_PI, ROUND, ALU.mult, ALU.add))
            step(d.tensor_scalar(W(8), W(8), ROUND, None, ALU.subtract))
            for c in (PI_C1, PI_C2, PI_C3):
                step(d.scalar_tensor_tensor(W(3), W(8), -c, W(3), ALU.mult, ALU.add))
            d.tensor_scalar(W(4), W(3), PI_SAFE, -PI_SAFE, ALU.min, ALU.max).then_inc(s_th, 1)
            step(d.tensor_scalar(W(20), W(3), 1.0 / TWO_PI, None, ALU.mult))
            step(d.tensor_scalar(W(21), W(20), ROUND14, None, ALU.add))
            step(d.tensor_scalar(W(21), W(21), ROUND14, None, ALU.subtract))
            d.tensor_tensor(W(22), W(20), W(21), ALU.subtract).then_inc(s_tau, 1)
            dve.wait_ge(s_x, 16 * TT)
            for t in range(TT):
                norm(h[:, t, :], t + 1, step).then_inc(s_xhat, 1)
                dve.wait_ge(s_xhat, t + 1)
            dve.wait_ge(s_sc, 2)
            step(d.tensor_tensor(W(9), W(2), W(7), ALU.mult))
            step(d.tensor_scalar(W(9), W(9), 1.0, None, ALU.subtract))
            step(d.tensor_tensor(W(10), W(2), W(5), ALU.mult))
            step(d.tensor_tensor(W(11), lr, lr, ALU.mult))
            step(d.tensor_tensor(W(12), li, li, ALU.mult))
            step(d.tensor_tensor(W(11), W(11), W(12), ALU.add))
            step(d.reciprocal(W(11), W(11)))
            for dst, (p0, q0), (p1, q1), op in ((14, (9, lr), (10, li), ALU.add), (15, (10, lr), (9, li), ALU.subtract)):
                step(d.tensor_tensor(W(12), W(p0), q0, ALU.mult))
                step(d.tensor_tensor(W(13), W(p1), q1, ALU.mult))
                step(d.tensor_tensor(W(dst), W(12), W(13), op))
                step(d.tensor_tensor(W(dst), W(dst), W(11), ALU.mult))
            dve.wait_ge(s_par[1], 32)
            cr, ci = (spw[:, q, :].unsqueeze(2).to_broadcast([P, SJ, GROUP]) for q in (14, 15))
            tmp = m[:, 0:2, 0:SJ * GROUP].rearrange("p r (j c) -> p r j c", c=GROUP)
            dve.wait_ge(s_const, 2)
            step(d.memset(bblk[:, :, :, :], 0.0))
            for r, (x0, x1, op) in enumerate(((cr, ci, ALU.subtract), (ci, cr, ALU.add))):
                step(d.tensor_tensor(tmp[:, 0], x0, braw[:, 0], ALU.mult))
                step(d.tensor_tensor(tmp[:, 1], x1, braw[:, 1], ALU.mult))
                for w in range(2):
                    rows = slice(64 * w, 64 * w + 64)
                    ins = d.tensor_tensor(bblk[rows, r, :, GROUP * w:GROUP * w + GROUP], tmp[rows, 0], tmp[rows, 1], op)
                    if r == 1 and w == 1:
                        ins.then_inc(s_bb, 1)
                    else:
                        step(ins)
            step(d.memset(cblk[:, :, :, :], 0.0))
            for r in range(2):
                dve.wait_ge(s_cT, 4 * r + 4)
                src = ps[2 + r][:, :].rearrange("p (j w c) -> p j w c", w=2, c=GROUP)
                for w in range(2):
                    rows = slice(64 * w, 64 * w + 64)
                    ins = d.tensor_scalar(cblk[rows, r, :, GROUP * w:GROUP * w + GROUP], src[rows, :, w, :],
                                          1.0 if r == 0 else -1.0, None, ALU.mult)
                    if (r, w) == (1, 1):
                        ins.then_inc(s_cblk, 1)
                        dve.wait_ge(s_cblk, 1)
                    else:
                        step(ins)

            def s5(j):
                dve.wait_ge(s_bu, j + 1)
                dve.wait_ge(s_phfree, j + 1)
                c, sn = trig[:, j % 2, 0, :], trig[:, j % 2, 1, :]
                br, bi = ps[2], ps[3]
                step(d.tensor_tensor(m[:, 0, :], br[:, :], c, ALU.mult))
                step(d.tensor_tensor(m[:, 1, :], bi[:, :], sn, ALU.mult))
                step(d.tensor_tensor(m[:, 2, :], bi[:, :], c, ALU.mult))
                d.tensor_tensor(m[:, 3, :], br[:, :], sn, ALU.mult).then_inc(s_bufree, 1)
                dve.wait_ge(s_bufree, j + 1)
                step(d.tensor_tensor(m[:, 0, :], m[:, 0, :], m[:, 1, :], ALU.add))
                step(d.tensor_tensor(m[:, 2, :], m[:, 2, :], m[:, 3, :], ALU.subtract))
                decay = spw[:, 2, j:j + 1].to_broadcast([P, SEQ])
                step(d.tensor_tensor_scan(m[:, 1, :], decay, m[:, 0, :], 0.0, ALU.mult, ALU.add))
                step(d.tensor_tensor_scan(m[:, 3, :], decay, m[:, 2, :], 0.0, ALU.mult, ALU.add))
                if j >= 2:
                    dve.wait_ge(s_stfree, j - 1)
                wr, w_im = w_st[:, j % 2, 0, :], w_st[:, j % 2, 1, :]
                step(d.tensor_tensor(m[:, 0, :], m[:, 1, :], c, ALU.mult))
                step(d.tensor_tensor(m[:, 2, :], m[:, 3, :], sn, ALU.mult))
                step(d.tensor_tensor(wr, m[:, 0, :], m[:, 2, :], ALU.subtract))
                step(d.tensor_tensor(m[:, 0, :], m[:, 1, :], sn, ALU.mult))
                d.tensor_tensor(m[:, 2, :], m[:, 3, :], c, ALU.mult).then_inc(s_rot, 1)
                dve.wait_ge(s_rot, j + 1)
                d.tensor_tensor(w_im, m[:, 0, :], m[:, 2, :], ALU.add).then_inc(s_st, 1)
                dve.wait_ge(s_st, j + 1)

            def y_out(q):
                dve.wait_ge(s_stfree, 4 * q + 4)
                if q == 0:
                    dve.wait_ge(s_par[3], 64)
                d.scalar_tensor_tensor(uT[:, q, :], uT[:, q, :], dskip[:, q:q + 1], ps[4][:, :],
                                       ALU.mult, ALU.add).then_inc(s_yfree, 1)

            for j in range(SJ):
                s5(j)
                if j >= 5 and j % 4 == 1:
                    y_out((j - 5) // 4)
            y_out(3)

            dve.wait_ge(s_wi, 1)
            step(d.tensor_scalar(wi[:, :, :], wi_ps(ps), HEADS ** -0.5, None, ALU.mult))
            step(d.tensor_tensor(m[:, 0, 0:P], ident[:, :], tcol[:, 0:P], ALU.mult))
            step(d.reduce_sum(qpos[:, 0:1], m[:, 0, 0:P], AXL.X))
            for t in range(1, TT):
                step(d.tensor_scalar(qpos[:, t:t + 1], qpos[:, 0:1], float(P * t), None, ALU.add))
            dve.wait_ge(s_bbT, 8)
            d.tensor_scalar(far[:, 0, :], tcol[:, :], -1.0, qpos[:, 0:1], ALU.mult, ALU.add).then_inc(s_far0, 1)
            for t in range(1, TT):
                nk = NQT[t]
                sc = score[:, t % 2, 0:nk]
                for hh in range(HEADS):
                    n = HEADS * (t - 1) + hh
                    dve.wait_ge(s_relu, n + 1)
                    src, wcol = relu[:, n % 2, 0:nk], wi[:, t, hh:hh + 1]
                    if hh == 0:
                        ins = d.tensor_scalar(sc, src, wcol, None, ALU.mult)
                    else:
                        ins = d.scalar_tensor_tensor(sc, src, wcol, sc, ALU.mult, ALU.add)
                    ins.then_inc(s_relufree, 1)
                    dve.wait_ge(s_relufree, n + 1)
                dve.wait_ge(s_masked, t + 1)
                for _ in range(NSEL // 8):
                    step(d.max(top8[:, :], sc))
                    step(d.match_replace(sc, top8[:, :], sc, TAKEN))
                step(d.tensor_scalar(far[:, t, 0:nk], sc, TAKEN, FAR, ALU.not_equal, ALU.mult))
                d.scalar_tensor_tensor(far[:, t, 0:nk], far[:, t, 0:nk], qpos[:, t:t + 1], tcol[:, 0:nk],
                                       ALU.add, ALU.subtract).then_inc(s_far, 1)
                dve.wait_ge(s_far, t)
            dve.wait_ge(s_masked, 1)

            def logits(i):
                t, hh = STEPS[i]
                nk = NQT[t]
                dve.wait_ge(s_qk, i + 1)
                if i >= 2:
                    dve.wait_ge(s_pr, i - 1)
                lgt = logit[:, i % 2, 0:nk]
                step(d.scalar_tensor_tensor(lgt, far[:, t, 0:nk], -SLOPES[hh] * HD ** 0.5, ps[5 + i % 2][:, 0:nk],
                                            ALU.mult, ALU.add))
                step(d.reduce_max(top8[:, 0:1], lgt, AXL.X))
                d.tensor_scalar(amax[:, i % 2:i % 2 + 1], top8[:, 0:1], -HD ** -0.5, None, ALU.mult).then_inc(s_lg, 1)
                dve.wait_ge(s_lg, i + 1)

            nval = [0]

            def value(i):
                n = first_tile["gg"] + 2 * i + 1
                dve.wait_ge(s_tile, n + 1)
                dve.wait_ge(s_tile_a, taken[n - 1][1])
                d.tensor_tensor(glu_t[:, i % 2, :], glu_t[:, i % 2, :], ps[n % 2][:, :], ALU.mult).then_inc(s_tile_v, 1)
                dve.wait_ge(s_tile_v, i + 1)
                step(d.tensor_tensor(gate[:, i, :], gate[:, i, :], glu_t[:, i % 2, :], ALU.mult))

            for i in range(len(STEPS) + 2):
                if i < len(STEPS):
                    logits(i)
                if i % 4 == 3:
                    value(i // 4)
                if i >= 2 and STEPS[i - 2][1] == HEADS - 1:
                    t = STEPS[i - 2][0]
                    dve.wait_ge(s_pv, i - 1)
                    dve.wait_ge(s_pr, i - 1)
                    step(d.reciprocal(rinv[:, :], rsum[:, t, :]))
                    if t > 0:
                        dve.wait_ge(s_oTp, t)
                    d.tensor_tensor(oq.rearrange("p o (h e) -> p (o h) e", h=HEADS),
                                    ps[2][:, :].rearrange("p (h e) -> p h e", h=HEADS),
                                    rinv[:, :].unsqueeze(2).to_broadcast([P, HEADS, HD]), ALU.mult).then_inc(s_on, 1)
                    dve.wait_ge(s_on, t + 1)
            for i in range(8):
                n = first_tile["at"] + i
                dve.wait_ge(s_tile, n + 1)
                d.tensor_tensor(mix_t[:, 0, :], gate[:, 8 + i, :], ps[n % 2][:, :], ALU.mult).then_inc(s_tile_v, 1)
                dve.wait_ge(s_tile_v, 8 + i + 1)
                d.tensor_tensor(mixT[:, i, :], gate[:, i, :], mix_t[:, 0, :], ALU.add).then_inc(s_mix, 1)
                dve.wait_ge(s_mix, i + 1)
            dve.wait_ge(s_hrow, TT)
            dve.wait_ge(s_gb2, 32)
            for t in range(TT):
                for r in range(2):
                    n = 2 * t + r
                    dve.wait_ge(s_wo, n + 1)
                    d.scalar_tensor_tensor(h[:, t, 512 * r:512 * r + 512], h[:, t, 512 * r:512 * r + 512], ALPHA,
                                           ps[2 + n % 4][:, :], ALU.mult, ALU.add).then_inc(s_wofree, 1)
                    dve.wait_ge(s_wofree, n + 1)
                step(norm(h[:, t, :], TT + t + 1, step))
                step(d.tensor_tensor(h[:, t, :], h[:, t, :], gb[:, 0, :], ALU.mult))
                d.tensor_tensor(h[:, t, :], h[:, t, :], gb[:, 1, :], ALU.add).then_inc(s_h1, 1)
                dve.wait_ge(s_lgt, t + 1)
                d.tensor_tensor(lg[:, :], b_rt[:, :], ps[0][:, 0:NE], ALU.add).then_inc(s_lgfree, 1)
                dve.wait_ge(s_lgfree, t + 1)
                step(d.max(rt8[:, t, :], lg[:, :]))
                step(d.max_index(ri8[:, t, :], rt8[:, t, :], lg[:, :]))
                d.tensor_scalar(gneg[:, :], rt8[:, t, 0:1], -1.0, None, ALU.mult).then_inc(s_v8, 1)
                step(d.tensor_copy(rif[:, t, :], ri8[:, t, :]))
                step(d.tensor_scalar(chosen[:, t, :], tcol[:, 0:NE], rif[:, t, 0:1], None, ALU.is_equal))
                for k in range(1, TOPK):
                    step(d.scalar_tensor_tensor(chosen[:, t, :], tcol[:, 0:NE], rif[:, t, k:k + 1], chosen[:, t, :],
                                                ALU.is_equal, ALU.add))
                d.tensor_copy(chosen_b[:, t, :], chosen[:, t, :]).then_inc(s_chosen, 1)
                dve.wait_ge(s_ge, t + 1)
                step(d.reciprocal(gsum[:, 1:2], gsum[:, 0:1]))
                step(d.tensor_scalar(gates[:, t, :], gates[:, t, :], gsum[:, 1:2], None, ALU.mult))
            dve.wait_ge(s_cnt, 1)
            cnt, more, upto_e, t0 = rw[:, 0, :], rw[:, 1, :], rw[:, 2, :], rw[:, 3, :]
            step(d.tensor_copy(cnt, ps[1][:, P:P + NE]))
            step(d.tensor_scalar(more, cnt, float(P), None, ALU.is_gt))
            for b in (2, 3):
                step(d.scalar_tensor_tensor(more, cnt, float(P * b), more, ALU.is_gt, ALU.add))
            step(d.memset(t0, 1.0))
            step(d.tensor_tensor_scan(upto_e, t0, more, 0.0, ALU.mult, ALU.add))
            step(d.tensor_tensor(t0, upto_e, more, ALU.subtract))
            step(d.tensor_scalar(t0, t0, float(NE - 1), None, ALU.add))
            step(d.tensor_tensor(t0, t0, tcol[:, 0:NE], ALU.subtract))
            for t in range(TT):
                pos, f, ad = posw[:, t, 0, :], posw[:, t, 1, :], posw[:, t, 2, :]
                step(d.tensor_copy(pos, ps[1][:, NE * t:NE * t + NE]))
                step(d.tensor_scalar(f, pos, float(P), None, ALU.is_ge))
                for b in (2, 3):
                    step(d.scalar_tensor_tensor(f, pos, float(P * b), f, ALU.is_ge, ALU.add))
                step(d.tensor_tensor(ad, t0, f, ALU.add))
                step(d.scalar_tensor_tensor(ad, f, 0.5, ad, ALU.is_gt, ALU.mult))
                step(d.tensor_tensor(ad, ad, tcol[:, 0:NE], ALU.add))
                step(d.scalar_tensor_tensor(pos, f, -float(P), pos, ALU.mult, ALU.add))
                step(d.scalar_tensor_tensor(ad, pos, float(NB), ad, ALU.mult, ALU.add))
                for k in range(TOPK):
                    step(d.scalar_tensor_tensor(pos, tcol[:, 0:NE], rif[:, t, k:k + 1], ad, ALU.is_equal, ALU.mult,
                                                accum_out=addr[:, t, k:k + 1]))
                d.tensor_copy(addr_i[:, TOPK * t:TOPK * t + TOPK], addr[:, t, :]).then_inc(s_adr, 1)
            step(d.tensor_copy(etab[0:1, 0:NE], tcol[0:1, 0:NE]))
            step(d.tensor_tensor(xcmp[:, :, :], upto_e[0:1, :].unsqueeze(1).to_broadcast([1, NB - NE, NE]),
                                 tcol[0:1, 0:NB - NE].unsqueeze(2).to_broadcast([1, NB - NE, NE]), ALU.is_le))
            step(d.reduce_sum(etab[0:1, NE:NB], xcmp[:, :, :], AXL.X))
            step(d.tensor_scalar(etab[0:1, NE:NB], etab[0:1, NE:NB], float(NE - 1), None, ALU.min))
            step(d.tensor_scalar(etab[0:1, NB:NB + 1], upto_e[0:1, NE - 1:NE], float(NE), None, ALU.add))
            d.tensor_copy(etab_i[:, :], etab[:, :]).then_inc(s_tab, 1)
            dve.wait_ge(s_tab, 1)
            dve.wait_ge(s_bias, 96)
            for r in range(3):
                rows, later = slice(NE * r, NE * r + NE), range(r, 3)
                for q in range(r, 3):
                    rows = slice(NE * q, NE * q + NE)
                    step(d.tensor_copy(bias3[rows, :], braw_b[rows, :]))
                    if q > r:
                        step(d.tensor_copy(brem[rows, :], bias3[rows, :]))
                        step(d.tensor_tensor(braw_b[rows, :], braw_b[rows, :], brem[rows, :], ALU.subtract))
            dve.wait_ge(s_slots, 16)
            step(d.tensor_scalar(toks[:, :], slots[:, :], 2, None, ALU.arith_shift_right))
            nblk = dve.value_load(etab_i[0:1, NB:NB + 1], min_val=NE, max_val=NB - 1)
            dve.wait_ge(s_h1row, 16 * TT)
            d.tensor_copy(tok_now[:, :], toks[:, 0:1]).then_inc(s_tnow, 1)
            before_loop = step.n
            PER = 4
            with dve.Fori(0, nblk) as i:
                step.base, step.n = before_loop + i * PER, 0
                e = dve.value_load(etab_i[0:1, bass.ds(i, 1)], min_val=0, max_val=NE - 1)
                dve.wait_ge(s_cu, i * 6 + 1)
                d.tensor_copy(pick[:, :], eye96[:, bass.ds(e, 1)].to_broadcast([96, P])).then_inc(s_b3, 1)
                dve.wait_ge(s_gat, i * 16 + 16)
                nxt = i + 1
                d.tensor_copy(tok_now[:, :], toks[:, bass.ds(nxt, 1)]).then_inc(s_tnow, 1)
                for half in range(2):
                    n = i * 2 + half
                    G, L = ps[2 * half], ps[2 * half + 1]
                    dve.wait_ge(s_cu, i * 6 + 2 * half + 3)
                    d.tensor_scalar(swg, G[:, :], LIMIT, None, ALU.min).then_inc(s_g7, 1)
                    step(d.tensor_scalar(swl, L[:, :], LIMIT, -LIMIT, ALU.min, ALU.max))
                    dve.wait_ge(s_sig, n + 1)
                    step(d.tensor_tensor(swg, swg, sig, ALU.mult))
                    d.scalar_tensor_tensor(act_s[:, half, :], swl, 1.0, swg, ALU.add, ALU.mult).then_inc(s_act, 1)
                    dve.wait_ge(s_act, n + 1)
                dve.wait_ge(s_yout, i * 16 + 16)
                d.tensor_copy(row_now[:, :], slots[:, bass.ds(i, 1)]).then_inc(s_rnow, 1)
                assert step.n == PER
            dve.wait_ge(s_d, before_loop + nblk * PER)
            step = Steps(dve, s_dend)
            dve.wait_ge(s_gb3, 32)
            for t in range(TT):
                dve.wait_ge(s_yld[t], 16)
                step(d.tensor_scalar(h[:, t, :], h[:, t, :], ALPHA, None, ALU.mult))
                for k in range(TOPK):
                    step(d.scalar_tensor_tensor(h[:, t, :], ring[:, t, DM * k:DM * k + DM], gates[:, t, k:k + 1],
                                                h[:, t, :], ALU.mult, ALU.add))
                step(norm(h[:, t, :], 2 * TT + t + 1, step))
                step(d.tensor_tensor(h[:, t, :], h[:, t, :], gb[:, 0, :], ALU.mult))
                d.tensor_tensor(h[:, t, :], h[:, t, :], gb[:, 1, :], ALU.add).then_inc(s_oln, 1)

        @block.tensor
        def _(pe):
            mm, tr = nc.tensor.matmul, nc.tensor.transpose
            pe.wait_ge(s_const, 1)
            pe.wait_ge(s_par[2], 64)
            for r in range(2):
                for q in range(4):
                    tr(ps[2 + r][:, P * q:P * q + P], craw[:, r, q, :], ident[:, :]).then_inc(s_cT, 1)
            for k in range(KD):
                if k >= 4:
                    pe.wait_ge(s_hT, k - 3)
                for t in range(TT):
                    if k == 0:
                        pe.wait_ge(s_xhat, t + 1)
                    ins = tr(ps[4 + k % 4][:, P * t:P * t + P], h[:, t, P * k:P * k + P], ident[:, :])
                ins.then_inc(s_lnT, 1)
            pe.wait_ge(s_hT, KD)
            pe.wait_ge(s_bb, 1)
            for q in range(8):
                r, qq = q // 4, q % 4
                if q >= 4:
                    pe.wait_ge(s_bT, q - 3)
                tr(ps[4 + q % 4][:, 0:P], bblk[:, r, 4 * qq:4 * qq + 4, :].rearrange("p j c -> p (j c)"), ident[:, :])\
                    .then_inc(s_bbT, 1)

            done = [0]

            def arrive(n):
                count = 0
                for c in range(n % 2, n + 1, 2):
                    count += 32 if FRONT[c][0] == "glu" else 16
                pe.wait_ge(s_w[n % 2], count)

            def tile(n, chunk_n, last=False):
                kind, i, _ = tiles[n]
                if n >= 2:
                    pe.wait_ge(*taken[n - 2])
                o = ps[n % 2]
                w = ring[:, chunk_n % 2, :]
                if kind == "ki":
                    for k in range(KD):
                        ins = mm(o[:, :], small[:, k, 0:P], hT[:, k, :], start=k == 0, stop=k == KD - 1)
                elif kind == "v":
                    w = w.rearrange("p (k n) -> p k n", k=KD)
                    for k in range(KD):
                        ins = mm(o[:, :], hT[:, k, P * i:P * i + P], w[:, k, :], start=k == 0, stop=k == KD - 1)
                elif kind in ("gg", "val"):
                    w = w.rearrange("p (k r n) -> p k r n", k=4, r=2)
                    c = P * (i % 4)
                    for k in range(4):
                        ins = mm(o[:, :], w[:, k, 1 if kind == "gg" else 0, c:c + P], uT[:, k, :], start=k == 0,
                                 stop=k == 3)
                elif kind == "at":
                    w = w.rearrange("p (k n) -> p k n", k=4)
                    for k in range(4):
                        ins = mm(o[:, :], w[:, k, P * i:P * i + P], qiT[:, k, :], start=k == 0, stop=k == 3)
                else:
                    w = w.rearrange("p (k n) -> p k n", k=KD)
                    c = P * (i % 4)
                    for k in range(KD):
                        ins = mm(o[:, :], w[:, k, c:c + P], hT[:, k, :], start=k == 0, stop=k == KD - 1)
                ins.then_inc(s_tile, 1)

            arrive(0)
            n = 0
            for i in range(4):
                tile(n, 0)
                n += 1
            pe.wait_ge(*taken[n - 1])
            pe.wait_ge(s_bT, 8)
            pe.wait_ge(s_cblk, 1)

            def bu(j):
                rows = slice(32 * (j % 4), 32 * (j % 4) + 32)
                if j >= 1:
                    pe.wait_ge(s_bufree, j)
                for r in range(2):
                    ins = mm(ps[2 + r][:, :], bT[rows, r, j // 4, :], uT[rows, j // 4, :], start=True, stop=True)
                ins.then_inc(s_bu, 1)

            def ymm(j):
                q, rows = j // 4, slice(32 * (j % 4), 32 * (j % 4) + 32)
                pe.wait_ge(s_st, j + 1)
                if j % 4 == 0 and q > 0:
                    pe.wait_ge(s_yfree, q)
                for r in range(2):
                    ins = mm(ps[4][rows, :], cblk[:, r, j, :], w_st[:, j % 2, r, :], start=r == 0, stop=r == 1)
                ins.then_inc(s_stfree, 1)

            order = [(1, 4), ("small", 1), (2, 4), (3, 4), (4, 4)]
            flat = [(c, i == cnt - 1) for c, cnt in order for i in range(cnt)]
            for j, (c, last) in enumerate(flat):
                if j < SJ:
                    bu(j)
                if c == "small":
                    pe.wait_ge(s_small, 32)
                elif c != (flat[j - 1][0] if j else None):
                    arrive(c)
                tile(n, c if c != "small" else 0)
                n += 1
                if 1 <= j <= SJ:
                    ymm(j - 1)
            for t in range(TT):
                for k in range(KD):
                    ins = mm(ps[7][:, HEADS * t:HEADS * t + HEADS], hT[:, k, P * t:P * t + P], small[:, k, P:P + HEADS],
                             start=k == 0, stop=k == KD - 1)
            ins.then_inc(s_wi, 1)
            pe.wait_ge(*taken[n - 1])
            for i in range(24):
                t, hh = 1 + i // HEADS, i % HEADS
                rows = slice(64 * (hh % 2), 64 * (hh % 2) + 64)
                if i >= 2:
                    pe.wait_ge(s_relu, i - 1)
                mm(ps[5 + i % 2][:, 0:NQT[t]], qiT[rows, hh // 2, P * t:P * t + P], kiT[rows, 0:NQT[t]], start=True,
                   stop=True).then_inc(s_dot, 1)
            for c in range(5, 9):
                arrive(c)
                for i in range(4):
                    tile(n, c)
                    n += 1

            def qk(i):
                t, hh = STEPS[i]
                rows = slice(64 * (hh % 2), 64 * (hh % 2) + 64)
                if i == 0:
                    pe.wait_ge(s_relu, 24)
                if i >= 2:
                    pe.wait_ge(s_lg, i - 1)
                mm(ps[5 + i % 2][:, 0:NQT[t]], qT[rows, hh // 2, P * t:P * t + P], kT[rows, hh // 2, 0:NQT[t]],
                   start=True, stop=True).then_inc(s_qk, 1)

            def probsT(i):
                t, hh = STEPS[i]
                pe.wait_ge(s_pr, i + 1)
                if i >= 1:
                    pe.wait_ge(s_pT, i)
                for c in range(t + 1):
                    ins = tr(ps[7][:, P * c:P * c + P], prob[:, i % 2, P * c:P * c + P], ident[:, :])
                ins.then_inc(s_pTp, 1)
                return ins

            def pv(i):
                t, hh = STEPS[i]
                pe.wait_ge(s_pT, i + 1)
                if hh == 0 and t > 0:
                    pe.wait_ge(s_on, t)
                for c in range(t + 1):
                    ins = mm(ps[2][:, HD * hh:HD * hh + HD], pT[:, i % 2, P * c:P * c + P],
                             v[:, c, HD * hh:HD * hh + HD], start=c == 0, stop=c == t)
                ins.then_inc(s_pv, 1)

            def o_T(t):
                pe.wait_ge(s_on, t + 1)
                if t > 0:
                    pe.wait_ge(s_oT, t)
                for k in range(4):
                    ins = tr(ps[3][:, P * k:P * k + P], scr[:, 12, P * k:P * k + P], ident[:, :])
                ins.then_inc(s_oTp, 1)

            pe.wait_ge(s_gelu, 4)
            pe.wait_ge(s_far, TT - 1)
            pe.wait_ge(s_st, SJ)
            for i in range(len(STEPS) + 3):
                if i < len(STEPS):
                    qk(i)
                if i % 2 == 0 and n < first_tile["at"]:
                    c = 9 + (n - first_tile["gg"]) // 8
                    if (n - first_tile["gg"]) % 8 == 0:
                        arrive(c)
                    tile(n, c)
                    n += 1
                if 1 <= i <= len(STEPS):
                    probsT_wait = probsT(i - 1)
                if 2 <= i <= len(STEPS) + 1:
                    pv(i - 2)
                if i >= 3 and STEPS[i - 3][1] == HEADS - 1:
                    o_T(STEPS[i - 3][0])
            pe.wait_ge(s_oT, TT)
            arrive(11)
            for i in range(8):
                tile(n, 11)
                n += 1
            arrive(12)
            arrive(13)

            def w_out(t):
                for r in range(2):
                    i = 2 * t + r
                    if i >= 4:
                        pe.wait_ge(s_wofree, i - 3)
                    w = ring[:, r, :].rearrange("p (k n) -> p k n", k=KD)
                    for k in range(KD):
                        if i == 0:
                            pe.wait_ge(s_mix, k + 1)
                        ins = mm(ps[2 + i % 4][:, :], mixT[:, k, P * t:P * t + P], w[:, k, :], start=k == 0,
                                 stop=k == KD - 1)
                    ins.then_inc(s_wo, 1)

            def route(t):
                pe.wait_ge(s_h1, t + 1)
                for r in range(2):
                    if t > 0:
                        pe.wait_ge(s_h1e, 2 * t)
                    for k in range(4):
                        ins = tr(ps[6 + r][:, P * k:P * k + P], h[:, t, 512 * r + P * k:512 * r + P * k + P],
                                 ident[:, :])
                    ins.then_inc(s_h1T, 1)
                pe.wait_ge(s_h1e, 2 * t + 2)
                if t > 0:
                    pe.wait_ge(s_lgfree, t)
                for k in range(KD):
                    ins = mm(ps[0][:, 0:NE], hT1[:, k, :], w_rt[:, k, :], start=k == 0, stop=k == KD - 1)
                ins.then_inc(s_lgt, 1)

            pe.wait_ge(s_par[3], 64)
            for t in range(TT):
                w_out(t)
                if t > 0:
                    route(t - 1)
            route(TT - 1)
            for t in range(TT):
                pe.wait_ge(s_chosen, t + 1)
                for b in range(t + 1):
                    mm(ps[1][:, NE * t:NE * t + NE], before[:, :] if b == t else ones_b[:, :], chosen_b[:, b, :],
                       start=b == 0, stop=b == t)
            for b in range(TT):
                ins = mm(ps[1][:, P:P + NE], ones_b[:, :], chosen_b[:, b, :], start=b == 0, stop=b == TT - 1)
            ins.then_inc(s_cnt, 1)

            pe.wait_ge(s_tab, 1)
            nblk = pe.value_load(etab_i[0:1, NB:NB + 1], min_val=NE, max_val=NB - 1)

            def rowsT(i, half):
                for k in range(4):
                    c = P * (4 * half + k)
                    ins = tr(ps[6 + half][:, P * k:P * k + P], xg[:, c:c + P], ident[:, :])
                ins.then_inc(s_tr, 1)

            pe.sem_inc(s_cu, 1)
            pe.wait_ge(s_gat, 16)
            rowsT(0, 0)
            rowsT(0, 1)
            base = [16 * sum((32 if FRONT[c][0] == "glu" else 16) for c in range(s, NFRONT, 2)) // 16 for s in (0, 1)]
            base += [0, 0, 0, 0]
            with pe.Fori(0, nblk) as i:
                pe.wait_ge(s_ev, i * 4 + 2)
                pe.wait_ge(s_b3, i + 1)
                for c in range(4):
                    half, lin = c // 2, c % 2
                    pe.wait_ge(s_w[c], i * 16 + base[c] + 16)
                    o = ps[c]
                    col = DFF * lin + 512 * half
                    mm(o[:, :], pick[:, :], bias3[:, col:col + 512], start=True, stop=False)
                    w = ring[:, c, :].rearrange("p (k n) -> p k n", k=KD)
                    for k in range(KD):
                        ins = mm(o[:, :], xT[:, k, :], w[:, k, :], start=False, stop=k == KD - 1)
                    ins.then_inc(s_cu, 1)
                    if c == 2:
                        actT_half(pe, tr, s_act, s_tr, ps, act_s, ident, i, 0, s_ev)
                for half in range(2):
                    c = 4 + half
                    if half == 1:
                        actT_half(pe, tr, s_act, s_tr, ps, act_s, ident, i, 1, s_ev)
                        pe.wait_ge(s_gat, i * 16 + 32)
                        pe.wait_ge(s_ev, i * 4 + 3)
                        rowsT(i, 0)
                        pe.wait_ge(s_ev, i * 4 + 4)
                        rowsT(i, 1)
                    pe.wait_ge(s_w[c], i * 16 + 16)
                    pe.wait_ge(s_ev, i * 4 + 3 + half)
                    if half == 0:
                        pe.wait_ge(s_ysb, i * 2 + 1)
                    w = ring[:, c, :].rearrange("p (k n) -> p k n", k=4)
                    for r in range(2):
                        if half == 0:
                            mm(ps[4 + r][:, :], pick[:, :], bias3[:, 2 * DFF + 512 * r:2 * DFF + 512 * r + 512],
                               start=True, stop=False)
                        for k in range(4):
                            ins = mm(ps[4 + r][:, :], actT[:, 4 * half + k, :], w[:, k, 512 * r:512 * r + 512],
                                     start=False, stop=half == 1 and k == 3)
                    ins.then_inc(s_cu, 1)


def wi_ps(ps):
    return ps[7][:, 0:TT * HEADS].rearrange("p (t h) -> p t h", h=HEADS)


def actT_half(pe, tr, s_act, s_tr, ps, act_s, ident, i, half, s_ev):
    pe.wait_ge(s_act, i * 2 + half + 1)
    for k in range(4):
        ins = tr(ps[6 + half][:, P * k:P * k + P], act_s[:, half, P * k:P * k + P], ident[:, :])
    ins.then_inc(s_tr, 1)


NAMES = ["x", "ln_in_g", "ln_in_b", "w_in", "b_gate", "lam_re", "lam_im", "log_dt", "b_re", "b_im", "c_re", "c_im",
         "d_skip", "w_glu", "w_attn_proj", "w_o", "ln1_g", "ln1_b", "w_router", "b_router", "w_up", "b_up",
         "w_down", "b_down", "ln2_g", "ln2_b"]


def kernel(**inputs):
    import numpy as _np
    import concourse.bacc as _bacc
    from concourse.bass_utils import run_bass_kernel_spmd as _run

    nc = _bacc.Bacc("TRN2", target_bir_lowering=False, num_devices=1)
    arrays, args = {}, {}
    for name in NAMES:
        x = _np.ascontiguousarray(inputs[name])
        arrays[f"in_{name}"] = x
        args[name] = nc.dram_tensor(f"in_{name}", x.shape, mybir.dt.from_np(x.dtype), kind="ExternalInput").ap()
    out = nc.dram_tensor("out_0", (1, SEQ, DM), F32, kind="ExternalOutput").ap()
    build(nc, args, out)
    r = _run(nc, [arrays], core_ids=[0])
    return r.results[0]["out_0"]
```

```python
from contextlib import ExitStack

import concourse.bass as bass
import numpy as np
from concourse import mybir

ACT = mybir.ActivationFunctionType
ALU = mybir.AluOpType
AXL = mybir.AxisListType
F32 = mybir.dt.float32
F32R = mybir.dt.float32r
BF16 = mybir.dt.bfloat16
I32 = mybir.dt.int32
U32 = mybir.dt.uint32

P = 128
SEQ = 512
DM = 1024
TT = SEQ // P
KD = DM // P
SSM = 512
GROUP = 16
STATES = 64
SJ = SSM // GROUP * STATES // P
HEADS = 8
HD = 64
NSEL = min(256, SEQ // 4)
NE = 32
TOPK = 4
DFF = 1024
BLK = 128
NB = NE + SEQ * TOPK // BLK + 1
BTAIL = NB - NE
PARTS = 12
PART = 2048
NRAW, NSPLIT = 6, 4
BY_POOL = [7, 8, 11, 12]
MORE = range(1, -(-SEQ // BLK))
NOROW = SEQ * TOPK
ALPHA = 2.0 ** 0.25
EPS = 1e-5
LIMIT = 7.0
SWI = 1.702
TWO_PI = 6.283185307179586
PI_C1 = 6.28125
PI_C2 = 2029.0 / 1048576.0
PI_C3 = TWO_PI - PI_C1 - PI_C2
PI_SAFE = 3.1415925
ROUND = 12582912.0
ROUND14 = 768.0
MASKED = -3.0e38
TAKEN = -3.3e38
FAR = 1.0e30
SLOPES = [2.0 ** (-8.0 * (h + 1) / HEADS) for h in range(HEADS)]
CHUNK = 4096
C_U, C_Q, C_K, C_V, C_QI, C_KI, C_WI, C_G = 0, 512, 1024, 1536, 2048, 2560, 2624, 2632
NSMALL = 136


class Steps:

    def __init__(self, engine, sem):
        self.engine, self.sem, self.n, self.base = engine, sem, 0, None

    def __call__(self, instruction):
        instruction.then_inc(self.sem, 1)
        self.n += 1
        self.engine.wait_ge(self.sem, self.n if self.base is None else self.base + self.n)


def build(nc, a, out):
    h1_rows = nc.dram_tensor("h1_rows", [SEQ, DM], F32, kind="Internal").ap()
    y_rows = nc.dram_tensor("y_rows", [SEQ * TOPK, DM], F32, kind="Internal").ap()
    slot_list = nc.dram_tensor("slot_list", [BLK * NB, 1], I32, kind="Internal").ap()

    x_v = a["x"][0].rearrange("(t p) d -> p t d", p=P)
    w_in = a["w_in"][0].rearrange("(k p) n -> p k n", p=P)
    w_glu = a["w_glu"][0].rearrange("(k p) n -> p k n", p=P)
    w_att = a["w_attn_proj"][0].rearrange("(k p) n -> p k n", p=P)
    w_o = a["w_o"][0].rearrange("(k p) n -> p k n", p=P)
    out_v = out[0].rearrange("(t p) d -> p t d", p=P)

    with ExitStack() as ctx:
        def sb(name, shape, dt=F32):
            return ctx.enter_context(nc.sbuf_tensor(name, shape, dt))

        def sem(name):
            return ctx.enter_context(nc.semaphore(name))

        at_ring = -(-nc.sbuf_base // 32) * 32
        ring = sb("ring", [P, 6, CHUNK])
        hT = ring[:, 2, :].rearrange("p (k t) -> p k t", k=KD)
        qT = ring[:, 3, 0:2048].rearrange("p (k t) -> p k t", k=4)
        kT = ring[:, 3, 2048:4096].rearrange("p (k t) -> p k t", k=4)
        gate = ring[:, 4:6, :].rearrange("p s (k t) -> p (s k) t", k=KD)
        mixT = gate

        craw = ring[:, 4, 0:1024].rearrange("p (r q n) -> p r q n", r=2, q=4)
        bT = ring[:, 4, 1024:2048].rearrange("p (r q n) -> p r q n", r=2, q=4)
        small = ring[:, 4, 2048:2048 + KD * NSMALL].rearrange("p (k n) -> p k n", k=KD)
        cblk = ring[:, 5, 0:1024].rearrange("p (r j c) -> p r j c", r=2, j=SJ)

        h = sb("h", [P, TT, DM])
        at_u = -(-nc.sbuf_base // 32) * 32
        uT = sb("uT", [P, 4, SEQ])
        at_v = -(-nc.sbuf_base // 32) * 32
        v = sb("v", [P, TT, SSM])
        qiT = sb("qiT", [P, 4, SEQ])
        kiT = sb("kiT", [P, SEQ])
        wi = sb("wi", [P, TT, HEADS])
        far = sb("far", [P, TT, SEQ])
        ident = sb("ident", [P, P])
        tcol = sb("tcol", [P, SEQ])
        qpos = sb("qpos", [P, TT])
        gb = sb("gb", [P, 2, DM])
        gbc = sb("gbc", [P, 2, KD])
        bgate = sb("bgate", [P, 16])
        dskip = sb("dskip", [P, 4])
        eps = sb("eps", [P, 1])
        half_pi = sb("half_pi", [P, 1])
        stats = sb("stats", [P, 2, 6])
        mv = sb("mv", [P, 2])
        rstd = sb("rstd", [P, 2])
        sp_in = sb("sp_in", [P, 3, SJ])
        spw = sb("spw", [P, 24, SJ])
        tcol_i = far[:, 3, :].bitcast(I32)
        braw = far[:, 0:2, 0:SJ * GROUP].rearrange("p r (j c) -> p r j c", c=GROUP)
        bblk = far[:, 2:4, :].rearrange("p r (j c) -> p r j c", c=2 * GROUP)
        at_scr = -(-nc.sbuf_base // 32) * 32
        scr = sb("scr", [P, 16, SEQ])
        phase, turn, trig = scr[:, 0:2], scr[:, 2:4], scr[:, 4:8].rearrange("p (b r) t -> p b r t", b=2)
        m = scr[:, 8:12]
        w_st = scr[:, 12:16].rearrange("p (b r) t -> p b r t", b=2)
        score, relu = scr[:, 0:2], scr[:, 2:4]
        logit, prob, pT, glu_t = scr[:, 4:6], scr[:, 6:8], scr[:, 8:10], scr[:, 10:12]
        oq, mix_t = scr[:, 12:13], scr[:, 13:16]
        top8 = sb("top8", [P, 8])
        amax = sb("amax", [P, 2])
        rsum = sb("rsum", [P, TT, HEADS])
        rinv = sb("rinv", [P, HEADS])

        w_rt = sb("w_rt", [P, KD, NE])
        b_rt = sb("b_rt", [P, NE])
        lg = sb("lg", [P, NE])
        rt8 = sb("rt8", [P, TT, 8])
        ri8 = sb("ri8", [P, TT, 8], U32)
        rif = sb("rif", [P, TT, 8])
        gates = sb("gates", [P, TT, TOPK])
        gsum = sb("gsum", [P, 2])
        gneg = sb("gneg", [P, 1])
        chosen = sb("chosen", [P, TT, NE])
        chosen_b = sb("chosen_b", [P, TT, NE], BF16)
        before = sb("before", [P, P], BF16)
        ones_b = sb("ones_b", [P, P], BF16)
        rw = sb("rw", [P, 6, NE])
        posw = sb("posw", [P, TT, 3, NE])
        addr = sb("addr", [P, TT, TOPK])
        addr_i = sb("addr_i", [P, TT * TOPK], I32)
        code = sb("code", [P, TT * TOPK], I32)
        empty = sb("empty", [BLK, NB], I32)
        slots = sb("slots", [BLK, NB], I32)
        toks = sb("toks", [BLK, NB], I32)
        tok_now = sb("tok_now", [BLK, 1], I32)
        row_now = sb("row_now", [BLK, 1], I32)
        etab_i = sb("etab_i", [1, NB + 1], I32)
        etab = sb("etab", [1, NB + 1])
        bias3 = sb("bias3", [96, 3 * DFF], BF16)
        pick = sb("pick", [96, BLK], BF16)
        eye96 = sb("eye96", [96, NE])
        E = scr[:, :, :].rearrange("p a b -> p (a b)")
        xg = E[0:BLK, 6 * DFF:6 * DFF + DM]
        xcmp = far[0:1, 0:2, :].rearrange("o a b -> o (a b)")[:, 0:BTAIL * NE].rearrange("o (b e) -> o b e", e=NE)
        braw_b = E[0:96, 0:3 * DFF]
        brem = E[0:96, 3 * DFF:6 * DFF]
        hT1 = uT[:, 0:2, :].rearrange("p a t -> p (a t)").rearrange("p (k t) -> p k t", k=KD)
        def over(name, shape, dt, tensor_at, offset=0):
            return nc.alloc_sbuf_tensor_at(name, shape, dt, offset=tensor_at + offset)

        raw = over("raw", [P, NRAW, PART], F32, at_ring)
        split_at = [(at_ring, 4 * PART * (NRAW + 2 * r)) for r in range(NSPLIT - 1)] + [(at_scr, 0)]
        w_hi = [over(f"w_hi{r}", [P, PART], F32R, *where) for r, where in enumerate(split_at)]
        w_lo = [over(f"w_lo{r}", [P, PART], F32R, where[0], where[1] + 4 * PART) for r, where in enumerate(split_at)]
        x_hi, x_lo = (over(f"x_{q}", [P, KD, BLK], F32R, at_u, 4096 * r) for r, q in enumerate(("hi", "lo")))
        a_hi, a_lo = (over(f"a_{q}", [P, KD, BLK], F32R, at_v, 4096 * r) for r, q in enumerate(("hi", "lo")))
        act_s = far[:, 0:2, :]
        swg, sig, swl = (qiT[:, r, :] for r in range(3))
        ysb = far[0:BLK, 2:4, :]

        ps = [ctx.enter_context(nc.psum_tensor(f"ps{i}", [P, 512], F32)) for i in range(8)]

        s_x = [sem(f"x{t}_loaded") for t in range(TT)]
        s_dend = sem("last_vector_steps")
        s_par = [sem(f"params{i}_loaded") for i in range(4)]
        s_small = sem("small_loaded")
        s_lnp = sem("ln_in_params_loaded")
        s_gb1, s_gb2, s_gb3 = sem("ln_in_rows_loaded"), sem("ln1_rows_loaded"), sem("ln2_rows_loaded")
        s_w = [sem(f"weights_loaded{i}") for i in range(2)]
        s_w1o = sem("w_o_right_loaded")
        s_wi = sem("w_idx_done")
        s_const = sem("pool_constants")
        s_one = sem("vector_constants")
        s_d, s_a, s_g = sem("vector_steps"), sem("scalar_steps"), sem("pool_steps")
        s_xhat, s_rstd, s_var = sem("xhat_ready"), sem("std_ready"), sem("var_ready")
        s_lnT, s_hT = sem("xhat_transposed"), sem("hT_ready")
        s_hrow = sem("h_rows_ready")
        s_tile, s_tile_a, s_tile_v = sem("tile_done"), sem("tile_taken_by_scalar"), sem("tile_taken_by_vector")
        s_dt, s_sc = sem("dt_ready"), sem("sincos_ready")
        s_th, s_prod = sem("theta_ready"), sem("phase_products_ready")
        s_bb, s_bbT, s_bT = sem("b_blocks_ready"), sem("b_transposed"), sem("bT_ready")
        s_cT, s_cblk, s_tau = sem("c_transposed"), sem("c_blocks_ready"), sem("turns_ready")
        s_ph, s_trig, s_phfree, s_rot = sem("phase_ready"), sem("trig_ready"), sem("phase_used"), sem("trig_used")
        s_bu, s_bufree = sem("bu_done"), sem("bu_taken")
        s_st, s_stfree = sem("states_ready"), sem("states_used")
        s_y, s_yfree, s_gelu = sem("y_done"), sem("y_taken"), sem("gelu_done")
        s_dot, s_relu, s_relufree = sem("dots_done"), sem("relu_ready"), sem("relu_used")
        s_scored, s_masked, s_far0 = sem("scores_summed"), sem("scores_masked"), sem("first_tile_distances")
        s_far = sem("distances_ready")
        s_qk, s_lg, s_pr = sem("qk_done"), sem("logits_ready"), sem("probs_ready")
        s_pTp, s_pT, s_pv = sem("probs_transposed"), sem("pT_ready"), sem("pv_done")
        s_on, s_oTp, s_oT = sem("o_normed"), sem("o_transposed"), sem("oT_ready")
        s_gg, s_mix = sem("glu_gate_ready"), sem("mix_ready")
        s_wo, s_wofree = sem("wo_done"), sem("wo_taken")
        s_h1, s_h1T, s_h1e, s_lgt, s_lgfree = (sem("h1_ready"), sem("h1_transposed"), sem("h1T_ready"),
                                               sem("router_done"), sem("router_taken"))
        s_v8, s_ge = sem("top_ready"), sem("gate_exp_ready")
        s_h1row = sem("h1_rows_written")
        s_chosen, s_cnt, s_adr = sem("chosen_ready"), sem("counts_done"), sem("addresses_ready")
        s_scat, s_slots = sem("list_written"), sem("slots_loaded")
        s_tok, s_tab = sem("token_ids_ready"), sem("table_ready")
        s_bias, s_b3l, s_b3 = sem("biases_loaded"), sem("bias_parts_ready"), sem("pick_ready")
        s_gat, s_tnow, s_rnow = sem("rows_gathered"), sem("tokens_picked"), sem("rows_picked")
        s_tr, s_thi, s_tlo = sem("moe_transposed"), sem("transposed_upper"), sem("transposed_lower")
        s_raw = [sem(f"part_loaded{i}") for i in range(NRAW)]
        s_hi, s_lo, s_lo_g = sem("upper_parts_ready"), sem("part_split"), sem("part_split_by_pool")
        s_up, s_sig, s_act, s_upfree = sem("up_done"), sem("sigmoid_ready"), sem("act_ready"), sem("up_taken")
        s_g7 = sem("gate_clipped")
        s_cu = sem("chunk_used")
        s_ysb, s_yout = sem("y_ready"), sem("pool_stores_done")
        s_yld = [sem(f"y_loaded{t}") for t in range(TT)]
        s_ah1, s_nb, s_nrm = sem("alpha_h1_ready"), sem("last_shift_ready"), sem("last_rows_normed")
        s_oln_v, s_gend = sem("last_tile_out_ready"), sem("last_pool_steps")
        s_oln, s_out = sem("out_ready"), sem("out_written")

        FRONT = [("u", C_U), ("qi", C_QI), ("q", C_Q), ("k", C_K), ("v", C_V)]
        FRONT += [("g", C_G + 512 * i) for i in range(4)]
        FRONT += [("glu", 0), ("glu", 1), ("att", 0), ("wo", 0), ("wo", 1)]
        NFRONT = len(FRONT)

        tiles = []
        for kind, n in (("u", 4), ("qi", 4), ("ki", 1), ("q", 4), ("k", 4), ("v", 4), ("g", 16)):
            tiles += [(kind, i, "a") for i in range(n)]
        for i in range(8):
            tiles += [("gg", i, "a"), ("val", i, "v")]
        for i in range(8):
            tiles += [("at", i, "v")]
        taken, na, nv = [], 0, 0
        for _, _, who in tiles:
            na, nv = na + (who == "a"), nv + (who == "v")
            taken.append((s_tile_a, na) if who == "a" else (s_tile_v, nv))
        first_tile = {}
        for n, (kind, _, _) in enumerate(tiles):
            first_tile.setdefault(kind, n)

        tiles_upto = [4, 8, 13, 17, 21, 25, 29, 33, 37, 45, 53, 61]

        def gates_after(i):
            return {3: 1, HEADS - 1: 3}.get(i % HEADS, 0)

        NQT = [P * (t + 1) for t in range(TT)]
        STEPS = [(t, hh) for t in range(TT) for hh in range(HEADS)]

        def part_of(c, last):
            if c > PARTS:
                return (1, c - PARTS)
            if c <= 9 or last:
                return (0, c)
            return (1, 0) if c == 10 else (0, c - 1)

        def turns(lo, hi, last):
            return range(lo, min(hi, PARTS - 1) + 1) if last else range(lo, hi + 1)

        def wait_split(engine, i, c):
            engine.wait_ge(s_lo, i * PARTS + c + 1)
            if c in BY_POOL:
                engine.wait_ge(s_lo_g, i * len(BY_POOL) + BY_POOL.index(c) + 1)

        ctx.enter_context(nc.allow_non_contiguous_dma(reason="small parameters, one number for each partition"))
        block = ctx.enter_context(nc.Block())

        @block.sync
        def _(sp):
            for t in range(TT):
                sp.dma_start(h[:, t, :], x_v[:, t, :]).then_inc(s_x[t], 16)

            def chunk(n):
                kind, c = FRONT[n]
                dst = ring[:, n % 2, :]
                if n == NFRONT - 1:
                    sp.dma_start(ring[:, 2, :].rearrange("p (k n) -> p k n", k=KD), w_o[:, :, 512:1024])\
                        .then_inc(s_w1o, 16)
                    return
                if n >= 2:
                    sp.wait_ge(s_tile, tiles_upto[n - 2])
                if kind == "glu":
                    d4 = dst.rearrange("p (k r n) -> p k r n", k=4, r=2)
                    for r in range(2):
                        sp.dma_start(d4[:, :, r, :], w_glu[:, :, DM * r + 512 * c:DM * r + 512 * c + 512])\
                            .then_inc(s_w[n % 2], 8 * 2)
                elif kind == "att":
                    sp.dma_start(dst.rearrange("p (k n) -> p k n", k=4), w_att).then_inc(s_w[n % 2], 16)
                else:
                    src = w_o[:, :, 512 * c:512 * c + 512] if kind == "wo" else w_in[:, :, c:c + 512]
                    sp.dma_start(dst.rearrange("p (k n) -> p k n", k=KD), src).then_inc(s_w[n % 2], 16)

            chunk(0)
            sp.dma_start(small[:, :, 0:64], w_in[:, :, C_KI:C_KI + 64]).then_inc(s_small, 16)
            sp.dma_start(small[:, :, 64:136], w_in[:, :, C_KI:C_KI + 72]).then_inc(s_small, 16)
            for n in range(1, NFRONT - 1):
                chunk(n)
                if n == 10:
                    chunk(NFRONT - 1)
            sp.wait_ge(s_mix, 8)
            for r in range(3):
                sp.dma_start(braw_b[NE * r:NE * r + NE, 0:2 * DFF], a["b_up"][0]).then_inc(s_bias, 16)
                sp.dma_start(braw_b[NE * r:NE * r + NE, 2 * DFF:3 * DFF], a["b_down"][0]).then_inc(s_bias, 16)

            def part(c, p, e):
                if p < 8:
                    col = DFF * (p // 2 % 2) + 512 * (p // 4)
                    rows = slice(512 * (p % 2), 512 * (p % 2) + 512)
                    src = a["w_up"][0, bass.ds(e, 1), rows, col:col + 512].rearrange("o (k p) n -> p (o k) n", p=P)
                    dst = raw[:, c % NRAW, :].rearrange("p (k n) -> p k n", k=4)
                else:
                    rows = slice(256 * (p - 8), 256 * (p - 8) + 256)
                    src = a["w_down"][0, bass.ds(e, 1), rows, :].rearrange("o (k p) n -> p (o k) n", p=P)
                    dst = raw[:, c % NRAW, :].rearrange("p (k n) -> p k n", k=2)
                sp.dma_start(dst, src).then_inc(s_raw[c % NRAW], 16)

            sp.wait_ge(s_wo, 2 * TT)
            for p in range(NRAW):
                part(p, p, 0)
            sp.wait_ge(s_scat, 16 * TT * TOPK)
            sp.dma_start(slots[:, :], slot_list.rearrange("(p b) o -> p (b o)", p=BLK)).then_inc(s_slots, 16)
            sp.wait_ge(s_tab, 1)
            final = sp.value_load(etab_i[0:1, NB:NB + 1], min_val=NE - 1, max_val=NB - 2)

            sp.wait_ge(s_lo, 1)
            sp.wait_ge(s_gat, 16)
            part(NRAW, NRAW, 0)

            def load_turns(i, lo, hi, last):
                now = sp.value_load(etab_i[0:1, bass.ds(i, 1)], min_val=0, max_val=NE - 1)
                later = None if last else sp.value_load(etab_i[0:1, bass.ds(i + 1, 1)], min_val=0, max_val=NE - 1)
                for c in turns(lo, hi, last):
                    on, p = part_of(c, last)
                    split = next(x for x in range(c - NRAW, 20) if x not in BY_POOL)
                    sp.wait_ge(s_lo, i * PARTS + split + 1)
                    part(c, p, later if on else now)

            with sp.Fori(0, final) as i:
                load_turns(i, NRAW + 1, PARTS + NRAW, False)
            load_turns(final, NRAW + 1, PARTS - 1, True)
            for t in range(TT):
                if t == 0:
                    out_rows = sp.snap(final * 16 + 32)
                    sp.wait_ge(s_yout, out_rows)
                sp.dma_start(ring[:, t, :], y_rows[P * TOPK * t:P * TOPK * (t + 1), :]
                             .rearrange("(p k) d -> p (k d)", k=TOPK)).then_inc(s_yld[t], 16)
            for t in range(TT):
                if t < TT - 1:
                    sp.wait_ge(s_oln, t + 1)
                else:
                    sp.wait_ge(s_oln_v, 1)
                sp.dma_start(out_v[:, t, :], h[:, t, :]).then_inc(s_out, 16)
            sp.wait_ge(s_out, 16 * TT)

        @block.gpsimd
        def _(pool):
            step = Steps(pool, s_g)
            g = nc.gpsimd
            step(g.memset(ident[:, :], 0.0))
            g.affine_select(out=ident[:, :], in_=ident[:, :], compare_op=ALU.not_equal, fill=1.0, base=0,
                            pattern=[[-1, P]], channel_multiplier=1).then_inc(s_const, 1)
            step(g.iota(tcol_i[:, :], pattern=[[1, SEQ]], base=0, channel_multiplier=0))
            g.tensor_copy(tcol[:, :], tcol_i[:, :]).then_inc(s_const, 1)
            pool.wait_ge(s_const, 2)
            for j in range(SJ):
                if j == 0:
                    pool.wait_ge(s_tau, 1)
                tau = spw[:, 20, j:j + 1]
                f, r = phase[:, j % 2, :], turn[:, 0, :]
                lo = turn[:, 1, :]
                step(g.tensor_scalar(r, tcol[:, :], tau, ROUND, ALU.mult, ALU.add))
                step(g.tensor_scalar(r, r, ROUND, None, ALU.subtract))
                pool.wait_ge(s_prod, 2 * j + 2)
                step(g.tensor_tensor(f, f, r, ALU.subtract))
                step(g.tensor_tensor(f, f, lo, ALU.add))
                g.tensor_scalar(f, f, 0.5 * 0.9999999, -0.5 * 0.9999999, ALU.min, ALU.max).then_inc(s_ph, 1)
            step(g.memset(ones_b[:, :], 1.0))
            step(g.memset(before[:, :], 1.0))
            step(g.affine_select(out=before[:, :], in_=before[:, :], compare_op=ALU.is_gt, fill=0.0, base=0,
                                 pattern=[[1, P]], channel_multiplier=-1))
            step(g.memset(empty[:, :], NOROW))
            g.dma_start(slot_list.rearrange("(p b) o -> p (b o)", p=BLK), empty[:, :]).then_inc(s_yout, 16)
            step(g.iota(code[:, :], pattern=[[P * TOPK, TT], [1, TOPK]], base=0, channel_multiplier=TOPK))
            step(g.memset(eye96[:, :], 0.0))
            for r in range(3):
                step(g.affine_select(out=eye96[:, :], in_=eye96[:, :], compare_op=ALU.not_equal, fill=1.0,
                                     base=-NE * r, pattern=[[-1, NE]], channel_multiplier=1))
            pool.wait_ge(s_gb1, 32)
            pool.wait_ge(s_lnT, KD)
            for t in range(TT):
                step(g.tensor_tensor(h[:, t, :], h[:, t, :], gb[:, 0, :], ALU.mult))
                g.tensor_tensor(h[:, t, :], h[:, t, :], gb[:, 1, :], ALU.add).then_inc(s_hrow, 1)
                pool.wait_ge(s_hrow, t + 1)
            pool.wait_ge(s_far0, 1)
            g.affine_select(out=far[:, 0, :], in_=far[:, 0, :], compare_op=ALU.is_ge, fill=FAR, base=0,
                            pattern=[[-1, SEQ]], channel_multiplier=1).then_inc(s_masked, 1)
            for t in range(1, TT):
                pool.wait_ge(s_relufree, HEADS * t)
                g.affine_select(out=score[:, t % 2, P * t:P * t + P], in_=score[:, t % 2, P * t:P * t + P],
                                compare_op=ALU.is_ge, fill=MASKED, base=0, pattern=[[-1, P]],
                                channel_multiplier=1).then_inc(s_masked, 1)
            pool.wait_ge(s_bias, 96)
            second, third = slice(NE, 2 * NE), slice(2 * NE, 3 * NE)
            step(g.tensor_copy(bias3[:, :], braw_b))
            step(g.tensor_copy(brem, bias3[:, :]))
            step(g.tensor_tensor(braw_b, braw_b, brem, ALU.subtract))
            step(g.tensor_copy(bias3[second, :], braw_b[second, :]))
            step(g.tensor_copy(bias3[third, :], braw_b[third, :]))
            step(g.tensor_copy(brem[third, :], bias3[third, :]))
            step(g.tensor_tensor(braw_b[third, :], braw_b[third, :], brem[third, :], ALU.subtract))
            g.tensor_copy(bias3[third, :], braw_b[third, :]).then_inc(s_b3l, 1)
            pool.wait_ge(s_b3l, 1)
            pool.wait_ge(s_yout, 16)
            for t in range(TT):
                pool.wait_ge(s_adr, t + 1)
                for k in range(TOPK):
                    c = TOPK * t + k
                    g.indirect_dma_start(slot_list, bass.IndirectOffsetOnAxis(ap=addr_i[:, c:c + 1], axis=0),
                                         code[:, c:c + 1], None, bounds_check=BLK * NB - 1,
                                         oob_is_err=False).then_inc(s_scat, 16)
            pool.wait_ge(s_tab, 1)
            final = pool.value_load(etab_i[0:1, NB:NB + 1], min_val=NE - 1, max_val=NB - 2)
            pool.wait_ge(s_h1row, 16 * TT)
            g.memset(xg[:, :], 0.0).then_inc(s_one, 1)
            pool.wait_ge(s_one, 1)

            zero, last_tok, last_row = (pool.alloc_register(x) for x in ("nothing", "last_token", "last_row"))
            pool.reg_mov(zero, 0)

            def gather(i):
                pool.wait_ge(s_tnow, i + 1)
                pool.reg_add(last_tok, zero, SEQ - 1)
                g.indirect_dma_start(xg[:, :], None, h1_rows,
                                     bass.IndirectOffsetOnAxis(ap=tok_now[:, 0:1], axis=0),
                                     bounds_check=last_tok, oob_is_err=False).then_inc(s_gat, 16)

            def rows_out(i):
                pool.wait_ge(s_rnow, i + 1)
                pool.wait_ge(s_ysb, i * 2 + 3)
                pool.reg_add(last_row, zero, SEQ * TOPK - 1)
                g.indirect_dma_start(y_rows, bass.IndirectOffsetOnAxis(ap=row_now[:, 0:1], axis=0),
                                     ysb.rearrange("p a b -> p (a b)"), None, bounds_check=last_row,
                                     oob_is_err=False).then_inc(s_yout, 16)

            def lo_share(i, c):
                pool.wait_ge(s_hi, i * PARTS + c + 1)
                g.tensor_tensor(w_lo[c % NSPLIT][:, PART // 2:], raw[:, c % NRAW, PART // 2:],
                                w_hi[c % NSPLIT][:, PART // 2:], ALU.subtract).then_inc(s_lo_g, 1)

            gather(0)
            for t in range(TT):
                g.tensor_scalar(h[:, t, :], h[:, t, :], ALPHA, None, ALU.mult).then_inc(s_ah1, 1)
                pool.wait_ge(s_ah1, t + 1)
            with pool.Fori(0, final) as i:
                pool.wait_ge(s_tr, i * 4 + 2)
                gather(i + 1)
                for c in BY_POOL:
                    lo_share(i, c)
                rows_out(i)
            for c in BY_POOL:
                if c < PARTS:
                    lo_share(final, c)
            rows_out(final)
            pool.wait_ge(s_yout, final * 16 + 32)
            pool.wait_ge(s_gat, final * 16 + 16)
            pool.wait_ge(s_gb3, 32)
            step.sem, step.n = s_gend, 0
            for t in range(TT - 1):
                pool.wait_ge(s_nrm, t + 1)
                step(g.tensor_tensor(h[:, t, :], h[:, t, :], gb[:, 0, :], ALU.mult))
                g.tensor_tensor(h[:, t, :], h[:, t, :], gb[:, 1, :], ALU.add).then_inc(s_oln, 1)

        @block.scalar
        def _(act):
            s = nc.scalar
            step = Steps(act, s_a)
            act.dma_start(sp_in[:, 0, :], a["lam_re"][0].rearrange("(j w) n -> (w n) j", w=2)).then_inc(s_par[0], 16)
            act.dma_start(sp_in[:, 1, :], a["lam_im"][0].rearrange("(j w) n -> (w n) j", w=2)).then_inc(s_par[0], 16)
            for w in range(2):
                src = a["log_dt"].rearrange("o (j w) -> w o j", w=2)[w].partition_broadcast(STATES)
                act.dma_start(sp_in[64 * w:64 * w + 64, 2, :], src.rearrange("p o j -> p (o j)")
                              if len(src.shape) == 3 else src).then_inc(s_par[0], 16)
            act.dma_start(gbc[:, 0, :], a["ln_in_g"].rearrange("(k p) -> p k", p=P)).then_inc(s_lnp, 16)
            act.dma_start(gbc[:, 1, :], a["ln_in_b"].rearrange("(k p) -> p k", p=P)).then_inc(s_lnp, 16)
            for r, nm in enumerate(("b_re", "b_im")):
                act.dma_start(braw[:, r], a[nm][0].rearrange("(j w) n c -> (w n) j c", w=2)).then_inc(s_par[1], 16)
            for t in range(TT):
                act.wait_ge(s_var, t + 1)
                s.activation(rstd[:, 0:1], mv[:, 1:2], ACT.Sqrt, bias=eps[:, 0:1]).then_inc(s_rstd, 1)
            for r, nm in enumerate(("c_re", "c_im")):
                src = a[nm][0].rearrange("(q g) c n -> (g c) q n", q=4)
                for dup in range(2):
                    act.dma_start(craw[:, r, :, 64 * dup:64 * dup + 64], src).then_inc(s_par[2], 16)
            act.dma_start(bgate[:, :], a["b_gate"][0].rearrange("(k p) -> p k", p=P)).then_inc(s_par[3], 16)
            act.dma_start(dskip[:, :], a["d_skip"][0].rearrange("(q g) c -> (g c) q", q=4)).then_inc(s_par[3], 16)
            for r, nm in enumerate(("ln_in_g", "ln_in_b")):
                act.dma_start(gb[:, r, :], a[nm].partition_broadcast(P)).then_inc(s_gb1, 16)
            act.dma_start(w_rt[:, :, :], a["w_router"][0].rearrange("(k p) n -> p k n", p=P)).then_inc(s_par[3], 16)
            act.dma_start(b_rt[:, :], a["b_router"][0].partition_broadcast(P)).then_inc(s_par[3], 16)

            act.wait_ge(s_lnp, 32)
            for k in range(KD):
                act.wait_ge(s_lnT, k + 1)
                s.activation(hT[:, k, :], ps[4 + k % 4][:, :], ACT.Identity, scale=gbc[:, 0, k:k + 1],
                             bias=gbc[:, 1, k:k + 1]).then_inc(s_hT, 1)
            act.wait_ge(s_par[0], 64)
            s.activation(spw[:, 0, :], sp_in[:, 2, :], ACT.Exp).then_inc(s_dt, 1)
            act.wait_ge(s_th, 1)
            s.activation(spw[:, 2, :], spw[:, 1, :], ACT.Exp).then_inc(s_dt, 1)
            act.wait_ge(s_th, 2)
            s.activation(spw[:, 5, :], spw[:, 4, :], ACT.Sin).then_inc(s_sc, 1)
            step(s.activation(spw[:, 6, :], spw[:, 4, :], ACT.Abs))
            s.activation(spw[:, 7, :], spw[:, 6, :], ACT.Sin, scale=-1.0, bias=half_pi[:, 0:1]).then_inc(s_sc, 1)
            def phase_products(j):
                if j >= 1:
                    act.wait_ge(s_ph, j)
                if j >= 2:
                    act.wait_ge(s_phfree, j - 1)
                s.activation(phase[:, j % 2, :], tcol[:, :], ACT.Copy, scale=spw[:, 21, j:j + 1]).then_inc(s_prod, 1)
                s.activation(turn[:, 1, :], tcol[:, :], ACT.Copy, scale=spw[:, 22, j:j + 1]).then_inc(s_prod, 1)

            def trigs(j):
                if j + 1 < SJ:
                    phase_products(j + 1)
                act.wait_ge(s_ph, j + 1)
                if j >= 2:
                    act.wait_ge(s_rot, j - 1)
                s.activation(trig[:, j % 2, 1, :], phase[:, j % 2, :], ACT.Sin, scale=TWO_PI).then_inc(s_trig, 1)
                step(s.activation(trig[:, j % 2, 0, :], phase[:, j % 2, :], ACT.Abs))
                s.activation(trig[:, j % 2, 0, :], trig[:, j % 2, 0, :], ACT.Sin, scale=-TWO_PI,
                             bias=half_pi[:, 0:1]).then_inc(s_phfree, 1)

            def gelu(q):
                act.wait_ge(s_yfree, q + 1)
                s.activation(uT[:, q, :], uT[:, q, :], ACT.Gelu_apprx_tanh).then_inc(s_gelu, 1)

            def relus(n):
                act.wait_ge(s_dot, n + 1)
                if n >= 2:
                    act.wait_ge(s_relufree, n - 1)
                t = 1 + n // HEADS
                s.activation(relu[:, n % 2, 0:NQT[t]], ps[5 + n % 2][:, 0:NQT[t]], ACT.Relu,
                             scale=64.0 ** -0.5).then_inc(s_relu, 1)

            def take(n):
                kind, i, _ = tiles[n]
                act.wait_ge(s_tile, n + 1)
                src = ps[n % 2]
                if kind == "g":
                    ins = s.activation(gate[:, i, :], src[:, :], ACT.Sigmoid, bias=bgate[:, i:i + 1])
                elif kind == "gg":
                    if i >= 2:
                        act.wait_ge(s_tile_v, i - 1)
                    ins = s.activation(glu_t[:, i % 2, :], src[:, :], ACT.Sigmoid)
                elif kind == "ki":
                    ins = s.activation(kiT[:, :], src[:, :], ACT.Copy)
                else:
                    dst = {"u": uT, "qi": qiT, "q": qT, "k": kT, "v": v}[kind]
                    ins = s.activation(dst[:, i, :], src[:, :], ACT.Copy)
                ins.then_inc(s_tile_a, 1)

            n = 0
            while tiles[n][0] == "u":
                take(n)
                n += 1
                if n == 2:
                    for q in range(8):
                        act.wait_ge(s_bbT, q + 1)
                        r, qq = q // 4, q % 4
                        s.activation(bT[:, r, qq, :], ps[4 + q % 4][:, 0:P], ACT.Copy).then_inc(s_bT, 1)
                    act.wait_ge(s_tau, 1)
                    act.wait_ge(s_const, 2)
                    phase_products(0)
            for j in range(SJ):
                trigs(j)
                take(n)
                n += 1
            while tiles[n][0] != "g":
                take(n)
                n += 1
            act.wait_ge(s_par[3], 64)
            for i in range(24):
                relus(i)
                for _ in range(gates_after(i)):
                    take(n)
                    n += 1
            for q in range(4):
                gelu(q)
            while tiles[n][0] == "g":
                take(n)
                n += 1

            def exps(i):
                t, hh = STEPS[i]
                act.wait_ge(s_lg, i + 1)
                if i >= 2:
                    act.wait_ge(s_pTp, i - 1)
                s.activation(prob[:, i % 2, 0:NQT[t]], logit[:, i % 2, 0:NQT[t]], ACT.Exp, scale=HD ** -0.5,
                             bias=amax[:, i % 2:i % 2 + 1], accum_out=rsum[:, t, hh:hh + 1]).then_inc(s_pr, 1)

            def keep_pT(i):
                t, hh = STEPS[i]
                act.wait_ge(s_pTp, i + 1)
                if i >= 2:
                    act.wait_ge(s_pv, i - 1)
                s.activation(pT[:, i % 2, 0:NQT[t]], ps[7][:, 0:NQT[t]], ACT.Copy).then_inc(s_pT, 1)

            for i in range(len(STEPS) + 2):
                if i < len(STEPS):
                    exps(i)
                if 1 <= i <= len(STEPS):
                    keep_pT(i - 1)
                if i % 4 == 1 and n < first_tile["at"]:
                    take(n)
                    n += 2
                if i >= 2 and STEPS[i - 2][1] == HEADS - 1:
                    t = STEPS[i - 2][0]
                    act.wait_ge(s_oTp, t + 1)
                    s.activation(qiT[:, :, P * t:P * t + P], ps[3][:, :].rearrange("p (k q) -> p k q", k=4),
                                 ACT.Copy).then_inc(s_oT, 1)
            while n < first_tile["at"]:
                take(n)
                n += 2
            act.wait_ge(s_hrow, TT)
            for r, nm in enumerate(("ln1_g", "ln1_b")):
                act.dma_start(gb[:, r, :], a[nm][0].partition_broadcast(P)).then_inc(s_gb2, 16)
            for t in range(TT):
                act.wait_ge(s_var, TT + t + 1)
                s.activation(rstd[:, 0:1], mv[:, 1:2], ACT.Sqrt, bias=eps[:, 0:1]).then_inc(s_rstd, 1)
                act.wait_ge(s_h1, t + 1)
                act.dma_start(h1_rows.rearrange("(t p) d -> p t d", p=P)[:, t, :], h[:, t, :]).then_inc(s_h1row, 16)
                for r in range(2):
                    act.wait_ge(s_h1T, 2 * t + r + 1)
                    if t > 0:
                        act.wait_ge(s_lgt, t)
                    s.activation(hT1[:, 4 * r:4 * r + 4, :], ps[6 + r][:, :].rearrange("p (k q) -> p k q", k=4),
                                 ACT.Copy).then_inc(s_h1e, 1)
                act.wait_ge(s_v8, t + 1)
                s.activation(gates[:, t, :], rt8[:, t, 0:TOPK], ACT.Exp, bias=gneg[:, 0:1],
                             accum_out=gsum[:, 0:1]).then_inc(s_ge, 1)
            for r, nm in enumerate(("ln2_g", "ln2_b")):
                act.dma_start(gb[:, r, :], a[nm][0].partition_broadcast(P)).then_inc(s_gb3, 16)
            def hi(i, c):
                act.wait_ge(s_raw[c % NRAW], (i * 2 + c // NRAW) * 16 + 16)
                if c >= NSPLIT:
                    act.wait_ge(s_cu, i * PARTS + c - NSPLIT + 1)
                s.activation(w_hi[c % NSPLIT][:, :], raw[:, c % NRAW, :], ACT.Copy).then_inc(s_hi, 1)

            for c in range(3):
                hi(0, c)
            act.wait_ge(s_tab, 1)
            final = act.value_load(etab_i[0:1, NB:NB + 1], min_val=NE - 1, max_val=NB - 2)

            def T_hi(dst, half, job, bank):
                act.wait_ge(s_tr, job + 1)
                s.activation(dst[:, 4 * half:4 * half + 4, :].rearrange("p k t -> p (k t)"), ps[bank][:, :], ACT.Copy).then_inc(s_thi, 1)

            def sigm(i, half):
                act.wait_ge(s_g7, i * 2 + half + 1)
                s.activation(sig, swg, ACT.Sigmoid, scale=SWI).then_inc(s_sig, 1)

            def blk(i, last):
                def his(lo, up):
                    for c in turns(lo, up, last):
                        hi(i, c)
                his(5, 6)
                sigm(i, 0)
                his(7, 9)
                T_hi(a_hi, 0, i * 4 + 2, 6)
                his(10, 10)
                sigm(i, 1)
                if not last:
                    T_hi(x_hi, 0, i * 4 + 3, 7)
                    T_hi(x_hi, 1, i * 4 + 4, 6)
                his(11, 12)
                T_hi(a_hi, 1, i * 4 + 5 - (2 if last else 0), 7)
                his(13, 15)
                act.wait_ge(s_cu, i * PARTS + (12 if last else 13))
                act.wait_ge(s_rnow, i + 1)
                for r in range(2):
                    s.activation(ysb[:, r, :], ps[4 + r][0:BLK, :], ACT.Copy).then_inc(s_ysb, 1)
                his(16, 16)

            act.sem_inc(s_ysb, 1)
            for half in range(2):
                T_hi(x_hi, half, half, 6 + half)
            act.wait_ge(s_b3l, 1)
            for c in range(3, 5):
                hi(0, c)
            with act.Fori(0, final) as i:
                blk(i, False)
            blk(final, True)
            for t in range(TT):
                act.wait_ge(s_var, 2 * TT + t + 1)
                s.activation(rstd[:, 0:1], mv[:, 1:2], ACT.Sqrt, bias=eps[:, 0:1]).then_inc(s_rstd, 1)
                act.wait_ge(s_nb, t + 1)
                s.activation(h[:, t, :], h[:, t, :], ACT.Identity, scale=rstd[:, 1:2], bias=gneg[:, 0:1])\
                    .then_inc(s_nrm, 1)

        @block.vector
        def _(dve):
            d = nc.vector
            step = Steps(dve, s_d)
            nvar = [0]
            step(d.memset(eps[:, :], EPS))
            step(d.memset(half_pi[:, :], TWO_PI / 4))

            def norm(row, n, step):
                for r in range(2):
                    step(d.bn_stats(stats[:, r, :], row[:, 512 * r:512 * r + 512]))
                d.bn_aggr(mv[:, :], stats[:, :, :]).then_inc(s_var, 1)
                dve.wait_ge(s_rstd, n)
                step(d.reciprocal(rstd[:, 1:2], rstd[:, 0:1]))
                dve.wait_ge(s_var, n)
                return d.tensor_scalar(row, row, mv[:, 0:1], rstd[:, 1:2], ALU.subtract, ALU.mult)

            for t in range(TT):
                dve.wait_ge(s_x[t], 16)
                norm(h[:, t, :], t + 1, step).then_inc(s_xhat, 1)
                dve.wait_ge(s_xhat, t + 1)
            lr, li = sp_in[:, 0, :], sp_in[:, 1, :]
            W = lambda q: spw[:, q, :]
            dve.wait_ge(s_dt, 1)
            d.tensor_tensor(W(1), lr, W(0), ALU.mult).then_inc(s_th, 1)
            step(d.tensor_tensor(W(3), li, W(0), ALU.mult))
            step(d.tensor_scalar(W(8), W(3), 1.0 / TWO_PI, ROUND, ALU.mult, ALU.add))
            step(d.tensor_scalar(W(8), W(8), ROUND, None, ALU.subtract))
            for c in (PI_C1, PI_C2, PI_C3):
                step(d.scalar_tensor_tensor(W(3), W(8), -c, W(3), ALU.mult, ALU.add))
            d.tensor_scalar(W(4), W(3), PI_SAFE, -PI_SAFE, ALU.min, ALU.max).then_inc(s_th, 1)
            step(d.tensor_scalar(W(20), W(3), 1.0 / TWO_PI, None, ALU.mult))
            step(d.tensor_scalar(W(21), W(20), ROUND14, None, ALU.add))
            step(d.tensor_scalar(W(21), W(21), ROUND14, None, ALU.subtract))
            d.tensor_tensor(W(22), W(20), W(21), ALU.subtract).then_inc(s_tau, 1)
            dve.wait_ge(s_sc, 2)
            step(d.tensor_tensor(W(9), W(2), W(7), ALU.mult))
            step(d.tensor_scalar(W(9), W(9), 1.0, None, ALU.subtract))
            step(d.tensor_tensor(W(10), W(2), W(5), ALU.mult))
            step(d.tensor_tensor(W(11), lr, lr, ALU.mult))
            step(d.tensor_tensor(W(12), li, li, ALU.mult))
            step(d.tensor_tensor(W(11), W(11), W(12), ALU.add))
            step(d.reciprocal(W(11), W(11)))
            for dst, (p0, q0), (p1, q1), op in ((14, (9, lr), (10, li), ALU.add), (15, (10, lr), (9, li), ALU.subtract)):
                step(d.tensor_tensor(W(12), W(p0), q0, ALU.mult))
                step(d.tensor_tensor(W(13), W(p1), q1, ALU.mult))
                step(d.tensor_tensor(W(dst), W(12), W(13), op))
                step(d.tensor_tensor(W(dst), W(dst), W(11), ALU.mult))
            dve.wait_ge(s_par[1], 32)
            cr, ci = (spw[:, q, :].unsqueeze(2).to_broadcast([P, SJ, GROUP]) for q in (14, 15))
            tmp = m[:, 0:2, 0:SJ * GROUP].rearrange("p r (j c) -> p r j c", c=GROUP)
            dve.wait_ge(s_const, 2)
            step(d.memset(bblk[:, :, :, :], 0.0))
            for r, (x0, x1, op) in enumerate(((cr, ci, ALU.subtract), (ci, cr, ALU.add))):
                step(d.tensor_tensor(tmp[:, 0], x0, braw[:, 0], ALU.mult))
                step(d.tensor_tensor(tmp[:, 1], x1, braw[:, 1], ALU.mult))
                for w in range(2):
                    rows = slice(64 * w, 64 * w + 64)
                    ins = d.tensor_tensor(bblk[rows, r, :, GROUP * w:GROUP * w + GROUP], tmp[rows, 0], tmp[rows, 1], op)
                    if r == 1 and w == 1:
                        ins.then_inc(s_bb, 1)
                    else:
                        step(ins)
            step(d.memset(cblk[:, :, :, :], 0.0))
            for r in range(2):
                dve.wait_ge(s_cT, 4 * r + 4)
                src = ps[2 + r][:, :].rearrange("p (j w c) -> p j w c", w=2, c=GROUP)
                for w in range(2):
                    rows = slice(64 * w, 64 * w + 64)
                    ins = d.tensor_scalar(cblk[rows, r, :, GROUP * w:GROUP * w + GROUP], src[rows, :, w, :],
                                          1.0 if r == 0 else -1.0, None, ALU.mult)
                    if (r, w) == (1, 1):
                        ins.then_inc(s_cblk, 1)
                        dve.wait_ge(s_cblk, 1)
                    else:
                        step(ins)

            def s5(j):
                dve.wait_ge(s_bu, j + 1)
                dve.wait_ge(s_phfree, j + 1)
                c, sn = trig[:, j % 2, 0, :], trig[:, j % 2, 1, :]
                br, bi = ps[2], ps[3]
                step(d.tensor_tensor(m[:, 0, :], br[:, :], c, ALU.mult))
                step(d.tensor_tensor(m[:, 1, :], bi[:, :], sn, ALU.mult))
                step(d.tensor_tensor(m[:, 2, :], bi[:, :], c, ALU.mult))
                d.tensor_tensor(m[:, 3, :], br[:, :], sn, ALU.mult).then_inc(s_bufree, 1)
                dve.wait_ge(s_bufree, j + 1)
                step(d.tensor_tensor(m[:, 0, :], m[:, 0, :], m[:, 1, :], ALU.add))
                step(d.tensor_tensor(m[:, 2, :], m[:, 2, :], m[:, 3, :], ALU.subtract))
                decay = spw[:, 2, j:j + 1].to_broadcast([P, SEQ])
                step(d.tensor_tensor_scan(m[:, 1, :], decay, m[:, 0, :], 0.0, ALU.mult, ALU.add))
                step(d.tensor_tensor_scan(m[:, 3, :], decay, m[:, 2, :], 0.0, ALU.mult, ALU.add))
                if j >= 2:
                    dve.wait_ge(s_stfree, j - 1)
                wr, w_im = w_st[:, j % 2, 0, :], w_st[:, j % 2, 1, :]
                step(d.tensor_tensor(m[:, 0, :], m[:, 1, :], c, ALU.mult))
                step(d.tensor_tensor(m[:, 2, :], m[:, 3, :], sn, ALU.mult))
                step(d.tensor_tensor(wr, m[:, 0, :], m[:, 2, :], ALU.subtract))
                step(d.tensor_tensor(m[:, 0, :], m[:, 1, :], sn, ALU.mult))
                d.tensor_tensor(m[:, 2, :], m[:, 3, :], c, ALU.mult).then_inc(s_rot, 1)
                dve.wait_ge(s_rot, j + 1)
                d.tensor_tensor(w_im, m[:, 0, :], m[:, 2, :], ALU.add).then_inc(s_st, 1)
                dve.wait_ge(s_st, j + 1)

            def y_out(q):
                dve.wait_ge(s_stfree, 4 * q + 4)
                if q == 0:
                    dve.wait_ge(s_par[3], 64)
                d.scalar_tensor_tensor(uT[:, q, :], uT[:, q, :], dskip[:, q:q + 1], ps[5 - q % 2][:, :],
                                       ALU.mult, ALU.add).then_inc(s_yfree, 1)

            for j in range(SJ):
                s5(j)
                if j >= 5 and j % 4 == 1:
                    y_out((j - 5) // 4)
            y_out(3)

            dve.wait_ge(s_wi, 1)
            step(d.tensor_scalar(wi[:, :, :], wi_ps(ps), HEADS ** -0.5, None, ALU.mult))
            step(d.tensor_tensor(m[:, 0, 0:P], ident[:, :], tcol[:, 0:P], ALU.mult))
            step(d.reduce_sum(qpos[:, 0:1], m[:, 0, 0:P], AXL.X))
            for t in range(1, TT):
                step(d.tensor_scalar(qpos[:, t:t + 1], qpos[:, 0:1], float(P * t), None, ALU.add))
            dve.wait_ge(s_bbT, 8)
            d.tensor_scalar(far[:, 0, :], tcol[:, :], -1.0, qpos[:, 0:1], ALU.mult, ALU.add).then_inc(s_far0, 1)
            for t in range(1, TT):
                nk = NQT[t]
                sc = score[:, t % 2, 0:nk]
                for hh in range(HEADS):
                    n = HEADS * (t - 1) + hh
                    dve.wait_ge(s_relu, n + 1)
                    src, wcol = relu[:, n % 2, 0:nk], wi[:, t, hh:hh + 1]
                    if hh == 0:
                        ins = d.tensor_scalar(sc, src, wcol, None, ALU.mult)
                    else:
                        ins = d.scalar_tensor_tensor(sc, src, wcol, sc, ALU.mult, ALU.add)
                    ins.then_inc(s_relufree, 1)
                    dve.wait_ge(s_relufree, n + 1)
                dve.wait_ge(s_masked, t + 1)
                for _ in range(NSEL // 8):
                    step(d.max(top8[:, :], sc))
                    step(d.match_replace(sc, top8[:, :], sc, TAKEN))
                step(d.tensor_scalar(far[:, t, 0:nk], sc, TAKEN, FAR, ALU.not_equal, ALU.mult))
                d.scalar_tensor_tensor(far[:, t, 0:nk], far[:, t, 0:nk], qpos[:, t:t + 1], tcol[:, 0:nk],
                                       ALU.add, ALU.subtract).then_inc(s_far, 1)
                dve.wait_ge(s_far, t)
            dve.wait_ge(s_masked, 1)

            def logits(i):
                t, hh = STEPS[i]
                nk = NQT[t]
                dve.wait_ge(s_qk, i + 1)
                if i >= 2:
                    dve.wait_ge(s_pr, i - 1)
                lgt = logit[:, i % 2, 0:nk]
                step(d.scalar_tensor_tensor(lgt, far[:, t, 0:nk], -SLOPES[hh] * HD ** 0.5, ps[5 + i % 2][:, 0:nk],
                                            ALU.mult, ALU.add))
                step(d.reduce_max(top8[:, 0:1], lgt, AXL.X))
                d.tensor_scalar(amax[:, i % 2:i % 2 + 1], top8[:, 0:1], -HD ** -0.5, None, ALU.mult).then_inc(s_lg, 1)
                dve.wait_ge(s_lg, i + 1)

            nval = [0]

            def value(i):
                n = first_tile["gg"] + 2 * i + 1
                dve.wait_ge(s_tile, n + 1)
                dve.wait_ge(s_tile_a, taken[n - 1][1])
                d.tensor_tensor(glu_t[:, i % 2, :], glu_t[:, i % 2, :], ps[n % 2][:, :], ALU.mult).then_inc(s_tile_v, 1)
                dve.wait_ge(s_tile_v, i + 1)
                step(d.tensor_tensor(gate[:, i, :], gate[:, i, :], glu_t[:, i % 2, :], ALU.mult))

            for i in range(len(STEPS) + 2):
                if i < len(STEPS):
                    logits(i)
                if i % 4 == 3:
                    value(i // 4)
                if i >= 2 and STEPS[i - 2][1] == HEADS - 1:
                    t = STEPS[i - 2][0]
                    dve.wait_ge(s_pv, i - 1)
                    dve.wait_ge(s_pr, i - 1)
                    step(d.reciprocal(rinv[:, :], rsum[:, t, :]))
                    if t > 0:
                        dve.wait_ge(s_oTp, t)
                    d.tensor_tensor(oq.rearrange("p o (h e) -> p (o h) e", h=HEADS),
                                    ps[2][:, :].rearrange("p (h e) -> p h e", h=HEADS),
                                    rinv[:, :].unsqueeze(2).to_broadcast([P, HEADS, HD]), ALU.mult).then_inc(s_on, 1)
                    dve.wait_ge(s_on, t + 1)
            for i in range(8):
                n = first_tile["at"] + i
                dve.wait_ge(s_tile, n + 1)
                d.tensor_tensor(mix_t[:, 0, :], gate[:, 8 + i, :], ps[n % 2][:, :], ALU.mult).then_inc(s_tile_v, 1)
                dve.wait_ge(s_tile_v, 8 + i + 1)
                d.tensor_tensor(mixT[:, i, :], gate[:, i, :], mix_t[:, 0, :], ALU.add).then_inc(s_mix, 1)
                dve.wait_ge(s_mix, i + 1)
            dve.wait_ge(s_hrow, TT)
            dve.wait_ge(s_gb2, 32)
            for t in range(TT):
                for r in range(2):
                    n = 2 * t + r
                    dve.wait_ge(s_wo, n + 1)
                    d.scalar_tensor_tensor(h[:, t, 512 * r:512 * r + 512], h[:, t, 512 * r:512 * r + 512], ALPHA,
                                           ps[2 + n % 4][:, :], ALU.mult, ALU.add).then_inc(s_wofree, 1)
                    dve.wait_ge(s_wofree, n + 1)
                step(norm(h[:, t, :], TT + t + 1, step))
                step(d.tensor_tensor(h[:, t, :], h[:, t, :], gb[:, 0, :], ALU.mult))
                d.tensor_tensor(h[:, t, :], h[:, t, :], gb[:, 1, :], ALU.add).then_inc(s_h1, 1)
                dve.wait_ge(s_lgt, t + 1)
                d.tensor_tensor(lg[:, :], b_rt[:, :], ps[0][:, 0:NE], ALU.add).then_inc(s_lgfree, 1)
                dve.wait_ge(s_lgfree, t + 1)
                step(d.max(rt8[:, t, :], lg[:, :]))
                step(d.max_index(ri8[:, t, :], rt8[:, t, :], lg[:, :]))
                d.tensor_scalar(gneg[:, :], rt8[:, t, 0:1], -1.0, None, ALU.mult).then_inc(s_v8, 1)
                step(d.tensor_copy(rif[:, t, :], ri8[:, t, :]))
                step(d.tensor_scalar(chosen[:, t, :], tcol[:, 0:NE], rif[:, t, 0:1], None, ALU.is_equal))
                for k in range(1, TOPK):
                    step(d.scalar_tensor_tensor(chosen[:, t, :], tcol[:, 0:NE], rif[:, t, k:k + 1], chosen[:, t, :],
                                                ALU.is_equal, ALU.add))
                d.tensor_copy(chosen_b[:, t, :], chosen[:, t, :]).then_inc(s_chosen, 1)
                dve.wait_ge(s_ge, t + 1)
                step(d.reciprocal(gsum[:, 1:2], gsum[:, 0:1]))
                step(d.tensor_scalar(gates[:, t, :], gates[:, t, :], gsum[:, 1:2], None, ALU.mult))
            dve.wait_ge(s_cnt, 1)
            cnt, more, upto_e, t0 = rw[:, 0, :], rw[:, 1, :], rw[:, 2, :], rw[:, 3, :]
            step(d.tensor_copy(cnt, ps[1][:, P:P + NE]))
            step(d.tensor_scalar(more, cnt, float(BLK), None, ALU.is_gt))
            for b in MORE[1:]:
                step(d.scalar_tensor_tensor(more, cnt, float(BLK * b), more, ALU.is_gt, ALU.add))
            step(d.memset(t0, 1.0))
            step(d.tensor_tensor_scan(upto_e, t0, more, 0.0, ALU.mult, ALU.add))
            step(d.tensor_tensor(t0, upto_e, more, ALU.subtract))
            step(d.tensor_scalar(t0, t0, float(NE - 1), None, ALU.add))
            step(d.tensor_tensor(t0, t0, tcol[:, 0:NE], ALU.subtract))
            for t in range(TT):
                pos, f, ad = posw[:, t, 0, :], posw[:, t, 1, :], posw[:, t, 2, :]
                step(d.tensor_copy(pos, ps[1][:, NE * t:NE * t + NE]))
                step(d.tensor_scalar(f, pos, float(BLK), None, ALU.is_ge))
                for b in MORE[1:]:
                    step(d.scalar_tensor_tensor(f, pos, float(BLK * b), f, ALU.is_ge, ALU.add))
                step(d.tensor_tensor(ad, t0, f, ALU.add))
                step(d.scalar_tensor_tensor(ad, f, 0.5, ad, ALU.is_gt, ALU.mult))
                step(d.tensor_tensor(ad, ad, tcol[:, 0:NE], ALU.add))
                step(d.scalar_tensor_tensor(pos, f, -float(BLK), pos, ALU.mult, ALU.add))
                step(d.scalar_tensor_tensor(ad, pos, float(NB), ad, ALU.mult, ALU.add))
                for k in range(TOPK):
                    step(d.scalar_tensor_tensor(pos, tcol[:, 0:NE], rif[:, t, k:k + 1], ad, ALU.is_equal, ALU.mult,
                                                accum_out=addr[:, t, k:k + 1]))
                d.tensor_copy(addr_i[:, TOPK * t:TOPK * t + TOPK], addr[:, t, :]).then_inc(s_adr, 1)
            step(d.tensor_copy(etab[0:1, 0:NE], tcol[0:1, 0:NE]))
            step(d.tensor_tensor(xcmp[:, :, :], upto_e[0:1, :].unsqueeze(1).to_broadcast([1, BTAIL, NE]),
                                 tcol[0:1, 0:BTAIL].unsqueeze(2).to_broadcast([1, BTAIL, NE]), ALU.is_le))
            step(d.reduce_sum(etab[0:1, NE:NB], xcmp[:, :, :], AXL.X))
            step(d.tensor_scalar(etab[0:1, NE:NB], etab[0:1, NE:NB], float(NE - 1), None, ALU.min))
            step(d.tensor_scalar(etab[0:1, NB:NB + 1], upto_e[0:1, NE - 1:NE], float(NE - 1), None, ALU.add))
            d.tensor_copy(etab_i[:, :], etab[:, :]).then_inc(s_tab, 1)
            dve.wait_ge(s_tab, 1)
            def pick_expert(i):
                e = 0 if isinstance(i, int) else dve.value_load(etab_i[0:1, bass.ds(i, 1)], min_val=0, max_val=NE - 1)
                d.tensor_copy(pick[:, :], eye96[:, bass.ds(e, 1)].to_broadcast([96, BLK])).then_inc(s_b3, 1)

            def lo(i, c):
                dve.wait_ge(s_hi, i * PARTS + c + 1)
                n = PART // 2 if c in BY_POOL else PART
                if c - 1 in BY_POOL and n == PART:
                    dve.wait_ge(s_lo_g, i * len(BY_POOL) + BY_POOL.index(c - 1) + 1)
                d.tensor_tensor(w_lo[c % NSPLIT][:, 0:n], raw[:, c % NRAW, 0:n], w_hi[c % NSPLIT][:, 0:n],
                                ALU.subtract).then_inc(s_lo, 1)

            for c in range(3):
                lo(0, c)
            pick_expert(0)
            dve.wait_ge(s_slots, 16)
            step(d.tensor_scalar(toks[:, :], slots[:, :], 2, None, ALU.arith_shift_right))
            final = dve.value_load(etab_i[0:1, NB:NB + 1], min_val=NE - 1, max_val=NB - 2)
            dve.wait_ge(s_h1row, 16 * TT)
            d.tensor_copy(tok_now[:, :], toks[:, 0:1]).then_inc(s_tnow, 1)

            def T_lo(dst, upper, half, job, bank):
                dve.wait_ge(s_thi, job + 1)
                four = lambda x: x[:, 4 * half:4 * half + 4, :].rearrange("p k t -> p (k t)")
                d.tensor_tensor(four(dst), ps[bank][:, :], four(upper), ALU.subtract).then_inc(s_tlo, 1)

            def swiglu(i, half):
                n = i * 2 + half
                G, L = ps[2 * half], ps[2 * half + 1]
                dve.wait_ge(s_cu, i * PARTS + 4 * half + 4)
                d.tensor_scalar(swg, G[:, :], LIMIT, None, ALU.min).then_inc(s_g7, 1)
                step(d.tensor_scalar(swl, L[:, :], LIMIT, -LIMIT, ALU.min, ALU.max))
                dve.wait_ge(s_sig, n + 1)
                step(d.tensor_tensor(swg, swg, sig, ALU.mult))
                d.scalar_tensor_tensor(act_s[:, half, :], swl, 1.0, swg, ALU.add, ALU.mult).then_inc(s_act, 1)
                dve.wait_ge(s_act, n + 1)

            def blk(i, last):
                def los(first, up):
                    for c in turns(first, up, last):
                        lo(i, c)
                if not last:
                    dve.wait_ge(s_gat, i * 16 + 16)
                    nx = i + 1
                    d.tensor_copy(tok_now[:, :], toks[:, bass.ds(nx, 1)]).then_inc(s_tnow, 1)
                los(5, 6)
                swiglu(i, 0)
                los(7, 9)
                T_lo(a_lo, a_hi, 0, i * 4 + 2, 6)
                los(10, 10)
                swiglu(i, 1)
                if not last:
                    T_lo(x_lo, x_hi, 0, i * 4 + 3, 7)
                    T_lo(x_lo, x_hi, 1, i * 4 + 4, 6)
                    dve.wait_ge(s_cu, i * PARTS + 8)
                    pick_expert(i + 1)
                los(11, 12)
                T_lo(a_lo, a_hi, 1, i * 4 + 5 - (2 if last else 0), 7)
                dve.wait_ge(s_yout, i * 16 + 16)
                d.tensor_copy(row_now[:, :], slots[:, bass.ds(i, 1)]).then_inc(s_rnow, 1)
                los(13, 16)

            for half in range(2):
                T_lo(x_lo, x_hi, half, half, 6 + half)
            for c in range(3, 5):
                lo(0, c)
            before_loop = step.n
            PER = 4
            with dve.Fori(0, final) as i:
                step.base, step.n = before_loop + i * PER, 0
                blk(i, False)
                assert step.n == PER
            step.base, step.n = before_loop + final * PER, 0
            blk(final, True)
            dve.wait_ge(s_d, before_loop + final * PER + PER)
            step = Steps(dve, s_dend)
            dve.wait_ge(s_gb3, 32)
            dve.wait_ge(s_ah1, TT)
            for t in range(TT):
                dve.wait_ge(s_yld[t], 16)
                for k in range(TOPK):
                    step(d.scalar_tensor_tensor(h[:, t, :], ring[:, t, DM * k:DM * k + DM], gates[:, t, k:k + 1],
                                                h[:, t, :], ALU.mult, ALU.add))
                for r in range(2):
                    step(d.bn_stats(stats[:, r, :], h[:, t, 512 * r:512 * r + 512]))
                if t > 0:
                    dve.wait_ge(s_nrm, t)
                d.bn_aggr(mv[:, :], stats[:, :, :]).then_inc(s_var, 1)
                dve.wait_ge(s_rstd, 2 * TT + t + 1)
                step(d.reciprocal(rstd[:, 1:2], rstd[:, 0:1]))
                d.scalar_tensor_tensor(gneg[:, :], mv[:, 0:1], -1.0, rstd[:, 1:2], ALU.mult, ALU.mult).then_inc(s_nb, 1)
            dve.wait_ge(s_nrm, TT)
            step(d.tensor_tensor(h[:, TT - 1, :], h[:, TT - 1, :], gb[:, 0, :], ALU.mult))
            d.tensor_tensor(h[:, TT - 1, :], h[:, TT - 1, :], gb[:, 1, :], ALU.add).then_inc(s_oln_v, 1)

        @block.tensor
        def _(pe):
            mm, tr = nc.tensor.matmul, nc.tensor.transpose
            pe.wait_ge(s_const, 1)
            for k in range(KD):
                if k >= 4:
                    pe.wait_ge(s_hT, k - 3)
                for t in range(TT):
                    if k == 0:
                        pe.wait_ge(s_xhat, t + 1)
                    ins = tr(ps[4 + k % 4][:, P * t:P * t + P], h[:, t, P * k:P * k + P], ident[:, :])
                ins.then_inc(s_lnT, 1)
            pe.wait_ge(s_hT, KD)

            def arrive(n):
                count = 0
                for c in range(n % 2, n + 1, 2):
                    count += 32 if FRONT[c][0] == "glu" else 16
                pe.wait_ge(s_w[n % 2], count)

            def tile(n, chunk_n, last=False):
                kind, i, _ = tiles[n]
                if n >= 2:
                    pe.wait_ge(*taken[n - 2])
                o = ps[n % 2]
                w = ring[:, chunk_n % 2, :]
                if kind == "ki":
                    for k in range(KD):
                        ins = mm(o[:, :], small[:, k, 0:P], hT[:, k, :], start=k == 0, stop=k == KD - 1)
                elif kind == "v":
                    w = w.rearrange("p (k n) -> p k n", k=KD)
                    for k in range(KD):
                        ins = mm(o[:, :], hT[:, k, P * i:P * i + P], w[:, k, :], start=k == 0, stop=k == KD - 1)
                elif kind in ("gg", "val"):
                    w = w.rearrange("p (k r n) -> p k r n", k=4, r=2)
                    c = P * (i % 4)
                    for k in range(4):
                        ins = mm(o[:, :], w[:, k, 1 if kind == "gg" else 0, c:c + P], uT[:, k, :], start=k == 0,
                                 stop=k == 3)
                elif kind == "at":
                    w = w.rearrange("p (k n) -> p k n", k=4)
                    for k in range(4):
                        ins = mm(o[:, :], w[:, k, P * i:P * i + P], qiT[:, k, :], start=k == 0, stop=k == 3)
                else:
                    w = w.rearrange("p (k n) -> p k n", k=KD)
                    c = P * (i % 4)
                    for k in range(KD):
                        ins = mm(o[:, :], w[:, k, c:c + P], hT[:, k, :], start=k == 0, stop=k == KD - 1)
                ins.then_inc(s_tile, 1)

            arrive(0)
            n = 0
            for i in range(4):
                tile(n, 0)
                n += 1
                if i == 1:
                    pe.wait_ge(s_par[2], 64)
                    for r in range(2):
                        for q in range(4):
                            tr(ps[2 + r][:, P * q:P * q + P], craw[:, r, q, :], ident[:, :]).then_inc(s_cT, 1)
                    pe.wait_ge(s_bb, 1)
                    for q in range(8):
                        r, qq = q // 4, q % 4
                        if q >= 4:
                            pe.wait_ge(s_bT, q - 3)
                        tr(ps[4 + q % 4][:, 0:P], bblk[:, r, 4 * qq:4 * qq + 4, :].rearrange("p j c -> p (j c)"), ident[:, :])\
                            .then_inc(s_bbT, 1)

            pe.wait_ge(*taken[n - 1])
            pe.wait_ge(s_bT, 8)
            pe.wait_ge(s_cblk, 1)

            def bu(j):
                rows = slice(32 * (j % 4), 32 * (j % 4) + 32)
                if j >= 1:
                    pe.wait_ge(s_bufree, j)
                for r in range(2):
                    ins = mm(ps[2 + r][:, :], bT[rows, r, j // 4, :], uT[rows, j // 4, :], start=True, stop=True)
                ins.then_inc(s_bu, 1)

            def ymm(j):
                q, rows = j // 4, slice(32 * (j % 4), 32 * (j % 4) + 32)
                pe.wait_ge(s_st, j + 1)
                if j % 4 == 0 and q > 1:
                    pe.wait_ge(s_yfree, q - 1)
                for r in range(2):
                    ins = mm(ps[5 - q % 2][rows, :], cblk[:, r, j, :], w_st[:, j % 2, r, :], start=r == 0, stop=r == 1)
                ins.then_inc(s_stfree, 1)

            order = [(1, 4), ("small", 1), (2, 4), (3, 4), (4, 4)]
            flat = [(c, i == cnt - 1) for c, cnt in order for i in range(cnt)]
            for j, (c, last) in enumerate(flat):
                if j < SJ:
                    bu(j)
                if c == "small":
                    pe.wait_ge(s_small, 32)
                elif c != (flat[j - 1][0] if j else None):
                    arrive(c)
                tile(n, c if c != "small" else 0)
                n += 1
                if 1 <= j <= SJ:
                    ymm(j - 1)
            for t in range(TT):
                for k in range(KD):
                    ins = mm(ps[7][:, HEADS * t:HEADS * t + HEADS], hT[:, k, P * t:P * t + P], small[:, k, P:P + HEADS],
                             start=k == 0, stop=k == KD - 1)
            ins.then_inc(s_wi, 1)
            def gate_tile(n):
                c = 5 + (n - first_tile["g"]) // 4
                if (n - first_tile["g"]) % 4 == 0:
                    arrive(c)
                tile(n, c)

            pe.wait_ge(*taken[n - 1])
            for i in range(24):
                t, hh = 1 + i // HEADS, i % HEADS
                rows = slice(64 * (hh % 2), 64 * (hh % 2) + 64)
                if i == 0:
                    pe.wait_ge(s_yfree, 3)
                if i >= 2:
                    pe.wait_ge(s_relu, i - 1)
                mm(ps[5 + i % 2][:, 0:NQT[t]], qiT[rows, hh // 2, P * t:P * t + P], kiT[rows, 0:NQT[t]], start=True,
                   stop=True).then_inc(s_dot, 1)
                for _ in range(gates_after(i)):
                    gate_tile(n)
                    n += 1
            while n < first_tile["gg"]:
                gate_tile(n)
                n += 1

            def qk(i):
                t, hh = STEPS[i]
                rows = slice(64 * (hh % 2), 64 * (hh % 2) + 64)
                if i == 0:
                    pe.wait_ge(s_relu, 24)
                if i >= 2:
                    pe.wait_ge(s_lg, i - 1)
                mm(ps[5 + i % 2][:, 0:NQT[t]], qT[rows, hh // 2, P * t:P * t + P], kT[rows, hh // 2, 0:NQT[t]],
                   start=True, stop=True).then_inc(s_qk, 1)

            def probsT(i):
                t, hh = STEPS[i]
                pe.wait_ge(s_pr, i + 1)
                if i >= 1:
                    pe.wait_ge(s_pT, i)
                for c in range(t + 1):
                    ins = tr(ps[7][:, P * c:P * c + P], prob[:, i % 2, P * c:P * c + P], ident[:, :])
                ins.then_inc(s_pTp, 1)
                return ins

            def pv(i):
                t, hh = STEPS[i]
                pe.wait_ge(s_pT, i + 1)
                if hh == 0 and t > 0:
                    pe.wait_ge(s_on, t)
                for c in range(t + 1):
                    ins = mm(ps[2][:, HD * hh:HD * hh + HD], pT[:, i % 2, P * c:P * c + P],
                             v[:, c, HD * hh:HD * hh + HD], start=c == 0, stop=c == t)
                ins.then_inc(s_pv, 1)

            def o_T(t):
                pe.wait_ge(s_on, t + 1)
                if t > 0:
                    pe.wait_ge(s_oT, t)
                for k in range(4):
                    ins = tr(ps[3][:, P * k:P * k + P], scr[:, 12, P * k:P * k + P], ident[:, :])
                ins.then_inc(s_oTp, 1)

            pe.wait_ge(s_gelu, 4)
            pe.wait_ge(s_far, TT - 1)
            pe.wait_ge(s_st, SJ)
            for i in range(len(STEPS) + 3):
                if i < len(STEPS):
                    qk(i)
                if i % 2 == 0 and n < first_tile["at"]:
                    c = 9 + (n - first_tile["gg"]) // 8
                    if (n - first_tile["gg"]) % 8 == 0:
                        arrive(c)
                    tile(n, c)
                    n += 1
                if 1 <= i <= len(STEPS):
                    probsT_wait = probsT(i - 1)
                if 2 <= i <= len(STEPS) + 1:
                    pv(i - 2)
                if i >= 3 and STEPS[i - 3][1] == HEADS - 1:
                    o_T(STEPS[i - 3][0])
            pe.wait_ge(s_oT, TT)
            arrive(11)
            for i in range(8):
                tile(n, 11)
                n += 1
            arrive(12)

            def w_out(t):
                for r in range(2):
                    i = 2 * t + r
                    if i >= 4:
                        pe.wait_ge(s_wofree, i - 3)
                    if i == 1:
                        pe.wait_ge(s_w1o, 16)
                    w = ring[:, 2 * r, :].rearrange("p (k n) -> p k n", k=KD)
                    for k in range(KD):
                        if i == 0:
                            pe.wait_ge(s_mix, k + 1)
                        ins = mm(ps[2 + i % 4][:, :], mixT[:, k, P * t:P * t + P], w[:, k, :], start=k == 0,
                                 stop=k == KD - 1)
                    ins.then_inc(s_wo, 1)

            def route(t):
                pe.wait_ge(s_h1, t + 1)
                for r in range(2):
                    if t > 0:
                        pe.wait_ge(s_h1e, 2 * t)
                    for k in range(4):
                        ins = tr(ps[6 + r][:, P * k:P * k + P], h[:, t, 512 * r + P * k:512 * r + P * k + P],
                                 ident[:, :])
                    ins.then_inc(s_h1T, 1)
                pe.wait_ge(s_h1e, 2 * t + 2)
                if t > 0:
                    pe.wait_ge(s_lgfree, t)
                for k in range(KD):
                    ins = mm(ps[0][:, 0:NE], hT1[:, k, :], w_rt[:, k, :], start=k == 0, stop=k == KD - 1)
                ins.then_inc(s_lgt, 1)

            pe.wait_ge(s_par[3], 64)
            for t in range(TT):
                w_out(t)
                if t > 0:
                    route(t - 1)
            route(TT - 1)
            for t in range(TT):
                pe.wait_ge(s_chosen, t + 1)
                for b in range(t + 1):
                    mm(ps[1][:, NE * t:NE * t + NE], before[:, :] if b == t else ones_b[:, :], chosen_b[:, b, :],
                       start=b == 0, stop=b == t)
            for b in range(TT):
                ins = mm(ps[1][:, P:P + NE], ones_b[:, :], chosen_b[:, b, :], start=b == 0, stop=b == TT - 1)
            ins.then_inc(s_cnt, 1)

            pe.wait_ge(s_tab, 1)
            final = pe.value_load(etab_i[0:1, NB:NB + 1], min_val=NE - 1, max_val=NB - 2)

            def T4(src, job, bank):
                pe.wait_ge(s_tlo, job - 1)
                for k in range(4):
                    ins = tr(ps[bank][:, BLK * k:BLK * k + BLK], src[:, P * k:P * k + P], ident[:, :])
                ins.then_inc(s_tr, 1)

            def product(o, xh, xl, c, w, stop):
                col = slice(w, w + 512)
                mm(o, xh, w_hi[c % NSPLIT][:, col], start=False, stop=False)
                mm(o, xl, w_hi[c % NSPLIT][:, col], start=False, stop=False)
                return mm(o, xh, w_lo[c % NSPLIT][:, col], start=False, stop=stop)

            def turn_products(i, c, p):
                if p < 8 and p % 2 == 0:
                    col = DFF * (p // 2 % 2) + 512 * (p // 4)
                    mm(ps[p // 2][:, :], pick[:, :], bias3[:, col:col + 512], start=True, stop=False)
                wait_split(pe, i, c)
                for k in range(4):
                    if p < 8:
                        kk = 4 * (p % 2) + k
                        ins = product(ps[p // 2][:, :], x_hi[:, kk, :], x_lo[:, kk, :], c, 512 * k, kk == KD - 1)
                    else:
                        kk, r = 2 * (p - 8) + k // 2, k % 2
                        ins = product(ps[4 + r][:, :], a_hi[:, kk, :], a_lo[:, kk, :], c, 512 * k, kk == KD - 1)
                ins.then_inc(s_cu, 1)

            def blk(i, last):
                A1 = i * 4 + (3 if last else 5)
                for c in turns(1, PARTS, last):
                    on, p = part_of(c, last)
                    if c == 7:
                        pe.wait_ge(s_ysb, i * 2 + 1)
                        for r in range(2):
                            mm(ps[4 + r][:, :], pick[:, :], bias3[:, 2 * DFF + 512 * r:2 * DFF + 512 * r + 512],
                               start=True, stop=False)
                    if c == 8:
                        if not last:
                            pe.wait_ge(s_gat, i * 16 + 32)
                            T4(xg[:, 0:512], i * 4 + 3, 7)
                            T4(xg[:, 512:1024], i * 4 + 4, 6)
                        pe.wait_ge(s_tlo, i * 4 + 3)
                    if c == 10:
                        pe.wait_ge(s_act, i * 2 + 2)
                        T4(act_s[:, 1, :], A1, 7)
                        if not last:
                            pe.wait_ge(s_tlo, i * 4 + 5)
                            pe.wait_ge(s_b3, i + 2)
                    if p == 10:
                        pe.wait_ge(s_tlo, A1 + 1)
                    turn_products(i, c, p)
                    if c == 5:
                        pe.wait_ge(s_act, i * 2 + 1)
                        T4(act_s[:, 0, :], i * 4 + 2, 6)

            pe.wait_ge(s_gat, 16)
            for half in range(2):
                for k in range(4):
                    c = 512 * half + P * k
                    ins = tr(ps[6 + half][:, BLK * k:BLK * k + BLK], xg[:, c:c + P], ident[:, :])
                ins.then_inc(s_tr, 1)
            pe.wait_ge(s_tlo, 2)
            pe.wait_ge(s_b3, 1)
            pe.wait_ge(s_b3l, 1)
            turn_products(0, 0, 0)
            with pe.Fori(0, final) as i:
                blk(i, False)
            blk(final, True)


def wi_ps(ps):
    return ps[7][:, 0:TT * HEADS].rearrange("p (t h) -> p t h", h=HEADS)


NAMES = ["x", "ln_in_g", "ln_in_b", "w_in", "b_gate", "lam_re", "lam_im", "log_dt", "b_re", "b_im", "c_re", "c_im",
         "d_skip", "w_glu", "w_attn_proj", "w_o", "ln1_g", "ln1_b", "w_router", "b_router", "w_up", "b_up",
         "w_down", "b_down", "ln2_g", "ln2_b"]


def kernel(**inputs):
    import numpy as _np
    import concourse.bacc as _bacc
    from concourse.bass_utils import run_bass_kernel_spmd as _run

    nc = _bacc.Bacc("TRN2", target_bir_lowering=False, num_devices=1)
    arrays, args = {}, {}
    for name in NAMES:
        x = _np.ascontiguousarray(inputs[name])
        arrays[f"in_{name}"] = x
        args[name] = nc.dram_tensor(f"in_{name}", x.shape, mybir.dt.from_np(x.dtype), kind="ExternalInput").ap()
    out = nc.dram_tensor("out_0", (1, SEQ, DM), F32, kind="ExternalOutput").ap()
    build(nc, args, out)
    r = _run(nc, [arrays], core_ids=[0])
    return r.results[0]["out_0"]
```

```python
from contextlib import ExitStack

import concourse.bass as bass
from concourse import mybir

ACT = mybir.ActivationFunctionType
ALU = mybir.AluOpType
AXL = mybir.AxisListType
F32 = mybir.dt.float32
F32R = mybir.dt.float32r
BF16 = mybir.dt.bfloat16
I32 = mybir.dt.int32
U32 = mybir.dt.uint32

P = 128
SEQ = 512
DM = 1024
TT = SEQ // P
KD = DM // P
SSM = 512
GROUP = 16
STATES = 64
SJ = SSM // GROUP * STATES // P
HEADS = 8
HD = 64
NSEL = min(256, SEQ // 4)
NE = 32
TOPK = 4
DFF = 1024
BLK = 96
NB = NE + SEQ * TOPK // BLK + 1
BTAIL = NB - NE
PARTS = 12
PART = 2048
NRAW, NSPLIT = 6, 4
BY_POOL = [7, 8, 11, 12]
MORE = range(1, -(-SEQ // BLK))
MORE_TILES = TT - BLK // P
FIRST = (TT - MORE_TILES) * TOPK
NOROW = SEQ * TOPK
ALPHA = 2.0 ** 0.25
EPS = 1e-5
LIMIT = 7.0
SWI = 1.702
TWO_PI = 6.283185307179586
PI_C1 = 6.28125
PI_C2 = 2029.0 / 1048576.0
PI_C3 = TWO_PI - PI_C1 - PI_C2
PI_SAFE = 3.1415925
ROUND = 12582912.0
ROUND14 = 768.0
MASKED = -3.0e38
TAKEN = -3.3e38
FAR = 1.0e30
SLOPES = [2.0 ** (-8.0 * (h + 1) / HEADS) for h in range(HEADS)]
CHUNK = 4096
C_U, C_Q, C_K, C_V, C_QI, C_KI, C_G = 0, 512, 1024, 1536, 2048, 2560, 2632
NSMALL = 136


class Steps:

    def __init__(self, engine, sem):
        self.engine, self.sem, self.n, self.base = engine, sem, 0, None

    def __call__(self, instruction):
        instruction.then_inc(self.sem, 1)
        self.n += 1
        self.engine.wait_ge(self.sem, self.n if self.base is None else self.base + self.n)


def build(nc, a, out):
    h1_rows = nc.dram_tensor("h1_rows", [SEQ, DM], F32, kind="Internal").ap()
    y_rows = nc.dram_tensor("y_rows", [SEQ * TOPK, DM], F32, kind="Internal").ap()
    first_list = nc.dram_tensor("first_list", [BLK * NE, 1], I32, kind="Internal").ap()
    more_list = nc.dram_tensor("more_list", [BLK * BTAIL, 1], I32, kind="Internal").ap()

    x_v = a["x"][0].rearrange("(t p) d -> p t d", p=P)
    w_in = a["w_in"][0].rearrange("(k p) n -> p k n", p=P)
    w_glu = a["w_glu"][0].rearrange("(k p) n -> p k n", p=P)
    w_att = a["w_attn_proj"][0].rearrange("(k p) n -> p k n", p=P)
    w_o = a["w_o"][0].rearrange("(k p) n -> p k n", p=P)
    out_v = out[0].rearrange("(t p) d -> p t d", p=P)

    with ExitStack() as ctx:
        def sb(name, shape, dt=F32):
            return ctx.enter_context(nc.sbuf_tensor(name, shape, dt))

        def sem(name):
            return ctx.enter_context(nc.semaphore(name))

        at_ring = -(-nc.sbuf_base // 32) * 32
        ring = sb("ring", [P, 6, CHUNK])
        hT = ring[:, 2, :].rearrange("p (k t) -> p k t", k=KD)
        qT = ring[:, 3, 0:2048].rearrange("p (k t) -> p k t", k=4)
        kT = ring[:, 3, 2048:4096].rearrange("p (k t) -> p k t", k=4)
        gate = ring[:, 4:6, :].rearrange("p s (k t) -> p (s k) t", k=KD)
        mixT = gate

        craw = ring[:, 4, 0:1024].rearrange("p (r q n) -> p r q n", r=2, q=4)
        bT = ring[:, 4, 1024:2048].rearrange("p (r q n) -> p r q n", r=2, q=4)
        small = ring[:, 4, 2048:2048 + KD * NSMALL].rearrange("p (k n) -> p k n", k=KD)
        cblk = ring[:, 5, 0:1024].rearrange("p (r j c) -> p r j c", r=2, j=SJ)

        h = sb("h", [P, TT, DM])
        at_u = -(-nc.sbuf_base // 32) * 32
        uT = sb("uT", [P, 4, SEQ])
        at_v = -(-nc.sbuf_base // 32) * 32
        v = sb("v", [P, TT, SSM])
        qiT = sb("qiT", [P, 4, SEQ])
        kiT = sb("kiT", [P, SEQ])
        wi = sb("wi", [P, TT, HEADS])
        far = sb("far", [P, TT, SEQ])
        ident = sb("ident", [P, P])
        tcol = sb("tcol", [P, SEQ])
        qpos = sb("qpos", [P, TT])
        gb = sb("gb", [P, 2, DM])
        gbc = sb("gbc", [P, 2, KD])
        bgate = sb("bgate", [P, 16])
        dskip = sb("dskip", [P, 4])
        eps = sb("eps", [P, 1])
        half_pi = sb("half_pi", [P, 1])
        stats = sb("stats", [P, 2, 6])
        mv = sb("mv", [P, 2])
        rstd = sb("rstd", [P, 2])
        sp_in = sb("sp_in", [P, 3, SJ])
        spw = sb("spw", [P, 24, SJ])
        tcol_i = far[:, 3, :].bitcast(I32)
        braw = far[:, 0:2, 0:SJ * GROUP].rearrange("p r (j c) -> p r j c", c=GROUP)
        bblk = far[:, 2:4, :].rearrange("p r (j c) -> p r j c", c=2 * GROUP)
        at_scr = -(-nc.sbuf_base // 32) * 32
        scr = sb("scr", [P, 16, SEQ])
        phase, turn, trig = scr[:, 0:2], scr[:, 2:4], scr[:, 4:8].rearrange("p (b r) t -> p b r t", b=2)
        m = scr[:, 8:12]
        w_st = scr[:, 12:16].rearrange("p (b r) t -> p b r t", b=2)
        score, relu = scr[:, 0:2], scr[:, 2:4]
        logit, prob, pT, glu_t = scr[:, 4:6], scr[:, 6:8], scr[:, 8:10], scr[:, 10:12]
        oq, mix_t = scr[:, 12:13], scr[:, 13:16]
        top8 = sb("top8", [P, 8])
        amax = sb("amax", [P, 2])
        rsum = sb("rsum", [P, TT, HEADS])
        rinv = sb("rinv", [P, HEADS])

        w_rt = sb("w_rt", [P, KD, NE])
        b_rt = sb("b_rt", [P, NE])
        lg = sb("lg", [P, NE])
        rt8 = sb("rt8", [P, TT, 8])
        ri8 = sb("ri8", [P, TT, 8], U32)
        rif = sb("rif", [P, TT, 8])
        gates = sb("gates", [P, TT, TOPK])
        gsum = sb("gsum", [P, 2])
        gneg = sb("gneg", [P, 1])
        chosen = sb("chosen", [P, TT, NE])
        chosen_b = sb("chosen_b", [P, TT, NE], BF16)
        before = sb("before", [P, P], BF16)
        ones_b = sb("ones_b", [P, P], BF16)
        rw = sb("rw", [P, 6, NE])
        pos = sb("pos", [P, TT, NE])
        adw = sb("adw", [P, TT, 2, NE])
        fw = sb("fw", [P, TT, NE])
        addr = sb("addr", [P, TT, TOPK])
        addr_i = sb("addr_i", [P, TT * TOPK], I32)
        more_i = sb("more_i", [P, MORE_TILES * TOPK], I32)
        code = sb("code", [P, TT * TOPK], I32)
        empty = sb("empty", [BLK, NB], I32)
        slots = sb("slots", [BLK, NB], I32)
        slot_now = sb("slot_now", [BLK, 1], I32)
        tok_now = sb("tok_now", [BLK, 1], I32)
        row_now = sb("row_now", [BLK, 1], I32)
        etab_i = sb("etab_i", [1, NB + 1], I32)
        etab = sb("etab", [1, NB + 1])
        bias3 = sb("bias3", [96, 3 * DFF], BF16)
        pick = sb("pick", [96, BLK], BF16)
        eye96 = sb("eye96", [96, NE])
        E = scr[:, :, :].rearrange("p a b -> p (a b)")
        xg = E[0:BLK, 6 * DFF:6 * DFF + DM]
        xcmp = far[0:1, 0:2, :].rearrange("o a b -> o (a b)")[:, 0:BTAIL * NE].rearrange("o (b e) -> o b e", e=NE)
        braw_b = E[0:96, 0:3 * DFF]
        brem = E[0:96, 3 * DFF:6 * DFF]
        hT1 = far[:, 2:4, :].rearrange("p a t -> p (a t)").rearrange("p (k t) -> p k t", k=KD)
        def over(name, shape, dt, tensor_at, offset=0):
            return nc.alloc_sbuf_tensor_at(name, shape, dt, offset=tensor_at + offset)

        hT_hi = over("hT_hi", [P, KD, SEQ], F32R, at_scr, 4 * 4 * SEQ)
        hT_lo = over("hT_lo", [P, KD, SEQ], F32R, at_ring, 4 * 2 * CHUNK)
        wg_hi = over("wg_hi", [P, 2, KD, P], F32R, at_scr, 4 * 12 * SEQ)
        wg_lo = over("wg_lo", [P, 2, KD, 512], F32R, at_ring)
        u_hi = over("u_hi", [P, 4, SEQ], F32R, at_scr)
        u_lo = over("u_lo", [P, 4, SEQ], F32R, at_u)
        wglu_hi = over("wglu_hi", [P, 8, 4, P], F32R, at_ring, 4 * 2 * CHUNK)
        mix_lo, mix_hi = (over(f"mix_{q}", [P, KD, SEQ], F32R, at_ring, 4 * (4 + r) * CHUNK)
                          for r, q in enumerate(("lo", "hi")))
        wo_raw = [ring[:, c, :].rearrange("p (k n) -> p k n", k=KD) for c in (0, 3)]
        wo_lo = [over(f"wo_lo{r}", [P, KD, 512], F32R, at_ring, 4 * c * CHUNK) for r, c in enumerate((0, 3))]
        wo_hi = [over("wo_hi0", [P, KD, 512], F32R, at_ring, 4 * 2 * CHUNK), over("wo_hi1", [P, KD, 512], F32R, at_u)]
        raw = over("raw", [P, NRAW, PART], F32, at_ring)
        split_at = [(at_ring, 4 * PART * (NRAW + 2 * r)) for r in range(NSPLIT - 1)] + [(at_scr, 0)]
        w_hi = [over(f"w_hi{r}", [P, PART], F32R, *where) for r, where in enumerate(split_at)]
        w_lo = [over(f"w_lo{r}", [P, PART], F32R, where[0], where[1] + 4 * PART) for r, where in enumerate(split_at)]
        x_hi, x_lo = (over(f"x_{q}", [P, KD, BLK], F32R, at_u, 4096 * r) for r, q in enumerate(("hi", "lo")))
        a_hi, a_lo = (over(f"a_{q}", [P, KD, BLK], F32R, at_v, 4096 * r) for r, q in enumerate(("hi", "lo")))
        act_s = far[0:BLK, 0:2, :]
        swg, sig, swl = (qiT[0:BLK, r, :] for r in range(3))
        ysb = far[0:BLK, 2:4, :]

        ps = [ctx.enter_context(nc.psum_tensor(f"ps{i}", [P, 512], F32)) for i in range(8)]

        s_x = [sem(f"x{t}_loaded") for t in range(TT)]
        s_dend = sem("last_vector_steps")
        s_par = [sem(f"params{i}_loaded") for i in range(4)]
        s_small = sem("small_loaded")
        s_lnp = sem("ln_in_params_loaded")
        s_gb1, s_gb2, s_gb3 = sem("ln_in_rows_loaded"), sem("ln1_rows_loaded"), sem("ln2_rows_loaded")
        s_w = [sem(f"weights_loaded{i}") for i in range(2)]
        s_hThi, s_hTlo, s_hTlo_g = sem("hT_upper"), sem("hT_lower_front"), sem("hT_lower_back")
        s_whi, s_wlo = sem("gate_weights_upper"), sem("gate_weights_lower")
        s_uhi, s_ulo, s_gluhi, s_glulo = (sem(x) for x in ("u_upper", "u_lower", "glu_weights_upper",
                                                           "glu_weights_lower"))
        s_wohi, s_wolo, s_mixhi, s_mixlo = (sem(x) for x in ("w_o_upper", "w_o_lower", "mix_upper", "mix_lower"))
        s_w1o = sem("w_o_right_loaded")
        s_wi = sem("w_idx_done")
        s_const = sem("pool_constants")
        s_one = sem("row_space_cleared")
        s_d, s_a, s_g = sem("vector_steps"), sem("scalar_steps"), sem("pool_steps")
        s_xhat, s_rstd, s_var = sem("xhat_ready"), sem("std_ready"), sem("var_ready")
        s_lnT, s_hT = sem("xhat_transposed"), sem("hT_ready")
        s_hrow = sem("h_rows_ready")
        s_tile, s_tile_a, s_tile_v = sem("tile_done"), sem("tile_taken_by_scalar"), sem("tile_taken_by_vector")
        s_dt, s_sc = sem("dt_ready"), sem("sincos_ready")
        s_th, s_prod = sem("theta_ready"), sem("phase_products_ready")
        s_bb, s_bbT, s_bT = sem("b_blocks_ready"), sem("b_transposed"), sem("bT_ready")
        s_cT, s_cblk, s_tau = sem("c_transposed"), sem("c_blocks_ready"), sem("turns_ready")
        s_ph, s_trig, s_phfree, s_rot = sem("phase_ready"), sem("trig_ready"), sem("phase_used"), sem("trig_used")
        s_bu, s_bufree = sem("bu_done"), sem("bu_taken")
        s_st, s_stfree = sem("states_ready"), sem("states_used")
        s_yfree, s_gelu = sem("y_taken"), sem("gelu_done")
        s_dot, s_relu, s_relufree = sem("dots_done"), sem("relu_ready"), sem("relu_used")
        s_masked, s_far0 = sem("scores_masked"), sem("first_tile_distances")
        s_far = sem("distances_ready")
        s_qk, s_lg, s_pr = sem("qk_done"), sem("logits_ready"), sem("probs_ready")
        s_pTp, s_pT, s_pv = sem("probs_transposed"), sem("pT_ready"), sem("pv_done")
        s_on, s_oTp, s_oT = sem("o_normed"), sem("o_transposed"), sem("oT_ready")
        s_mix = sem("mix_ready")
        s_wo, s_wofree = sem("wo_done"), sem("wo_taken")
        s_h1, s_h1T, s_h1e, s_lgt, s_lgfree = (sem("h1_ready"), sem("h1_transposed"), sem("h1T_ready"),
                                               sem("router_done"), sem("router_taken"))
        s_v8, s_ge = sem("top_ready"), sem("gate_exp_ready")
        s_h1row = sem("h1_rows_written")
        s_chosen, s_cnt, s_adr = sem("chosen_ready"), sem("counts_done"), sem("addresses_ready")
        s_scat, s_slots = sem("list_written"), sem("slots_loaded")
        s_pos, s_clr, s_adr_m = sem("places_ready"), sem("further_list_cleared"), sem("further_addresses_ready")
        s_scat_m, s_slots_m = sem("further_list_written"), sem("further_slots_loaded")
        s_bc, s_bs = sem("bias_parts_copied"), sem("bias_rests_ready")
        s_tab = sem("table_ready")
        s_bias, s_b3l, s_b3 = sem("biases_loaded"), sem("bias_parts_ready"), sem("pick_ready")
        s_gat, s_tnow, s_rnow = sem("rows_gathered"), sem("tokens_picked"), sem("rows_picked")
        s_tr, s_thi, s_tlo = sem("moe_transposed"), sem("transposed_upper"), sem("transposed_lower")
        s_raw = [sem(f"part_loaded{i}") for i in range(NRAW)]
        s_hi, s_lo, s_lo_g = sem("upper_parts_ready"), sem("part_split"), sem("part_split_by_pool")
        s_sig, s_act = sem("sigmoid_ready"), sem("act_ready")
        s_g7 = sem("gate_clipped")
        s_cu = sem("turn_done")
        s_ysb, s_yout = sem("y_ready"), sem("pool_stores_done")
        s_yld = [sem(f"y_loaded{t}") for t in range(TT)]
        s_ah1, s_nb, s_nrm = sem("alpha_h1_ready"), sem("last_shift_ready"), sem("last_rows_normed")
        s_oln_v, s_gend = sem("last_tile_out_ready"), sem("last_pool_steps")
        s_oln, s_out = sem("out_ready"), sem("out_written")

        FRONT = [("u", C_U), ("qi", C_QI), ("q", C_Q), ("k", C_K), ("v", C_V)]
        FRONT += [("g", C_G + 512 * i) for i in range(4)]
        FRONT += [("glu", 0), ("glu", 1), ("att", 0), ("wo", 0), ("wo", 1)]
        NFRONT = len(FRONT)

        tiles = []
        for kind, n in (("u", 4), ("qi", 4), ("ki", 1), ("q", 4), ("k", 4), ("v", 4), ("g", 16)):
            tiles += [(kind, i, "a") for i in range(n)]
        for i in range(8):
            tiles += [("gg", i, "a"), ("val", i, "v")]
        for i in range(8):
            tiles += [("at", i, "v")]
        taken, na, nv = [], 0, 0
        for _, _, who in tiles:
            na, nv = na + (who == "a"), nv + (who == "v")
            taken.append((s_tile_a, na) if who == "a" else (s_tile_v, nv))
        first_tile = {}
        for n, (kind, _, _) in enumerate(tiles):
            first_tile.setdefault(kind, n)

        tiles_upto = [4, 8, 13, 17, 21, 25, 29, 33, 37, 45, 53, 61]

        def gates_after(i):
            return {3: 1, HEADS - 1: 3}.get(i % HEADS, 0)

        def gate_weights(g):
            return ring[:, (5 + g // 4) % 2, :].rearrange("p (k n) -> p k n", k=KD)[:, :, P * (g % 4):P * (g % 4) + P]

        def wait_chunk(engine, n):
            count = 0
            for c in range(n % 2, n + 1, 2):
                count += 32 if FRONT[c][0] == "glu" else 16
            engine.wait_ge(s_w[n % 2], count)

        def glu_part(whole, m):
            r, c = 1 - m % 2, P * (m // 2 % 4)
            return whole[:, :, r, c:c + P]

        NQT = [P * (t + 1) for t in range(TT)]
        STEPS = [(t, hh) for t in range(TT) for hh in range(HEADS)]

        def part_of(c, last):
            if c > PARTS:
                return (1, c - PARTS)
            if c <= 9 or last:
                return (0, c)
            return (1, 0) if c == 10 else (0, c - 1)

        def turns(lo, hi, last):
            return range(lo, min(hi, PARTS - 1) + 1) if last else range(lo, hi + 1)

        def wait_split(engine, i, c):
            engine.wait_ge(s_lo, i * PARTS + c + 1)
            if c in BY_POOL:
                engine.wait_ge(s_lo_g, i * len(BY_POOL) + BY_POOL.index(c) + 1)

        ctx.enter_context(nc.allow_non_contiguous_dma(reason="small parameters, one number for each partition"))
        block = ctx.enter_context(nc.Block())

        @block.sync
        def _(sp):
            for t in range(TT):
                sp.dma_start(h[:, t, :], x_v[:, t, :]).then_inc(s_x[t], 16)

            def chunk(n):
                kind, c = FRONT[n]
                dst = ring[:, n % 2, :]
                if n == NFRONT - 1:
                    sp.wait_ge(s_qk, len(STEPS))
                    sp.dma_start(wo_raw[1], w_o[:, :, 512:1024]).then_inc(s_w1o, 16)
                    return
                if n >= 2:
                    sp.wait_ge(s_tile, tiles_upto[n - 2])
                if kind == "glu":
                    d4 = dst.rearrange("p (k r n) -> p k r n", k=4, r=2)
                    for r in range(2):
                        sp.dma_start(d4[:, :, r, :], w_glu[:, :, DM * r + 512 * c:DM * r + 512 * c + 512])\
                            .then_inc(s_w[n % 2], 8 * 2)
                elif kind == "att":
                    sp.dma_start(dst.rearrange("p (k n) -> p k n", k=4), w_att).then_inc(s_w[n % 2], 16)
                else:
                    src = w_o[:, :, 512 * c:512 * c + 512] if kind == "wo" else w_in[:, :, c:c + 512]
                    sp.dma_start(dst.rearrange("p (k n) -> p k n", k=KD), src).then_inc(s_w[n % 2], 16)

            chunk(0)
            sp.dma_start(small[:, :, 0:64], w_in[:, :, C_KI:C_KI + 64]).then_inc(s_small, 16)
            sp.dma_start(small[:, :, 64:136], w_in[:, :, C_KI:C_KI + 72]).then_inc(s_small, 16)
            for n in range(1, NFRONT):
                chunk(n)
            sp.wait_ge(s_mix, 8)
            for r in range(3):
                sp.dma_start(braw_b[NE * r:NE * r + NE, 0:2 * DFF], a["b_up"][0]).then_inc(s_bias, 16)
                sp.dma_start(braw_b[NE * r:NE * r + NE, 2 * DFF:3 * DFF], a["b_down"][0]).then_inc(s_bias, 16)

            def part(c, p, e):
                if p < 8:
                    col = DFF * (p // 2 % 2) + 512 * (p // 4)
                    rows = slice(512 * (p % 2), 512 * (p % 2) + 512)
                    src = a["w_up"][0, bass.ds(e, 1), rows, col:col + 512].rearrange("o (k p) n -> p (o k) n", p=P)
                    dst = raw[:, c % NRAW, :].rearrange("p (k n) -> p k n", k=4)
                else:
                    rows = slice(256 * (p - 8), 256 * (p - 8) + 256)
                    src = a["w_down"][0, bass.ds(e, 1), rows, :].rearrange("o (k p) n -> p (o k) n", p=P)
                    dst = raw[:, c % NRAW, :].rearrange("p (k n) -> p k n", k=2)
                sp.dma_start(dst, src).then_inc(s_raw[c % NRAW], 16)

            sp.wait_ge(s_wo, 2 * TT)
            for p in range(NRAW):
                part(p, p, 0)
            for c in range(NRAW, NRAW + 2):
                sp.wait_ge(s_lo, c - NRAW + 1)
                part(c, c, 0)
            sp.wait_ge(s_scat, 16 * TT * TOPK)
            sp.dma_start(slots[:, 0:NE], first_list.rearrange("(p b) o -> p (b o)", p=BLK)).then_inc(s_slots, 16)
            sp.wait_ge(s_tab, 1)
            final = sp.value_load(etab_i[0:1, NB:NB + 1], min_val=NE - 1, max_val=NB - 2)

            sp.wait_ge(s_gat, 16)

            def load_turns(i, lo, hi, last):
                now = sp.value_load(etab_i[0:1, bass.ds(i, 1)], min_val=0, max_val=NE - 1)
                later = None if last else sp.value_load(etab_i[0:1, bass.ds(i + 1, 1)], min_val=0, max_val=NE - 1)
                for c in turns(lo, hi, last):
                    on, p = part_of(c, last)
                    split = next(x for x in range(c - NRAW, 20) if x not in BY_POOL)
                    sp.wait_ge(s_lo, i * PARTS + split + 1)
                    part(c, p, later if on else now)

            with sp.Fori(0, final) as i:
                load_turns(i, NRAW + 2, PARTS + NRAW + 1, False)
            load_turns(final, NRAW + 2, PARTS - 1, True)
            for t in range(TT):
                if t == 0:
                    out_rows = sp.snap(final * 16 + 32)
                    sp.wait_ge(s_yout, out_rows)
                sp.dma_start(ring[:, t, :], y_rows[P * TOPK * t:P * TOPK * (t + 1), :]
                             .rearrange("(p k) d -> p (k d)", k=TOPK)).then_inc(s_yld[t], 16)
            for t in range(TT):
                if t < TT - 1:
                    sp.wait_ge(s_oln, t + 1)
                else:
                    sp.wait_ge(s_oln_v, 1)
                sp.dma_start(out_v[:, t, :], h[:, t, :]).then_inc(s_out, 16)
            sp.wait_ge(s_out, 16 * TT)

        @block.gpsimd
        def _(pool):
            step = Steps(pool, s_g)
            g = nc.gpsimd
            step(g.memset(ident[:, :], 0.0))
            g.affine_select(out=ident[:, :], in_=ident[:, :], compare_op=ALU.not_equal, fill=1.0, base=0,
                            pattern=[[-1, P]], channel_multiplier=1).then_inc(s_const, 1)
            step(g.iota(tcol_i[:, :], pattern=[[1, SEQ]], base=0, channel_multiplier=0))
            g.tensor_copy(tcol[:, :], tcol_i[:, :]).then_inc(s_const, 1)
            pool.wait_ge(s_const, 2)
            for j in range(SJ):
                if j == 0:
                    pool.wait_ge(s_tau, 1)
                tau = spw[:, 20, j:j + 1]
                f, r = phase[:, j % 2, :], turn[:, 0, :]
                lo = turn[:, 1, :]
                step(g.tensor_scalar(r, tcol[:, :], tau, ROUND, ALU.mult, ALU.add))
                step(g.tensor_scalar(r, r, ROUND, None, ALU.subtract))
                pool.wait_ge(s_prod, 2 * j + 2)
                step(g.tensor_tensor(f, f, r, ALU.subtract))
                step(g.tensor_tensor(f, f, lo, ALU.add))
                g.tensor_scalar(f, f, 0.5 * 0.9999999, -0.5 * 0.9999999, ALU.min, ALU.max).then_inc(s_ph, 1)
            step(g.memset(ones_b[:, :], 1.0))
            step(g.memset(before[:, :], 1.0))
            step(g.affine_select(out=before[:, :], in_=before[:, :], compare_op=ALU.is_gt, fill=0.0, base=0,
                                 pattern=[[1, P]], channel_multiplier=-1))
            step(g.memset(empty[:, :], NOROW))
            g.dma_start(first_list.rearrange("(p b) o -> p (b o)", p=BLK), empty[:, 0:NE]).then_inc(s_yout, 16)
            g.dma_start(more_list.rearrange("(p b) o -> p (b o)", p=BLK), empty[:, NE:]).then_inc(s_clr, 16)
            step(g.iota(code[:, :], pattern=[[P * TOPK, TT], [1, TOPK]], base=0, channel_multiplier=TOPK))
            step(g.memset(eye96[:, :], 0.0))
            for r in range(3):
                step(g.affine_select(out=eye96[:, :], in_=eye96[:, :], compare_op=ALU.not_equal, fill=1.0,
                                     base=-NE * r, pattern=[[-1, NE]], channel_multiplier=1))
            pool.wait_ge(s_gb1, 32)
            pool.wait_ge(s_lnT, KD)
            for t in range(TT):
                step(g.tensor_tensor(h[:, t, :], h[:, t, :], gb[:, 0, :], ALU.mult))
                g.tensor_tensor(h[:, t, :], h[:, t, :], gb[:, 1, :], ALU.add).then_inc(s_hrow, 1)
                pool.wait_ge(s_hrow, t + 1)
            pool.wait_ge(s_far0, 1)
            g.affine_select(out=far[:, 0, :], in_=far[:, 0, :], compare_op=ALU.is_ge, fill=FAR, base=0,
                            pattern=[[-1, SEQ]], channel_multiplier=1).then_inc(s_masked, 1)
            def gate_lo(g_tile):
                pool.wait_ge(s_whi, g_tile + 1)
                w = wg_lo[:, (5 + g_tile // 4) % 2, :, P * (g_tile % 4):P * (g_tile % 4) + P]
                g.tensor_tensor(w, gate_weights(g_tile), wg_hi[:, g_tile % 2], ALU.subtract).then_inc(s_wlo, 1)

            pool.wait_ge(s_wi, 1)
            pool.wait_ge(s_hThi, 1)
            g.tensor_tensor(hT_lo[:, 4:8, :], hT[:, 4:8, :], hT_hi[:, 4:8, :], ALU.subtract).then_inc(s_hTlo_g, 1)
            pool.wait_ge(s_hTlo_g, 1)
            gate_lo(0)
            pool.wait_ge(s_wlo, 1)
            gate_lo(1)
            pool.wait_ge(s_wlo, 2)
            g_tile = 2
            for i in range((TT - 1) * HEADS):
                if i % HEADS == HEADS - 1:
                    t = i // HEADS + 1
                    pool.wait_ge(s_relufree, HEADS * t)
                    g.affine_select(out=score[:, t % 2, P * t:P * t + P], in_=score[:, t % 2, P * t:P * t + P],
                                    compare_op=ALU.is_ge, fill=MASKED, base=0, pattern=[[-1, P]],
                                    channel_multiplier=1).then_inc(s_masked, 1)
                    pool.wait_ge(s_masked, t + 1)
                for _ in range(gates_after(i)):
                    gate_lo(g_tile)
                    pool.wait_ge(s_wlo, g_tile + 1)
                    g_tile += 1
            for g_tile in range(g_tile, 16):
                gate_lo(g_tile)
                pool.wait_ge(s_wlo, g_tile + 1)
            for m in range(16):
                if m % 8 == 0:
                    wait_chunk(pool, 9 + m // 8)
                pool.wait_ge(s_tile, first_tile["gg"] + max(m - 7, 0))
                slot = (9 + m // 8) % 2
                w = glu_part(ring[:, slot, :].rearrange("p (k r n) -> p k r n", k=4, r=2), m)
                g.tensor_copy(wglu_hi[:, m % 8], w).then_inc(s_gluhi, 1)
                pool.wait_ge(s_gluhi, m + 1)
                g.tensor_tensor(glu_part(wg_lo[:, slot].rearrange("p (k r) n -> p k r n", r=2), m), w,
                                wglu_hi[:, m % 8], ALU.subtract).then_inc(s_glulo, 1)
                pool.wait_ge(s_glulo, m + 1)
            for n in range(2 * KD):
                r, k = n // KD, n % KD
                pool.wait_ge(s_wohi, n + 1)
                g.tensor_tensor(wo_lo[r][:, k, :], wo_raw[r][:, k, :], wo_hi[r][:, k, :], ALU.subtract)\
                    .then_inc(s_wolo, 1)
                pool.wait_ge(s_wolo, n + 1)
            third = slice(2 * NE, 3 * NE)
            pool.wait_ge(s_bc, 1)
            g.tensor_tensor(braw_b, braw_b, brem, ALU.subtract).then_inc(s_bs, 1)
            pool.wait_ge(s_bs, 1)
            g.memset(xg[:, :], 0.0).then_inc(s_one, 1)
            pool.wait_ge(s_one, 1)
            def write_first(t):
                pool.wait_ge(s_adr, t + 1)
                for k in range(TOPK):
                    c = TOPK * t + k
                    g.indirect_dma_start(first_list, bass.IndirectOffsetOnAxis(ap=addr_i[:, c:c + 1], axis=0),
                                         code[:, c:c + 1], None, bounds_check=BLK * NE - 1,
                                         oob_is_err=False).then_inc(s_scat, 16)

            pool.wait_ge(s_yout, 16)
            write_first(0)
            pool.wait_ge(s_scat, 16 * TOPK)
            pool.wait_ge(s_bc, 2)
            g.tensor_tensor(braw_b[third, :], braw_b[third, :], brem[third, :], ALU.subtract).then_inc(s_bs, 1)
            pool.wait_ge(s_bs, 2)
            for t in range(1, TT):
                write_first(t)
            pool.wait_ge(s_tab, 1)
            final = pool.value_load(etab_i[0:1, NB:NB + 1], min_val=NE - 1, max_val=NB - 2)
            pool.wait_ge(s_h1row, 16 * TT)
            zero, last_tok, last_row = (pool.alloc_register(x) for x in ("nothing", "last_token", "last_row"))
            pool.reg_mov(zero, 0)

            def gather(i):
                pool.wait_ge(s_tnow, i + 1)
                pool.reg_add(last_tok, zero, SEQ - 1)
                g.indirect_dma_start(xg[:, :], None, h1_rows,
                                     bass.IndirectOffsetOnAxis(ap=tok_now[:, 0:1], axis=0),
                                     bounds_check=last_tok, oob_is_err=False).then_inc(s_gat, 16)

            def rows_out(i):
                pool.wait_ge(s_rnow, i + 1)
                pool.wait_ge(s_ysb, i * 2 + 3)
                pool.reg_add(last_row, zero, SEQ * TOPK - 1)
                g.indirect_dma_start(y_rows, bass.IndirectOffsetOnAxis(ap=row_now[:, 0:1], axis=0),
                                     ysb.rearrange("p a b -> p (a b)"), None, bounds_check=last_row,
                                     oob_is_err=False).then_inc(s_yout, 16)

            def lo_share(i, c):
                pool.wait_ge(s_hi, i * PARTS + c + 1)
                g.tensor_tensor(w_lo[c % NSPLIT][:, PART // 2:], raw[:, c % NRAW, PART // 2:],
                                w_hi[c % NSPLIT][:, PART // 2:], ALU.subtract).then_inc(s_lo_g, 1)

            gather(0)
            pool.wait_ge(s_clr, 16)
            for c in range(MORE_TILES * TOPK):
                if c % TOPK == 0:
                    pool.wait_ge(s_adr_m, c // TOPK + 1)
                g.indirect_dma_start(more_list, bass.IndirectOffsetOnAxis(ap=more_i[:, c:c + 1], axis=0),
                                     code[:, FIRST + c:FIRST + c + 1], None, bounds_check=BLK * BTAIL - 1,
                                     oob_is_err=False).then_inc(s_scat_m, 16)
            pool.wait_ge(s_scat_m, 16 * MORE_TILES * TOPK)
            g.dma_start(slots[:, NE:], more_list.rearrange("(p b) o -> p (b o)", p=BLK)).then_inc(s_slots_m, 16)
            with pool.Fori(0, final) as i:
                pool.wait_ge(s_tr, i * 4 + 2)
                gather(i + 1)
                for c in BY_POOL:
                    lo_share(i, c)
                rows_out(i)
            for c in BY_POOL:
                if c < PARTS:
                    lo_share(final, c)
            rows_out(final)
            pool.wait_ge(s_yout, final * 16 + 32)
            pool.wait_ge(s_gat, final * 16 + 16)
            pool.wait_ge(s_gb3, 32)
            step.sem, step.n = s_gend, 0
            for t in range(TT - 1):
                pool.wait_ge(s_nrm, t + 1)
                step(g.tensor_tensor(h[:, t, :], h[:, t, :], gb[:, 0, :], ALU.mult))
                g.tensor_tensor(h[:, t, :], h[:, t, :], gb[:, 1, :], ALU.add).then_inc(s_oln, 1)

        @block.scalar
        def _(act):
            s = nc.scalar
            step = Steps(act, s_a)
            act.dma_start(sp_in[:, 0, :], a["lam_re"][0].rearrange("(j w) n -> (w n) j", w=2)).then_inc(s_par[0], 16)
            act.dma_start(sp_in[:, 1, :], a["lam_im"][0].rearrange("(j w) n -> (w n) j", w=2)).then_inc(s_par[0], 16)
            for w in range(2):
                src = a["log_dt"].rearrange("o (j w) -> w o j", w=2)[w].partition_broadcast(STATES)
                act.dma_start(sp_in[64 * w:64 * w + 64, 2, :], src.rearrange("p o j -> p (o j)")
                              if len(src.shape) == 3 else src).then_inc(s_par[0], 16)
            act.dma_start(gbc[:, 0, :], a["ln_in_g"].rearrange("(k p) -> p k", p=P)).then_inc(s_lnp, 16)
            act.dma_start(gbc[:, 1, :], a["ln_in_b"].rearrange("(k p) -> p k", p=P)).then_inc(s_lnp, 16)
            for r, nm in enumerate(("b_re", "b_im")):
                act.dma_start(braw[:, r], a[nm][0].rearrange("(j w) n c -> (w n) j c", w=2)).then_inc(s_par[1], 16)
            for t in range(TT):
                act.wait_ge(s_var, t + 1)
                s.activation(rstd[:, 0:1], mv[:, 1:2], ACT.Sqrt, bias=eps[:, 0:1]).then_inc(s_rstd, 1)
            for r, nm in enumerate(("c_re", "c_im")):
                src = a[nm][0].rearrange("(q g) c n -> (g c) q n", q=4)
                for dup in range(2):
                    act.dma_start(craw[:, r, :, 64 * dup:64 * dup + 64], src).then_inc(s_par[2], 16)
            act.dma_start(bgate[:, :], a["b_gate"][0].rearrange("(k p) -> p k", p=P)).then_inc(s_par[3], 16)
            act.dma_start(dskip[:, :], a["d_skip"][0].rearrange("(q g) c -> (g c) q", q=4)).then_inc(s_par[3], 16)
            for r, nm in enumerate(("ln_in_g", "ln_in_b")):
                act.dma_start(gb[:, r, :], a[nm].partition_broadcast(P)).then_inc(s_gb1, 16)
            act.dma_start(w_rt[:, :, :], a["w_router"][0].rearrange("(k p) n -> p k n", p=P)).then_inc(s_par[3], 16)
            act.dma_start(b_rt[:, :], a["b_router"][0].partition_broadcast(P)).then_inc(s_par[3], 16)

            act.wait_ge(s_lnp, 32)
            for k in range(KD):
                act.wait_ge(s_lnT, k + 1)
                s.activation(hT[:, k, :], ps[4 + k % 4][:, :], ACT.Identity, scale=gbc[:, 0, k:k + 1],
                             bias=gbc[:, 1, k:k + 1]).then_inc(s_hT, 1)
            act.wait_ge(s_par[0], 64)
            s.activation(spw[:, 0, :], sp_in[:, 2, :], ACT.Exp).then_inc(s_dt, 1)
            act.wait_ge(s_th, 1)
            s.activation(spw[:, 2, :], spw[:, 1, :], ACT.Exp).then_inc(s_dt, 1)
            act.wait_ge(s_th, 2)
            s.activation(spw[:, 5, :], spw[:, 4, :], ACT.Sin).then_inc(s_sc, 1)
            step(s.activation(spw[:, 6, :], spw[:, 4, :], ACT.Abs))
            s.activation(spw[:, 7, :], spw[:, 6, :], ACT.Sin, scale=-1.0, bias=half_pi[:, 0:1]).then_inc(s_sc, 1)
            def phase_products(j):
                if j >= 1:
                    act.wait_ge(s_ph, j)
                if j >= 2:
                    act.wait_ge(s_phfree, j - 1)
                s.activation(phase[:, j % 2, :], tcol[:, :], ACT.Copy, scale=spw[:, 21, j:j + 1]).then_inc(s_prod, 1)
                s.activation(turn[:, 1, :], tcol[:, :], ACT.Copy, scale=spw[:, 22, j:j + 1]).then_inc(s_prod, 1)

            def trigs(j):
                if j + 1 < SJ:
                    phase_products(j + 1)
                act.wait_ge(s_ph, j + 1)
                if j >= 2:
                    act.wait_ge(s_rot, j - 1)
                s.activation(trig[:, j % 2, 1, :], phase[:, j % 2, :], ACT.Sin, scale=TWO_PI).then_inc(s_trig, 1)
                step(s.activation(trig[:, j % 2, 0, :], phase[:, j % 2, :], ACT.Abs))
                s.activation(trig[:, j % 2, 0, :], trig[:, j % 2, 0, :], ACT.Sin, scale=-TWO_PI,
                             bias=half_pi[:, 0:1]).then_inc(s_phfree, 1)

            def gelu(q):
                act.wait_ge(s_yfree, q + 1)
                s.activation(uT[:, q, :], uT[:, q, :], ACT.Gelu_apprx_tanh).then_inc(s_gelu, 1)

            def relus(n):
                act.wait_ge(s_dot, n + 1)
                if n >= 2:
                    act.wait_ge(s_relufree, n - 1)
                t = 1 + n // HEADS
                s.activation(relu[:, n % 2, 0:NQT[t]], ps[5 + n % 2][:, 0:NQT[t]], ACT.Relu,
                             scale=64.0 ** -0.5).then_inc(s_relu, 1)

            def take(n):
                kind, i, _ = tiles[n]
                act.wait_ge(s_tile, n + 1)
                src = ps[n % 2]
                if kind == "g":
                    ins = s.activation(gate[:, i, :], src[:, :], ACT.Sigmoid, bias=bgate[:, i:i + 1])
                elif kind == "gg":
                    if i >= 2:
                        act.wait_ge(s_tile_v, i - 1)
                    ins = s.activation(glu_t[:, i % 2, :], src[:, :], ACT.Sigmoid)
                elif kind == "ki":
                    ins = s.activation(kiT[:, :], src[:, :], ACT.Copy)
                else:
                    dst = {"u": uT, "qi": qiT, "q": qT, "k": kT, "v": v}[kind]
                    ins = s.activation(dst[:, i, :], src[:, :], ACT.Copy)
                ins.then_inc(s_tile_a, 1)

            n = 0
            while tiles[n][0] == "u":
                take(n)
                n += 1
                if n == 2:
                    for q in range(8):
                        act.wait_ge(s_bbT, q + 1)
                        r, qq = q // 4, q % 4
                        s.activation(bT[:, r, qq, :], ps[4 + q % 4][:, 0:P], ACT.Copy).then_inc(s_bT, 1)
                    act.wait_ge(s_tau, 1)
                    act.wait_ge(s_const, 2)
                    phase_products(0)
            for j in range(SJ):
                trigs(j)
                take(n)
                n += 1
            while tiles[n][0] != "g":
                take(n)
                n += 1
            def gate_hi(g):
                c = 5 + g // 4
                act.wait_ge(s_w[c % 2], 16 * (c // 2 + 1))
                s.activation(wg_hi[:, g % 2], gate_weights(g), ACT.Copy).then_inc(s_whi, 1)

            act.wait_ge(s_far0, 1)
            s.activation(hT_hi[:, :, :], hT, ACT.Copy).then_inc(s_hThi, 1)
            act.wait_ge(s_stfree, SJ)
            gate_hi(0)
            gate_hi(1)
            act.wait_ge(s_par[3], 64)
            g_done = 0
            for i in range(24):
                relus(i)
                for _ in range(gates_after(i)):
                    take(n)
                    n += 1
                    gate_hi(g_done + 2)
                    g_done += 1
            for q in range(4):
                gelu(q)
            while tiles[n][0] == "g":
                take(n)
                n += 1
                if g_done == 13:
                    act.wait_ge(s_far, TT - 1)
                    act.wait_ge(s_gelu, 4)
                    s.activation(u_hi[:, :, :], uT[:, :, :], ACT.Copy).then_inc(s_uhi, 1)
                if g_done + 2 < 16:
                    gate_hi(g_done + 2)
                g_done += 1

            def exps(i):
                t, hh = STEPS[i]
                act.wait_ge(s_lg, i + 1)
                if i >= 2:
                    act.wait_ge(s_pTp, i - 1)
                s.activation(prob[:, i % 2, 0:NQT[t]], logit[:, i % 2, 0:NQT[t]], ACT.Exp, scale=HD ** -0.5,
                             bias=amax[:, i % 2:i % 2 + 1], accum_out=rsum[:, t, hh:hh + 1]).then_inc(s_pr, 1)

            def keep_pT(i):
                t, hh = STEPS[i]
                act.wait_ge(s_pTp, i + 1)
                if i >= 2:
                    act.wait_ge(s_pv, i - 1)
                s.activation(pT[:, i % 2, 0:NQT[t]], ps[7][:, 0:NQT[t]], ACT.Copy).then_inc(s_pT, 1)

            for i in range(len(STEPS) + 2):
                if i < len(STEPS):
                    exps(i)
                if 1 <= i <= len(STEPS):
                    keep_pT(i - 1)
                if i % 4 == 3 and n < first_tile["at"]:
                    take(n)
                    n += 2
                if i >= 2 and STEPS[i - 2][1] == HEADS - 1:
                    t = STEPS[i - 2][0]
                    act.wait_ge(s_oTp, t + 1)
                    s.activation(qiT[:, :, P * t:P * t + P], ps[3][:, :].rearrange("p (k q) -> p k q", k=4),
                                 ACT.Copy).then_inc(s_oT, 1)
            while n < first_tile["at"]:
                take(n)
                n += 2
            act.wait_ge(s_hrow, TT)
            for r, nm in enumerate(("ln1_g", "ln1_b")):
                act.dma_start(gb[:, r, :], a[nm][0].partition_broadcast(P)).then_inc(s_gb2, 16)
            wait_chunk(act, 12)
            for i in range(KD):
                if i == KD // 2:
                    act.wait_ge(s_w1o, 16)
                for n in (2 * i, 2 * i + 1):
                    s.activation(wo_hi[n // KD][:, n % KD, :], wo_raw[n // KD][:, n % KD, :], ACT.Copy)\
                        .then_inc(s_wohi, 1)
                act.wait_ge(s_mix, i + 1)
                s.activation(mix_hi[:, i, :], mixT[:, i, :], ACT.Copy).then_inc(s_mixhi, 1)
            def hi(i, c):
                act.wait_ge(s_raw[c % NRAW], (i * 2 + c // NRAW) * 16 + 16)
                if c >= NSPLIT:
                    act.wait_ge(s_cu, i * PARTS + c - NSPLIT + 1)
                s.activation(w_hi[c % NSPLIT][:, :], raw[:, c % NRAW, :], ACT.Copy).then_inc(s_hi, 1)

            second, third = slice(NE, 2 * NE), slice(2 * NE, 3 * NE)
            act.wait_ge(s_bias, 96)
            step(s.activation(bias3[:, :], braw_b, ACT.Copy))
            s.activation(brem, bias3[:, :], ACT.Copy).then_inc(s_bc, 1)
            for t in range(TT):
                act.wait_ge(s_var, TT + t + 1)
                s.activation(rstd[:, 0:1], mv[:, 1:2], ACT.Sqrt, bias=eps[:, 0:1]).then_inc(s_rstd, 1)
                if t == 1:
                    act.wait_ge(s_bs, 1)
                    step(s.activation(bias3[third, :], braw_b[third, :], ACT.Copy))
                    s.activation(brem[third, :], bias3[third, :], ACT.Copy).then_inc(s_bc, 1)
                if t == 2:
                    step(s.activation(bias3[second, :], braw_b[second, :], ACT.Copy))
                    act.wait_ge(s_bs, 2)
                    s.activation(bias3[third, :], braw_b[third, :], ACT.Copy).then_inc(s_b3l, 1)
                if t == 3:
                    for c in range(3):
                        hi(0, c)
                act.wait_ge(s_h1, t + 1)
                act.dma_start(h1_rows.rearrange("(t p) d -> p t d", p=P)[:, t, :], h[:, t, :]).then_inc(s_h1row, 16)
                for r in range(2):
                    act.wait_ge(s_h1T, 2 * t + r + 1)
                    if t > 0:
                        act.wait_ge(s_lgt, t)
                    s.activation(hT1[:, 4 * r:4 * r + 4, :], ps[6 + r][:, :].rearrange("p (k q) -> p k q", k=4),
                                 ACT.Copy).then_inc(s_h1e, 1)
                act.wait_ge(s_v8, t + 1)
                s.activation(gates[:, t, :], rt8[:, t, 0:TOPK], ACT.Exp, bias=gneg[:, 0:1],
                             accum_out=gsum[:, 0:1]).then_inc(s_ge, 1)
            for r, nm in enumerate(("ln2_g", "ln2_b")):
                act.dma_start(gb[:, r, :], a[nm][0].partition_broadcast(P)).then_inc(s_gb3, 16)
            act.wait_ge(s_h1row, 16 * TT)
            for t in range(TT):
                s.activation(h[:, t, :], h[:, t, :], ACT.Copy, scale=ALPHA).then_inc(s_ah1, 1)
            act.wait_ge(s_tab, 1)
            final = act.value_load(etab_i[0:1, NB:NB + 1], min_val=NE - 1, max_val=NB - 2)

            def T_hi(dst, half, job, bank):
                act.wait_ge(s_tr, job + 1)
                s.activation(dst[:, 4 * half:4 * half + 4, :].rearrange("p k t -> p (k t)"), ps[bank][:, 0:4 * BLK],
                             ACT.Copy).then_inc(s_thi, 1)

            def sigm(i, half):
                act.wait_ge(s_g7, i * 2 + half + 1)
                s.activation(sig, swg, ACT.Sigmoid, scale=SWI).then_inc(s_sig, 1)

            def blk(i, last):
                def his(lo, up):
                    for c in turns(lo, up, last):
                        hi(i, c)
                his(5, 6)
                sigm(i, 0)
                his(7, 9)
                T_hi(a_hi, 0, i * 4 + 2, 6)
                his(10, 10)
                sigm(i, 1)
                if not last:
                    T_hi(x_hi, 0, i * 4 + 3, 7)
                    T_hi(x_hi, 1, i * 4 + 4, 6)
                his(11, 12)
                T_hi(a_hi, 1, i * 4 + 5 - (2 if last else 0), 7)
                his(13, 15)
                act.wait_ge(s_cu, i * PARTS + (12 if last else 13))
                act.wait_ge(s_rnow, i + 1)
                for r in range(2):
                    s.activation(ysb[:, r, :], ps[4 + r][0:BLK, :], ACT.Copy).then_inc(s_ysb, 1)
                his(16, 16)

            act.sem_inc(s_ysb, 1)
            for half in range(2):
                T_hi(x_hi, half, half, 6 + half)
            for c in range(3, 5):
                hi(0, c)
            with act.Fori(0, final) as i:
                blk(i, False)
            blk(final, True)
            for t in range(TT):
                act.wait_ge(s_var, 2 * TT + t + 1)
                s.activation(rstd[:, 0:1], mv[:, 1:2], ACT.Sqrt, bias=eps[:, 0:1]).then_inc(s_rstd, 1)
                act.wait_ge(s_nb, t + 1)
                s.activation(h[:, t, :], h[:, t, :], ACT.Identity, scale=rstd[:, 1:2], bias=gneg[:, 0:1])\
                    .then_inc(s_nrm, 1)

        @block.vector
        def _(dve):
            d = nc.vector
            step = Steps(dve, s_d)
            step(d.memset(eps[:, :], EPS))
            step(d.memset(half_pi[:, :], TWO_PI / 4))

            def norm(row, n, step):
                for r in range(2):
                    step(d.bn_stats(stats[:, r, :], row[:, 512 * r:512 * r + 512]))
                d.bn_aggr(mv[:, :], stats[:, :, :]).then_inc(s_var, 1)
                dve.wait_ge(s_rstd, n)
                step(d.reciprocal(rstd[:, 1:2], rstd[:, 0:1]))
                dve.wait_ge(s_var, n)
                return d.tensor_scalar(row, row, mv[:, 0:1], rstd[:, 1:2], ALU.subtract, ALU.mult)

            for t in range(TT):
                dve.wait_ge(s_x[t], 16)
                norm(h[:, t, :], t + 1, step).then_inc(s_xhat, 1)
                dve.wait_ge(s_xhat, t + 1)
            lr, li = sp_in[:, 0, :], sp_in[:, 1, :]
            W = lambda q: spw[:, q, :]
            dve.wait_ge(s_dt, 1)
            d.tensor_tensor(W(1), lr, W(0), ALU.mult).then_inc(s_th, 1)
            step(d.tensor_tensor(W(3), li, W(0), ALU.mult))
            step(d.tensor_scalar(W(8), W(3), 1.0 / TWO_PI, ROUND, ALU.mult, ALU.add))
            step(d.tensor_scalar(W(8), W(8), ROUND, None, ALU.subtract))
            for c in (PI_C1, PI_C2, PI_C3):
                step(d.scalar_tensor_tensor(W(3), W(8), -c, W(3), ALU.mult, ALU.add))
            d.tensor_scalar(W(4), W(3), PI_SAFE, -PI_SAFE, ALU.min, ALU.max).then_inc(s_th, 1)
            step(d.tensor_scalar(W(20), W(3), 1.0 / TWO_PI, None, ALU.mult))
            step(d.tensor_scalar(W(21), W(20), ROUND14, None, ALU.add))
            step(d.tensor_scalar(W(21), W(21), ROUND14, None, ALU.subtract))
            d.tensor_tensor(W(22), W(20), W(21), ALU.subtract).then_inc(s_tau, 1)
            dve.wait_ge(s_sc, 2)
            step(d.tensor_tensor(W(9), W(2), W(7), ALU.mult))
            step(d.tensor_scalar(W(9), W(9), 1.0, None, ALU.subtract))
            step(d.tensor_tensor(W(10), W(2), W(5), ALU.mult))
            step(d.tensor_tensor(W(11), lr, lr, ALU.mult))
            step(d.tensor_tensor(W(12), li, li, ALU.mult))
            step(d.tensor_tensor(W(11), W(11), W(12), ALU.add))
            step(d.reciprocal(W(11), W(11)))
            for dst, (p0, q0), (p1, q1), op in ((14, (9, lr), (10, li), ALU.add), (15, (10, lr), (9, li), ALU.subtract)):
                step(d.tensor_tensor(W(12), W(p0), q0, ALU.mult))
                step(d.tensor_tensor(W(13), W(p1), q1, ALU.mult))
                step(d.tensor_tensor(W(dst), W(12), W(13), op))
                step(d.tensor_tensor(W(dst), W(dst), W(11), ALU.mult))
            dve.wait_ge(s_par[1], 32)
            cr, ci = (spw[:, q, :].unsqueeze(2).to_broadcast([P, SJ, GROUP]) for q in (14, 15))
            tmp = m[:, 0:2, 0:SJ * GROUP].rearrange("p r (j c) -> p r j c", c=GROUP)
            dve.wait_ge(s_const, 2)
            step(d.memset(bblk[:, :, :, :], 0.0))
            for r, (x0, x1, op) in enumerate(((cr, ci, ALU.subtract), (ci, cr, ALU.add))):
                step(d.tensor_tensor(tmp[:, 0], x0, braw[:, 0], ALU.mult))
                step(d.tensor_tensor(tmp[:, 1], x1, braw[:, 1], ALU.mult))
                for w in range(2):
                    rows = slice(64 * w, 64 * w + 64)
                    ins = d.tensor_tensor(bblk[rows, r, :, GROUP * w:GROUP * w + GROUP], tmp[rows, 0], tmp[rows, 1], op)
                    if r == 1 and w == 1:
                        ins.then_inc(s_bb, 1)
                    else:
                        step(ins)
            step(d.memset(cblk[:, :, :, :], 0.0))
            for r in range(2):
                dve.wait_ge(s_cT, 4 * r + 4)
                src = ps[2 + r][:, :].rearrange("p (j w c) -> p j w c", w=2, c=GROUP)
                for w in range(2):
                    rows = slice(64 * w, 64 * w + 64)
                    ins = d.tensor_scalar(cblk[rows, r, :, GROUP * w:GROUP * w + GROUP], src[rows, :, w, :],
                                          1.0 if r == 0 else -1.0, None, ALU.mult)
                    if (r, w) == (1, 1):
                        ins.then_inc(s_cblk, 1)
                        dve.wait_ge(s_cblk, 1)
                    else:
                        step(ins)

            def s5(j):
                dve.wait_ge(s_bu, j + 1)
                dve.wait_ge(s_phfree, j + 1)
                c, sn = trig[:, j % 2, 0, :], trig[:, j % 2, 1, :]
                br, bi = ps[2], ps[3]
                step(d.tensor_tensor(m[:, 0, :], br[:, :], c, ALU.mult))
                step(d.tensor_tensor(m[:, 1, :], bi[:, :], sn, ALU.mult))
                step(d.tensor_tensor(m[:, 2, :], bi[:, :], c, ALU.mult))
                d.tensor_tensor(m[:, 3, :], br[:, :], sn, ALU.mult).then_inc(s_bufree, 1)
                dve.wait_ge(s_bufree, j + 1)
                step(d.tensor_tensor(m[:, 0, :], m[:, 0, :], m[:, 1, :], ALU.add))
                step(d.tensor_tensor(m[:, 2, :], m[:, 2, :], m[:, 3, :], ALU.subtract))
                decay = spw[:, 2, j:j + 1].to_broadcast([P, SEQ])
                step(d.tensor_tensor_scan(m[:, 1, :], decay, m[:, 0, :], 0.0, ALU.mult, ALU.add))
                step(d.tensor_tensor_scan(m[:, 3, :], decay, m[:, 2, :], 0.0, ALU.mult, ALU.add))
                if j >= 2:
                    dve.wait_ge(s_stfree, j - 1)
                wr, w_im = w_st[:, j % 2, 0, :], w_st[:, j % 2, 1, :]
                step(d.tensor_tensor(m[:, 0, :], m[:, 1, :], c, ALU.mult))
                step(d.tensor_tensor(m[:, 2, :], m[:, 3, :], sn, ALU.mult))
                step(d.tensor_tensor(wr, m[:, 0, :], m[:, 2, :], ALU.subtract))
                step(d.tensor_tensor(m[:, 0, :], m[:, 1, :], sn, ALU.mult))
                d.tensor_tensor(m[:, 2, :], m[:, 3, :], c, ALU.mult).then_inc(s_rot, 1)
                dve.wait_ge(s_rot, j + 1)
                d.tensor_tensor(w_im, m[:, 0, :], m[:, 2, :], ALU.add).then_inc(s_st, 1)
                dve.wait_ge(s_st, j + 1)

            def y_out(q):
                dve.wait_ge(s_stfree, 4 * q + 4)
                if q == 0:
                    dve.wait_ge(s_par[3], 64)
                d.scalar_tensor_tensor(uT[:, q, :], uT[:, q, :], dskip[:, q:q + 1], ps[5 - q % 2][:, :],
                                       ALU.mult, ALU.add).then_inc(s_yfree, 1)

            for j in range(SJ):
                s5(j)
                if j >= 5 and j % 4 == 1:
                    y_out((j - 5) // 4)
            y_out(3)

            step(d.tensor_tensor(m[:, 0, 0:P], ident[:, :], tcol[:, 0:P], ALU.mult))
            step(d.reduce_sum(qpos[:, 0:1], m[:, 0, 0:P], AXL.X))
            for t in range(1, TT):
                step(d.tensor_scalar(qpos[:, t:t + 1], qpos[:, 0:1], float(P * t), None, ALU.add))
            dve.wait_ge(s_bbT, 8)
            d.tensor_scalar(far[:, 0, :], tcol[:, :], -1.0, qpos[:, 0:1], ALU.mult, ALU.add).then_inc(s_far0, 1)
            dve.wait_ge(s_wi, 1)
            dve.wait_ge(s_hThi, 1)
            d.tensor_tensor(hT_lo[:, 0:4, :], hT[:, 0:4, :], hT_hi[:, 0:4, :], ALU.subtract).then_inc(s_hTlo, 1)
            step(d.tensor_scalar(wi[:, :, :], wi_ps(ps), HEADS ** -0.5, None, ALU.mult))
            for t in range(1, TT):
                nk = NQT[t]
                sc = score[:, t % 2, 0:nk]
                for hh in range(HEADS):
                    n = HEADS * (t - 1) + hh
                    dve.wait_ge(s_relu, n + 1)
                    src, wcol = relu[:, n % 2, 0:nk], wi[:, t, hh:hh + 1]
                    if hh == 0:
                        ins = d.tensor_scalar(sc, src, wcol, None, ALU.mult)
                    else:
                        ins = d.scalar_tensor_tensor(sc, src, wcol, sc, ALU.mult, ALU.add)
                    ins.then_inc(s_relufree, 1)
                    dve.wait_ge(s_relufree, n + 1)
                dve.wait_ge(s_masked, t + 1)
                for _ in range(NSEL // 8):
                    step(d.max(top8[:, :], sc))
                    step(d.match_replace(sc, top8[:, :], sc, TAKEN))
                step(d.tensor_scalar(far[:, t, 0:nk], sc, TAKEN, FAR, ALU.not_equal, ALU.mult))
                d.scalar_tensor_tensor(far[:, t, 0:nk], far[:, t, 0:nk], qpos[:, t:t + 1], tcol[:, 0:nk],
                                       ALU.add, ALU.subtract).then_inc(s_far, 1)
                dve.wait_ge(s_far, t)
            dve.wait_ge(s_masked, 1)
            dve.wait_ge(s_uhi, 1)
            d.tensor_tensor(u_lo[:, :, :], uT[:, :, :], u_hi[:, :, :], ALU.subtract).then_inc(s_ulo, 1)

            def logits(i):
                t, hh = STEPS[i]
                nk = NQT[t]
                dve.wait_ge(s_qk, i + 1)
                if i >= 2:
                    dve.wait_ge(s_pr, i - 1)
                lgt = logit[:, i % 2, 0:nk]
                step(d.scalar_tensor_tensor(lgt, far[:, t, 0:nk], -SLOPES[hh] * HD ** 0.5, ps[5 + i % 2][:, 0:nk],
                                            ALU.mult, ALU.add))
                step(d.reduce_max(top8[:, 0:1], lgt, AXL.X))
                d.tensor_scalar(amax[:, i % 2:i % 2 + 1], top8[:, 0:1], -HD ** -0.5, None, ALU.mult).then_inc(s_lg, 1)
                dve.wait_ge(s_lg, i + 1)

            def value(i):
                n = first_tile["gg"] + 2 * i + 1
                dve.wait_ge(s_tile, n + 1)
                dve.wait_ge(s_tile_a, taken[n - 1][1])
                d.tensor_tensor(glu_t[:, i % 2, :], glu_t[:, i % 2, :], ps[n % 2][:, :], ALU.mult).then_inc(s_tile_v, 1)
                dve.wait_ge(s_tile_v, i + 1)
                step(d.tensor_tensor(gate[:, i, :], gate[:, i, :], glu_t[:, i % 2, :], ALU.mult))

            for i in range(len(STEPS) + 2):
                if i < len(STEPS):
                    logits(i)
                if i % 4 == 1 and i > 1:
                    value(i // 4 - 1)
                if i >= 2 and STEPS[i - 2][1] == HEADS - 1:
                    t = STEPS[i - 2][0]
                    dve.wait_ge(s_pv, i - 1)
                    dve.wait_ge(s_pr, i - 1)
                    step(d.reciprocal(rinv[:, :], rsum[:, t, :]))
                    if t > 0:
                        dve.wait_ge(s_oTp, t)
                    d.tensor_tensor(oq.rearrange("p o (h e) -> p (o h) e", h=HEADS),
                                    ps[2][:, :].rearrange("p (h e) -> p h e", h=HEADS),
                                    rinv[:, :].unsqueeze(2).to_broadcast([P, HEADS, HD]), ALU.mult).then_inc(s_on, 1)
                    dve.wait_ge(s_on, t + 1)
            def mix_lower(i):
                dve.wait_ge(s_mixhi, i + 1)
                d.tensor_tensor(mix_lo[:, i, :], mixT[:, i, :], mix_hi[:, i, :], ALU.subtract).then_inc(s_mixlo, 1)

            for i in range(8):
                n = first_tile["at"] + i
                dve.wait_ge(s_tile, n + 1)
                d.tensor_tensor(mix_t[:, 0, :], gate[:, 8 + i, :], ps[n % 2][:, :], ALU.mult).then_inc(s_tile_v, 1)
                dve.wait_ge(s_tile_v, 8 + i + 1)
                d.tensor_tensor(mixT[:, i, :], gate[:, i, :], mix_t[:, 0, :], ALU.add).then_inc(s_mix, 1)
                dve.wait_ge(s_mix, i + 1)
                if i > 0:
                    mix_lower(i - 1)
            mix_lower(KD - 1)
            def first_addresses(t):
                dve.wait_ge(s_pos, t + 1)
                step(d.tensor_copy(pos[:, t, :], ps[1][:, 0:NE]))
                ad, picked = adw[:, t, 0, :], adw[:, t, 1, :]
                step(d.scalar_tensor_tensor(ad, pos[:, t, :], float(NE), tcol[:, 0:NE], ALU.mult, ALU.add))
                for k in range(TOPK):
                    step(d.scalar_tensor_tensor(picked, tcol[:, 0:NE], rif[:, t, k:k + 1], ad, ALU.is_equal, ALU.mult,
                                                accum_out=addr[:, t, k:k + 1]))
                d.tensor_copy(addr_i[:, TOPK * t:TOPK * t + TOPK], addr[:, t, :]).then_inc(s_adr, 1)
                dve.wait_ge(s_adr, t + 1)

            def lo(i, c):
                dve.wait_ge(s_hi, i * PARTS + c + 1)
                n = PART // 2 if c in BY_POOL else PART
                if c - 1 in BY_POOL and n == PART:
                    dve.wait_ge(s_lo_g, i * len(BY_POOL) + BY_POOL.index(c - 1) + 1)
                d.tensor_tensor(w_lo[c % NSPLIT][:, 0:n], raw[:, c % NRAW, 0:n], w_hi[c % NSPLIT][:, 0:n],
                                ALU.subtract).then_inc(s_lo, 1)

            dve.wait_ge(s_hrow, TT)
            dve.wait_ge(s_gb2, 32)
            for t in range(TT):
                for r in range(2):
                    n = 2 * t + r
                    dve.wait_ge(s_wo, n + 1)
                    d.scalar_tensor_tensor(h[:, t, 512 * r:512 * r + 512], h[:, t, 512 * r:512 * r + 512], ALPHA,
                                           ps[2 + n % 4][:, :], ALU.mult, ALU.add).then_inc(s_wofree, 1)
                    dve.wait_ge(s_wofree, n + 1)
                step(norm(h[:, t, :], TT + t + 1, step))
                step(d.tensor_tensor(h[:, t, :], h[:, t, :], gb[:, 0, :], ALU.mult))
                d.tensor_tensor(h[:, t, :], h[:, t, :], gb[:, 1, :], ALU.add).then_inc(s_h1, 1)
                if t > 0:
                    first_addresses(t - 1)
                if t == TT - 1:
                    for c in range(2):
                        lo(0, c)
                dve.wait_ge(s_lgt, t + 1)
                d.tensor_tensor(lg[:, :], b_rt[:, :], ps[0][:, 0:NE], ALU.add).then_inc(s_lgfree, 1)
                dve.wait_ge(s_lgfree, t + 1)
                step(d.max(rt8[:, t, :], lg[:, :]))
                step(d.max_index(ri8[:, t, :], rt8[:, t, :], lg[:, :]))
                d.tensor_scalar(gneg[:, :], rt8[:, t, 0:1], -1.0, None, ALU.mult).then_inc(s_v8, 1)
                step(d.tensor_copy(rif[:, t, :], ri8[:, t, :]))
                step(d.tensor_scalar(chosen[:, t, :], tcol[:, 0:NE], rif[:, t, 0:1], None, ALU.is_equal))
                for k in range(1, TOPK):
                    step(d.scalar_tensor_tensor(chosen[:, t, :], tcol[:, 0:NE], rif[:, t, k:k + 1], chosen[:, t, :],
                                                ALU.is_equal, ALU.add))
                d.tensor_copy(chosen_b[:, t, :], chosen[:, t, :]).then_inc(s_chosen, 1)
                dve.wait_ge(s_ge, t + 1)
                step(d.reciprocal(gsum[:, 1:2], gsum[:, 0:1]))
                step(d.tensor_scalar(gates[:, t, :], gates[:, t, :], gsum[:, 1:2], None, ALU.mult))
            first_addresses(TT - 1)
            dve.wait_ge(s_cnt, 1)
            cnt, more, upto_e, t0 = rw[:, 0, :], rw[:, 1, :], rw[:, 2, :], rw[:, 3, :]
            step(d.tensor_copy(cnt, ps[2][:, 0:NE]))
            step(d.tensor_scalar(more, cnt, float(BLK), None, ALU.is_gt))
            for b in MORE[1:]:
                step(d.scalar_tensor_tensor(more, cnt, float(BLK * b), more, ALU.is_gt, ALU.add))
            step(d.memset(t0, 1.0))
            step(d.tensor_tensor_scan(upto_e, t0, more, 0.0, ALU.mult, ALU.add))
            step(d.tensor_copy(etab[0:1, 0:NE], tcol[0:1, 0:NE]))
            step(d.tensor_tensor(xcmp[:, :, :], upto_e[0:1, :].unsqueeze(1).to_broadcast([1, BTAIL, NE]),
                                 tcol[0:1, 0:BTAIL].unsqueeze(2).to_broadcast([1, BTAIL, NE]), ALU.is_le))
            step(d.reduce_sum(etab[0:1, NE:NB], xcmp[:, :, :], AXL.X))
            step(d.tensor_scalar(etab[0:1, NE:NB], etab[0:1, NE:NB], float(NE - 1), None, ALU.min))
            step(d.tensor_scalar(etab[0:1, NB:NB + 1], upto_e[0:1, NE - 1:NE], float(NE - 1), None, ALU.add))
            d.tensor_copy(etab_i[:, :], etab[:, :]).then_inc(s_tab, 1)
            dve.wait_ge(s_tab, 1)
            step(d.tensor_tensor(t0, upto_e, more, ALU.subtract))
            step(d.tensor_scalar(t0, t0, 1.0, None, ALU.subtract))

            def more_addresses(t):
                ad, f = adw[:, t, 0, :], fw[:, t, :]
                step(d.tensor_scalar(f, pos[:, t, :], float(BLK), None, ALU.is_ge))
                for b in [b for b in MORE[1:] if b * BLK < (t + 1) * P]:
                    step(d.scalar_tensor_tensor(f, pos[:, t, :], float(BLK * b), f, ALU.is_ge, ALU.add))
                step(d.tensor_tensor(ad, t0, f, ALU.add))
                step(d.scalar_tensor_tensor(pos[:, t, :], f, -float(BLK), pos[:, t, :], ALU.mult, ALU.add))
                step(d.scalar_tensor_tensor(ad, pos[:, t, :], float(BTAIL), ad, ALU.mult, ALU.add))
                step(d.tensor_scalar(f, f, 0.5, float(2 * BLK * NB), ALU.is_lt, ALU.mult))
                step(d.tensor_tensor(ad, ad, f, ALU.add))
                for k in range(TOPK):
                    step(d.scalar_tensor_tensor(adw[:, t, 1, :], tcol[:, 0:NE], rif[:, t, k:k + 1], ad, ALU.is_equal,
                                                ALU.mult, accum_out=addr[:, t, k:k + 1]))
                m0 = TOPK * t - FIRST
                d.tensor_copy(more_i[:, m0:m0 + TOPK], addr[:, t, :]).then_inc(s_adr_m, 1)

            for t in range(TT - MORE_TILES, 2):
                more_addresses(t)

            def pick_expert(i):
                e = 0 if isinstance(i, int) else dve.value_load(etab_i[0:1, bass.ds(i, 1)], min_val=0, max_val=NE - 1)
                d.tensor_copy(pick[:, :], eye96[:, bass.ds(e, 1)].to_broadcast([96, BLK])).then_inc(s_b3, 1)

            dve.wait_ge(s_slots, 16)
            dve.wait_ge(s_h1row, 16 * TT)
            d.tensor_scalar(tok_now[:, :], slots[:, 0:1], 2, None, ALU.arith_shift_right).then_inc(s_tnow, 1)
            lo(0, 2)
            final = dve.value_load(etab_i[0:1, NB:NB + 1], min_val=NE - 1, max_val=NB - 2)

            def T_lo(dst, upper, half, job, bank):
                dve.wait_ge(s_thi, job + 1)
                four = lambda x: x[:, 4 * half:4 * half + 4, :].rearrange("p k t -> p (k t)")
                d.tensor_tensor(four(dst), ps[bank][:, 0:4 * BLK], four(upper), ALU.subtract).then_inc(s_tlo, 1)

            def swiglu(i, half):
                n = i * 2 + half
                G, L = ps[2 * half][0:BLK, :], ps[2 * half + 1][0:BLK, :]
                dve.wait_ge(s_cu, i * PARTS + 4 * half + 4)
                d.tensor_scalar(swg, G, LIMIT, None, ALU.min).then_inc(s_g7, 1)
                step(d.tensor_scalar(swl, L, LIMIT, -LIMIT, ALU.min, ALU.max))
                dve.wait_ge(s_sig, n + 1)
                step(d.tensor_tensor(swg, swg, sig, ALU.mult))
                d.scalar_tensor_tensor(act_s[:, half, :], swl, 1.0, swg, ALU.add, ALU.mult).then_inc(s_act, 1)
                dve.wait_ge(s_act, n + 1)

            def blk(i, last):
                def los(first, up):
                    for c in turns(first, up, last):
                        lo(i, c)
                if not last:
                    dve.wait_ge(s_gat, i * 16 + 16)
                    nx = i + 1
                    step(d.tensor_copy(slot_now[:, :], slots[:, bass.ds(nx, 1)]))
                    d.tensor_scalar(tok_now[:, :], slot_now[:, :], 2, None, ALU.arith_shift_right).then_inc(s_tnow, 1)
                los(5, 6)
                swiglu(i, 0)
                los(7, 9)
                T_lo(a_lo, a_hi, 0, i * 4 + 2, 6)
                los(10, 10)
                swiglu(i, 1)
                if not last:
                    T_lo(x_lo, x_hi, 0, i * 4 + 3, 7)
                    T_lo(x_lo, x_hi, 1, i * 4 + 4, 6)
                    dve.wait_ge(s_cu, i * PARTS + 8)
                    pick_expert(i + 1)
                los(11, 12)
                T_lo(a_lo, a_hi, 1, i * 4 + 5 - (2 if last else 0), 7)
                dve.wait_ge(s_yout, i * 16 + 16)
                d.tensor_copy(row_now[:, :], slots[:, bass.ds(i, 1)]).then_inc(s_rnow, 1)
                dve.wait_ge(s_slots_m, 16)
                los(13, 16)

            for half in range(2):
                T_lo(x_lo, x_hi, half, half, 6 + half)
            pick_expert(0)
            more_addresses(2)
            lo(0, 3)
            more_addresses(3)
            lo(0, 4)
            before_loop = step.n
            PER = 5
            with dve.Fori(0, final) as i:
                step.base, step.n = before_loop + i * PER, 0
                blk(i, False)
                assert step.n == PER
            step.base, step.n = before_loop + final * PER, 0
            blk(final, True)
            step = Steps(dve, s_dend)
            dve.wait_ge(s_gb3, 32)
            dve.wait_ge(s_ah1, TT)
            for t in range(TT):
                dve.wait_ge(s_yld[t], 16)
                for k in range(TOPK):
                    step(d.scalar_tensor_tensor(h[:, t, :], ring[:, t, DM * k:DM * k + DM], gates[:, t, k:k + 1],
                                                h[:, t, :], ALU.mult, ALU.add))
                for r in range(2):
                    step(d.bn_stats(stats[:, r, :], h[:, t, 512 * r:512 * r + 512]))
                if t > 0:
                    dve.wait_ge(s_nrm, t)
                d.bn_aggr(mv[:, :], stats[:, :, :]).then_inc(s_var, 1)
                dve.wait_ge(s_rstd, 2 * TT + t + 1)
                step(d.reciprocal(rstd[:, 1:2], rstd[:, 0:1]))
                d.scalar_tensor_tensor(gneg[:, :], mv[:, 0:1], -1.0, rstd[:, 1:2], ALU.mult, ALU.mult).then_inc(s_nb, 1)
            dve.wait_ge(s_nrm, TT)
            step(d.tensor_tensor(h[:, TT - 1, :], h[:, TT - 1, :], gb[:, 0, :], ALU.mult))
            d.tensor_tensor(h[:, TT - 1, :], h[:, TT - 1, :], gb[:, 1, :], ALU.add).then_inc(s_oln_v, 1)

        @block.tensor
        def _(pe):
            mm, tr = nc.tensor.matmul, nc.tensor.transpose
            pe.wait_ge(s_const, 1)
            for k in range(KD):
                if k >= 4:
                    pe.wait_ge(s_hT, k - 3)
                for t in range(TT):
                    if k == 0:
                        pe.wait_ge(s_xhat, t + 1)
                    ins = tr(ps[4 + k % 4][:, P * t:P * t + P], h[:, t, P * k:P * k + P], ident[:, :])
                ins.then_inc(s_lnT, 1)
            pe.wait_ge(s_hT, KD)

            def arrive(n):
                wait_chunk(pe, n)

            def tile(n, chunk_n, last=False):
                kind, i, _ = tiles[n]
                if n >= 2:
                    pe.wait_ge(*taken[n - 2])
                o = ps[n % 2]
                w = ring[:, chunk_n % 2, :]
                if kind == "ki":
                    for k in range(KD):
                        ins = mm(o[:, :], small[:, k, 0:P], hT[:, k, :], start=k == 0, stop=k == KD - 1)
                elif kind == "v":
                    w = w.rearrange("p (k n) -> p k n", k=KD)
                    for k in range(KD):
                        ins = mm(o[:, :], hT[:, k, P * i:P * i + P], w[:, k, :], start=k == 0, stop=k == KD - 1)
                elif kind in ("gg", "val"):
                    m = n - first_tile["gg"]
                    if m == 0:
                        pe.wait_ge(s_ulo, 1)
                    pe.wait_ge(s_glulo, m + 1)
                    w_lower = glu_part(wg_lo[:, chunk_n % 2].rearrange("p (k r) n -> p k r n", r=2), m)
                    for k in range(4):
                        mm(o[:, :], wglu_hi[:, m % 8, k, :], u_hi[:, k, :], start=k == 0, stop=False)
                        mm(o[:, :], wglu_hi[:, m % 8, k, :], u_lo[:, k, :], start=False, stop=False)
                        ins = mm(o[:, :], w_lower[:, k, :], u_hi[:, k, :], start=False, stop=k == 3)
                elif kind == "at":
                    w = w.rearrange("p (k n) -> p k n", k=4)
                    for k in range(4):
                        ins = mm(o[:, :], w[:, k, P * i:P * i + P], qiT[:, k, :], start=k == 0, stop=k == 3)
                else:
                    w = w.rearrange("p (k n) -> p k n", k=KD)
                    c = P * (i % 4)
                    for k in range(KD):
                        ins = mm(o[:, :], w[:, k, c:c + P], hT[:, k, :], start=k == 0, stop=k == KD - 1)
                ins.then_inc(s_tile, 1)

            arrive(0)
            n = 0
            for i in range(4):
                tile(n, 0)
                n += 1
                if i == 1:
                    pe.wait_ge(s_par[2], 64)
                    for r in range(2):
                        for q in range(4):
                            tr(ps[2 + r][:, P * q:P * q + P], craw[:, r, q, :], ident[:, :]).then_inc(s_cT, 1)
                    pe.wait_ge(s_bb, 1)
                    for q in range(8):
                        r, qq = q // 4, q % 4
                        if q >= 4:
                            pe.wait_ge(s_bT, q - 3)
                        tr(ps[4 + q % 4][:, 0:P], bblk[:, r, 4 * qq:4 * qq + 4, :].rearrange("p j c -> p (j c)"),
                           ident[:, :])\
                            .then_inc(s_bbT, 1)

            pe.wait_ge(*taken[n - 1])
            pe.wait_ge(s_bT, 8)
            pe.wait_ge(s_cblk, 1)

            def bu(j):
                rows = slice(32 * (j % 4), 32 * (j % 4) + 32)
                if j >= 1:
                    pe.wait_ge(s_bufree, j)
                for r in range(2):
                    ins = mm(ps[2 + r][:, :], bT[rows, r, j // 4, :], uT[rows, j // 4, :], start=True, stop=True)
                ins.then_inc(s_bu, 1)

            def ymm(j):
                q, rows = j // 4, slice(32 * (j % 4), 32 * (j % 4) + 32)
                pe.wait_ge(s_st, j + 1)
                if j % 4 == 0 and q > 1:
                    pe.wait_ge(s_yfree, q - 1)
                for r in range(2):
                    ins = mm(ps[5 - q % 2][rows, :], cblk[:, r, j, :], w_st[:, j % 2, r, :], start=r == 0, stop=r == 1)
                ins.then_inc(s_stfree, 1)

            order = [(1, 4), ("small", 1), (2, 4), (3, 4), (4, 4)]
            flat = [(c, i == cnt - 1) for c, cnt in order for i in range(cnt)]
            for j, (c, last) in enumerate(flat):
                if j < SJ:
                    bu(j)
                if c == "small":
                    pe.wait_ge(s_small, 32)
                elif c != (flat[j - 1][0] if j else None):
                    arrive(c)
                tile(n, c if c != "small" else 0)
                n += 1
                if 1 <= j <= SJ:
                    ymm(j - 1)
            for t in range(TT):
                for k in range(KD):
                    ins = mm(ps[7][:, HEADS * t:HEADS * t + HEADS], hT[:, k, P * t:P * t + P], small[:, k, P:P + HEADS],
                             start=k == 0, stop=k == KD - 1)
            ins.then_inc(s_wi, 1)
            def gate_tile(n):
                g = n - first_tile["g"]
                pe.wait_ge(*taken[n - 2])
                if g == 0:
                    pe.wait_ge(s_hTlo, 1)
                    pe.wait_ge(s_hTlo_g, 1)
                pe.wait_ge(s_wlo, g + 1)
                w_lo_g = wg_lo[:, (5 + g // 4) % 2, :, P * (g % 4):P * (g % 4) + P]
                for k in range(KD):
                    mm(ps[n % 2][:, :], wg_hi[:, g % 2, k, :], hT_hi[:, k, :], start=k == 0, stop=False)
                    mm(ps[n % 2][:, :], wg_hi[:, g % 2, k, :], hT_lo[:, k, :], start=False, stop=False)
                    ins = mm(ps[n % 2][:, :], w_lo_g[:, k, :], hT_hi[:, k, :], start=False, stop=k == KD - 1)
                ins.then_inc(s_tile, 1)

            pe.wait_ge(*taken[n - 1])
            for i in range(24):
                t, hh = 1 + i // HEADS, i % HEADS
                rows = slice(64 * (hh % 2), 64 * (hh % 2) + 64)
                if i == 0:
                    pe.wait_ge(s_yfree, 3)
                if i >= 2:
                    pe.wait_ge(s_relu, i - 1)
                mm(ps[5 + i % 2][:, 0:NQT[t]], qiT[rows, hh // 2, P * t:P * t + P], kiT[rows, 0:NQT[t]], start=True,
                   stop=True).then_inc(s_dot, 1)
                for _ in range(gates_after(i)):
                    gate_tile(n)
                    n += 1
            while n < first_tile["gg"]:
                gate_tile(n)
                n += 1

            def qk(i):
                t, hh = STEPS[i]
                rows = slice(64 * (hh % 2), 64 * (hh % 2) + 64)
                if i == 0:
                    pe.wait_ge(s_relu, 24)
                if i >= 2:
                    pe.wait_ge(s_lg, i - 1)
                mm(ps[5 + i % 2][:, 0:NQT[t]], qT[rows, hh // 2, P * t:P * t + P], kT[rows, hh // 2, 0:NQT[t]],
                   start=True, stop=True).then_inc(s_qk, 1)

            def probsT(i):
                t, hh = STEPS[i]
                pe.wait_ge(s_pr, i + 1)
                if i >= 1:
                    pe.wait_ge(s_pT, i)
                for c in range(t + 1):
                    ins = tr(ps[7][:, P * c:P * c + P], prob[:, i % 2, P * c:P * c + P], ident[:, :])
                ins.then_inc(s_pTp, 1)
                return ins

            def pv(i):
                t, hh = STEPS[i]
                pe.wait_ge(s_pT, i + 1)
                if hh == 0 and t > 0:
                    pe.wait_ge(s_on, t)
                for c in range(t + 1):
                    ins = mm(ps[2][:, HD * hh:HD * hh + HD], pT[:, i % 2, P * c:P * c + P],
                             v[:, c, HD * hh:HD * hh + HD], start=c == 0, stop=c == t)
                ins.then_inc(s_pv, 1)

            def o_T(t):
                pe.wait_ge(s_on, t + 1)
                if t > 0:
                    pe.wait_ge(s_oT, t)
                for k in range(4):
                    ins = tr(ps[3][:, P * k:P * k + P], scr[:, 12, P * k:P * k + P], ident[:, :])
                ins.then_inc(s_oTp, 1)

            pe.wait_ge(s_gelu, 4)
            pe.wait_ge(s_far, TT - 1)
            pe.wait_ge(s_st, SJ)
            for i in range(len(STEPS) + 3):
                if i < len(STEPS):
                    qk(i)
                if i % 2 == 0 and i > 0 and n < first_tile["at"]:
                    tile(n, 9 + (n - first_tile["gg"]) // 8)
                    n += 1
                if 1 <= i <= len(STEPS):
                    probsT(i - 1)
                if 2 <= i <= len(STEPS) + 1:
                    pv(i - 2)
                if i >= 3 and STEPS[i - 3][1] == HEADS - 1:
                    o_T(STEPS[i - 3][0])
            pe.wait_ge(s_oT, TT)
            arrive(11)
            for i in range(8):
                tile(n, 11)
                n += 1

            def w_out(t):
                for r in range(2):
                    i = 2 * t + r
                    if i >= 4:
                        pe.wait_ge(s_wofree, i - 3)
                    for k in range(KD):
                        if i == 0:
                            pe.wait_ge(s_mixlo, k + 1)
                        if t == 0:
                            pe.wait_ge(s_wolo, KD * r + k + 1)
                        x, o = slice(P * t, P * t + P), ps[2 + i % 4]
                        mm(o[:, :], mix_hi[:, k, x], wo_hi[r][:, k, :], start=k == 0, stop=False)
                        mm(o[:, :], mix_hi[:, k, x], wo_lo[r][:, k, :], start=False, stop=False)
                        ins = mm(o[:, :], mix_lo[:, k, x], wo_hi[r][:, k, :], start=False, stop=k == KD - 1)
                    ins.then_inc(s_wo, 1)

            def route(t):
                pe.wait_ge(s_h1, t + 1)
                for r in range(2):
                    if t > 0:
                        pe.wait_ge(s_h1e, 2 * t)
                    for k in range(4):
                        ins = tr(ps[6 + r][:, P * k:P * k + P], h[:, t, 512 * r + P * k:512 * r + P * k + P],
                                 ident[:, :])
                    ins.then_inc(s_h1T, 1)
                pe.wait_ge(s_h1e, 2 * t + 2)
                if t > 0:
                    pe.wait_ge(s_lgfree, t)
                for k in range(KD):
                    ins = mm(ps[0][:, 0:NE], hT1[:, k, :], w_rt[:, k, :], start=k == 0, stop=k == KD - 1)
                ins.then_inc(s_lgt, 1)

            pe.wait_ge(s_par[3], 64)
            def place(t):
                pe.wait_ge(s_chosen, t + 1)
                if t > 0:
                    pe.wait_ge(s_adr, t)
                for b in range(t + 1):
                    ins = mm(ps[1][:, 0:NE], before[:, :] if b == t else ones_b[:, :], chosen_b[:, b, :],
                             start=b == 0, stop=b == t)
                ins.then_inc(s_pos, 1)

            for t in range(TT):
                w_out(t)
                if t > 1:
                    place(t - 2)
                if t > 0:
                    route(t - 1)
            place(TT - 2)
            route(TT - 1)
            place(TT - 1)
            for b in range(TT):
                ins = mm(ps[2][:, 0:NE], ones_b[:, :], chosen_b[:, b, :], start=b == 0, stop=b == TT - 1)
            ins.then_inc(s_cnt, 1)

            pe.wait_ge(s_tab, 1)
            final = pe.value_load(etab_i[0:1, NB:NB + 1], min_val=NE - 1, max_val=NB - 2)

            def T4(src, job, bank):
                pe.wait_ge(s_tlo, job - 1)
                for k in range(4):
                    ins = tr(ps[bank][:, BLK * k:BLK * k + BLK], src[:, P * k:P * k + P], ident[0:BLK, 0:BLK])
                ins.then_inc(s_tr, 1)

            def product(o, xh, xl, c, w, stop):
                col = slice(w, w + 512)
                mm(o, xh, w_hi[c % NSPLIT][:, col], start=False, stop=False)
                mm(o, xl, w_hi[c % NSPLIT][:, col], start=False, stop=False)
                return mm(o, xh, w_lo[c % NSPLIT][:, col], start=False, stop=stop)

            def turn_products(i, c, p):
                if p < 8 and p % 2 == 0:
                    col = DFF * (p // 2 % 2) + 512 * (p // 4)
                    mm(ps[p // 2][0:BLK, :], pick[:, :], bias3[:, col:col + 512], start=True, stop=False)
                wait_split(pe, i, c)
                for k in range(4):
                    if p < 8:
                        kk = 4 * (p % 2) + k
                        ins = product(ps[p // 2][0:BLK, :], x_hi[:, kk, :], x_lo[:, kk, :], c, 512 * k, kk == KD - 1)
                    else:
                        kk, r = 2 * (p - 8) + k // 2, k % 2
                        ins = product(ps[4 + r][0:BLK, :], a_hi[:, kk, :], a_lo[:, kk, :], c, 512 * k, kk == KD - 1)
                ins.then_inc(s_cu, 1)

            def blk(i, last):
                A1 = i * 4 + (3 if last else 5)
                for c in turns(1, PARTS, last):
                    on, p = part_of(c, last)
                    if c == 7:
                        pe.wait_ge(s_ysb, i * 2 + 1)
                        for r in range(2):
                            mm(ps[4 + r][0:BLK, :], pick[:, :], bias3[:, 2 * DFF + 512 * r:2 * DFF + 512 * r + 512],
                               start=True, stop=False)
                    if c == 8:
                        if not last:
                            pe.wait_ge(s_gat, i * 16 + 32)
                            T4(xg[:, 0:512], i * 4 + 3, 7)
                            T4(xg[:, 512:1024], i * 4 + 4, 6)
                        pe.wait_ge(s_tlo, i * 4 + 3)
                    if c == 10:
                        pe.wait_ge(s_act, i * 2 + 2)
                        T4(act_s[:, 1, :], A1, 7)
                        if not last:
                            pe.wait_ge(s_tlo, i * 4 + 5)
                            pe.wait_ge(s_b3, i + 2)
                    if p == 10:
                        pe.wait_ge(s_tlo, A1 + 1)
                    turn_products(i, c, p)
                    if c == 5:
                        pe.wait_ge(s_act, i * 2 + 1)
                        T4(act_s[:, 0, :], i * 4 + 2, 6)

            pe.wait_ge(s_gat, 16)
            for half in range(2):
                for k in range(4):
                    c = 512 * half + P * k
                    ins = tr(ps[6 + half][:, BLK * k:BLK * k + BLK], xg[:, c:c + P], ident[0:BLK, 0:BLK])
                ins.then_inc(s_tr, 1)
            pe.wait_ge(s_tlo, 2)
            pe.wait_ge(s_b3, 1)
            pe.wait_ge(s_b3l, 1)
            turn_products(0, 0, 0)
            with pe.Fori(0, final) as i:
                blk(i, False)
            blk(final, True)


def wi_ps(ps):
    return ps[7][:, 0:TT * HEADS].rearrange("p (t h) -> p t h", h=HEADS)


NAMES = ["x", "ln_in_g", "ln_in_b", "w_in", "b_gate", "lam_re", "lam_im", "log_dt", "b_re", "b_im", "c_re", "c_im",
         "d_skip", "w_glu", "w_attn_proj", "w_o", "ln1_g", "ln1_b", "w_router", "b_router", "w_up", "b_up",
         "w_down", "b_down", "ln2_g", "ln2_b"]


def kernel(**inputs):
    import numpy as _np
    import concourse.bacc as _bacc
    from concourse.bass_utils import run_bass_kernel_spmd as _run

    nc = _bacc.Bacc("TRN2", target_bir_lowering=False, num_devices=1)
    arrays, args = {}, {}
    for name in NAMES:
        x = _np.ascontiguousarray(inputs[name])
        arrays[f"in_{name}"] = x
        args[name] = nc.dram_tensor(f"in_{name}", x.shape, mybir.dt.from_np(x.dtype), kind="ExternalInput").ap()
    out = nc.dram_tensor("out_0", (1, SEQ, DM), F32, kind="ExternalOutput").ap()
    build(nc, args, out)
    r = _run(nc, [arrays], core_ids=[0])
    return r.results[0]["out_0"]
```
